# Optimizing a Trainium2 kernel written in Bass

```python
import math
import jax, jax.numpy as jnp
from jax import lax
import numpy as np

D_MODEL = 1024
BATCH = 1
SEQ = 256
DEPTH = 1
DEC_BATCH = 8
DEC_SEQ = 1
PAST_LEN = 2048
PAGE_SIZE = 128

D_MIX = D_MODEL
HEAD_DIM = 64
D_ATTN = D_MIX // 2
N_HEADS = D_ATTN // HEAD_DIM
N_KV = 2
Q_PER_KV = N_HEADS // N_KV
D_KV = N_KV * HEAD_DIM
WINDOW = 128
BLOCK = WINDOW
D_SSM = D_MIX - D_ATTN
SSM_H = 16
SSM_G = D_SSM // SSM_H
SSM_P = 64
D_IN = D_ATTN + 2 * D_KV + D_SSM
DT_MIN = 0.001
DT_MAX = 0.1
N_EXPERTS = 32
TOP_K = 4
D_FF = D_MODEL
SWIGLU_LIMIT = 7.0
SWIGLU_ALPHA = 1.702
PLE_DIM = 256
EPS = 1e-5

kernel_name = 'hymba_s5_swa_sink_moe_ple_step'

def _rms_norm(x, g):
    xf = x.astype(jnp.float32)
    y = xf * lax.rsqrt(jnp.mean(xf * xf, axis=-1, keepdims=True) + EPS)
    return (y * g.astype(jnp.float32)).astype(x.dtype)

def _alibi_slopes():
    return 2.0 ** (-8.0 * (jnp.arange(N_HEADS, dtype=jnp.float32) + 1.0) / N_HEADS)

def _window_attend(q, k, v, q_pos, k_pos, sinks):
    f32 = jnp.float32
    slopes = _alibi_slopes().reshape(N_KV, Q_PER_KV)
    s = jnp.einsum('bnqkgd,bnskd->bnkgqs', q.astype(f32), k.astype(f32)) * (HEAD_DIM ** -0.5)
    dist = q_pos[:, :, None] - k_pos[:, None, :]
    valid = (dist >= 0) & (dist <= WINDOW) & (k_pos[:, None, :] >= 0)
    bias = -slopes[None, None, :, :, None, None] * dist.astype(f32)[None, :, None, None]
    s = jnp.where(valid[None, :, None, None], s + bias, -jnp.inf)
    sink = jnp.broadcast_to(sinks.astype(f32).reshape(1, 1, N_KV, Q_PER_KV, 1, 1), s.shape[:-1] + (1,))
    pr = jax.nn.softmax(jnp.concatenate([s, sink], axis=-1), axis=-1)[..., :-1]
    out = jnp.einsum('bnkgqs,bnskd->bnqkgd', pr, v.astype(f32))
    return out.astype(q.dtype)

def _attention(q, k, v, k_cache, v_cache, sinks):
    B, L = q.shape[0], q.shape[1]
    if k_cache is None:
        nb = L // BLOCK
        qb = q.reshape(B, nb, BLOCK, N_KV, Q_PER_KV, HEAD_DIM)
        kb = k.reshape(B, nb, BLOCK, N_KV, HEAD_DIM)
        vb = v.reshape(B, nb, BLOCK, N_KV, HEAD_DIM)
        pad = ((0, 0), (1, 0), (0, 0), (0, 0), (0, 0))
        kband = jnp.concatenate([jnp.pad(kb[:, :-1], pad), kb], axis=2)
        vband = jnp.concatenate([jnp.pad(vb[:, :-1], pad), vb], axis=2)
        q_pos = jnp.arange(L, dtype=jnp.int32).reshape(nb, BLOCK)
        k_pos = (jnp.arange(nb, dtype=jnp.int32) * BLOCK - BLOCK)[:, None] + jnp.arange(2 * BLOCK, dtype=jnp.int32)[None]
        out = _window_attend(qb, kband, vband, q_pos, k_pos, sinks).reshape(B, L, D_ATTN)
        wb = min(WINDOW, L)
        return out, k[:, L - wb:], v[:, L - wb:]
    wb = k_cache.shape[1]
    k_all = jnp.concatenate([k_cache.astype(k.dtype), k], axis=1)
    v_all = jnp.concatenate([v_cache.astype(v.dtype), v], axis=1)
    q_pos = (PAST_LEN + jnp.arange(L, dtype=jnp.int32))[None]
    k_pos = jnp.concatenate([PAST_LEN - wb + jnp.arange(wb, dtype=jnp.int32),
                             PAST_LEN + jnp.arange(L, dtype=jnp.int32)])[None]
    out = _window_attend(q[:, None], k_all[:, None], v_all[:, None], q_pos, k_pos, sinks)[:, 0].reshape(B, L, D_ATTN)
    return out, k_all[:, -wb:], v_all[:, -wb:]

def _diag_combine(e1, e2):
    a1, b1 = e1
    a2, b2 = e2
    return a1 * a2, a2 * b1 + b2

def _s5(u, x0_re, x0_im, lam_re, lam_im, log_step, b_re, b_im, c_re, c_im, d_skip, w_glu, b_glu):
    f32 = jnp.float32
    B, L = u.shape[0], u.shape[1]
    lam = lax.complex(lam_re.astype(f32), lam_im.astype(f32))
    step = jnp.exp(log_step.astype(f32))[:, None]
    lam_bar = jnp.exp(lam * step)
    b_bar = ((lam_bar - 1.0) / lam)[:, :, None] * lax.complex(b_re.astype(f32), b_im.astype(f32))
    c = lax.complex(c_re.astype(f32), c_im.astype(f32))
    ug = u.astype(f32).reshape(B, L, SSM_G, SSM_H)
    bu = jnp.einsum('gph,blgh->blgp', b_bar, ug.astype(jnp.complex64))
    x0 = lax.complex(x0_re.astype(f32), x0_im.astype(f32))
    bu = bu.at[:, 0].add(lam_bar[None] * x0)
    a = jnp.broadcast_to(lam_bar, bu.shape)
    _, xs = lax.associative_scan(_diag_combine, (a, bu), axis=1)
    y = jnp.einsum('ghp,blgp->blgh', c, xs).real + d_skip.astype(f32) * ug
    y = jax.nn.gelu(y).reshape(B, L, D_SSM)
    y = y * jax.nn.sigmoid(y @ w_glu.astype(f32) + b_glu.astype(f32))
    x_last = xs[:, -1]
    return y.astype(u.dtype), jnp.real(x_last), jnp.imag(x_last)

def _moe(x, w_router, b_router, w_up, b_up, w_down, b_down):
    f32 = jnp.float32
    logits = (x @ w_router + b_router).astype(f32)
    top_v, top_i = lax.top_k(logits, TOP_K)
    top_w = jax.nn.softmax(top_v, axis=-1)
    gates = jnp.sum(jax.nn.one_hot(top_i, N_EXPERTS, dtype=f32) * top_w[..., None], axis=-2)

    def expert_step(acc, ep):
        w1, b1, w2, b2, g = ep
        hdn = x @ w1 + b1
        gt = jnp.minimum(hdn[:, :D_FF], SWIGLU_LIMIT)
        up = jnp.clip(hdn[:, D_FF:], -SWIGLU_LIMIT, SWIGLU_LIMIT)
        act = (up + 1.0) * gt * jax.nn.sigmoid(SWIGLU_ALPHA * gt)
        return acc + g[:, None] * (act @ w2 + b2), None

    acc, _ = lax.scan(expert_step, jnp.zeros((x.shape[0], D_MODEL), f32),
                      (w_up, b_up, w_down, b_down, gates.T))
    return acc.astype(x.dtype)

def _layer(h, p_l, k_cache, v_cache, s_re, s_im, lw):
    B, L, _ = h.shape
    xn = _rms_norm(h, lw['norm_mix'])
    proj = xn @ lw['w_in']
    q, k, v, u = jnp.split(proj, [D_ATTN, D_ATTN + D_KV, D_ATTN + 2 * D_KV], axis=-1)
    q = q.reshape(B, L, N_KV, Q_PER_KV, HEAD_DIM)
    k = k.reshape(B, L, N_KV, HEAD_DIM)
    v = v.reshape(B, L, N_KV, HEAD_DIM)
    attn, new_k, new_v = _attention(q, k, v, k_cache, v_cache, lw['sinks'])
    ssm, new_re, new_im = _s5(u, s_re, s_im, lw['lam_re'], lw['lam_im'], lw['log_step'],
                              lw['b_re'], lw['b_im'], lw['c_re'], lw['c_im'], lw['d_skip'],
                              lw['w_glu'], lw['b_glu'])
    mixed = jnp.concatenate([_rms_norm(attn, lw['norm_attn_out']),
                             _rms_norm(ssm, lw['norm_ssm_out'])], axis=-1)
    h = h + mixed @ lw['w_out']
    hn = _rms_norm(h, lw['norm_ffn']).reshape(B * L, D_MODEL)
    h = h + _moe(hn, lw['w_router'], lw['b_router'], lw['w_up'], lw['b_up'],
                 lw['w_down'], lw['b_down']).reshape(B, L, D_MODEL)
    gate = jax.nn.sigmoid(_rms_norm(h, lw['norm_ple']) @ lw['w_ple_gate'])
    h = h + gate * (p_l @ lw['w_ple_proj'])
    return h, new_k, new_v, new_re, new_im

def setup_inputs(seed: int = 0) -> dict:
    key = jax.random.key(seed)
    ks = jax.random.split(key, 40)
    f32 = jnp.float32
    wb = min(WINDOW, PAST_LEN)

    def nrm(k, shape, scale):
        return jax.random.normal(k, shape, f32) * scale

    lam_re = -0.5 * jnp.exp(nrm(ks[8], (DEPTH, SSM_G, SSM_P), 0.05))
    lam_im = math.pi * jnp.arange(SSM_P, dtype=f32)[None, None] + nrm(ks[9], (DEPTH, SSM_G, SSM_P), 0.01)
    log_step = jax.random.uniform(ks[10], (DEPTH, SSM_G), f32, math.log(DT_MIN), math.log(DT_MAX))
    return {
        'x_prompt': nrm(ks[0], (BATCH, SEQ, D_MODEL), 1.0),
        'x_sample': nrm(ks[1], (DEC_BATCH, DEC_SEQ, D_MODEL), 1.0),
        'cache_k_win': nrm(ks[2], (DEPTH, DEC_BATCH, wb, N_KV, HEAD_DIM), 1.0),
        'cache_v_win': nrm(ks[3], (DEPTH, DEC_BATCH, wb, N_KV, HEAD_DIM), 1.0),
        'state_ssm_re': nrm(ks[4], (DEPTH, DEC_BATCH, SSM_G, SSM_P), 0.1),
        'state_ssm_im': nrm(ks[5], (DEPTH, DEC_BATCH, SSM_G, SSM_P), 0.1),
        'p_prompt': nrm(ks[6], (DEPTH, BATCH, SEQ, PLE_DIM), 1.0),
        'p_sample': nrm(ks[7], (DEPTH, DEC_BATCH, DEC_SEQ, PLE_DIM), 1.0),
        'norm_mix': 1.0 + nrm(ks[11], (DEPTH, D_MODEL), 0.02),
        'w_in': nrm(ks[12], (DEPTH, D_MODEL, D_IN), D_MODEL ** -0.5),
        'sinks': nrm(ks[13], (DEPTH, N_HEADS), 0.5),
        'ssm_lam_re': lam_re,
        'ssm_lam_im': lam_im,
        'ssm_log_step': log_step,
        'ssm_b_re': nrm(ks[14], (DEPTH, SSM_G, SSM_P, SSM_H), (2.0 * SSM_H) ** -0.5),
        'ssm_b_im': nrm(ks[15], (DEPTH, SSM_G, SSM_P, SSM_H), (2.0 * SSM_H) ** -0.5),
        'ssm_c_re': nrm(ks[16], (DEPTH, SSM_G, SSM_H, SSM_P), (2.0 * SSM_P) ** -0.5),
        'ssm_c_im': nrm(ks[17], (DEPTH, SSM_G, SSM_H, SSM_P), (2.0 * SSM_P) ** -0.5),
        'ssm_d': nrm(ks[18], (DEPTH, SSM_G, SSM_H), 1.0),
        'w_glu': nrm(ks[19], (DEPTH, D_SSM, D_SSM), D_SSM ** -0.5),
        'b_glu': nrm(ks[20], (DEPTH, D_SSM), 0.01),
        'norm_attn_out': 1.0 + nrm(ks[21], (DEPTH, D_ATTN), 0.02),
        'norm_ssm_out': 1.0 + nrm(ks[22], (DEPTH, D_SSM), 0.02),
        'w_out': nrm(ks[23], (DEPTH, D_MIX, D_MODEL), D_MIX ** -0.5),
        'norm_ffn': 1.0 + nrm(ks[24], (DEPTH, D_MODEL), 0.02),
        'w_router': nrm(ks[25], (DEPTH, D_MODEL, N_EXPERTS), D_MODEL ** -0.5),
        'b_router': nrm(ks[26], (DEPTH, N_EXPERTS), 0.01),
        'w_up': nrm(ks[27], (DEPTH, N_EXPERTS, D_MODEL, 2 * D_FF), D_MODEL ** -0.5),
        'b_up': nrm(ks[28], (DEPTH, N_EXPERTS, 2 * D_FF), 0.01),
        'w_down': nrm(ks[29], (DEPTH, N_EXPERTS, D_FF, D_MODEL), D_FF ** -0.5),
        'b_down': nrm(ks[30], (DEPTH, N_EXPERTS, D_MODEL), 0.01),
        'norm_ple': 1.0 + nrm(ks[31], (DEPTH, D_MODEL), 0.02),
        'w_ple_gate': nrm(ks[32], (DEPTH, D_MODEL, D_MODEL), D_MODEL ** -0.5),
        'w_ple_proj': nrm(ks[33], (DEPTH, PLE_DIM, D_MODEL), PLE_DIM ** -0.5),
        'norm_final': 1.0 + nrm(ks[34], (D_MODEL,), 0.02),
    }

def reference(x_prompt, x_sample, cache_k_win, cache_v_win, state_ssm_re, state_ssm_im,
              p_prompt, p_sample, norm_mix, w_in, sinks, ssm_lam_re, ssm_lam_im, ssm_log_step,
              ssm_b_re, ssm_b_im, ssm_c_re, ssm_c_im, ssm_d, w_glu, b_glu, norm_attn_out,
              norm_ssm_out, w_out, norm_ffn, w_router, b_router, w_up, b_up, w_down, b_down,
              norm_ple, w_ple_gate, w_ple_proj, norm_final):
    hp = x_prompt
    hs = x_sample
    kp_l, vp_l, rp_l, ip_l = [], [], [], []
    ks_l, vs_l, rs_l, is_l = [], [], [], []
    for i in range(DEPTH):
        lw = dict(norm_mix=norm_mix[i], w_in=w_in[i], sinks=sinks[i],
                  lam_re=ssm_lam_re[i], lam_im=ssm_lam_im[i], log_step=ssm_log_step[i],
                  b_re=ssm_b_re[i], b_im=ssm_b_im[i], c_re=ssm_c_re[i], c_im=ssm_c_im[i],
                  d_skip=ssm_d[i], w_glu=w_glu[i], b_glu=b_glu[i],
                  norm_attn_out=norm_attn_out[i], norm_ssm_out=norm_ssm_out[i], w_out=w_out[i],
                  norm_ffn=norm_ffn[i], w_router=w_router[i], b_router=b_router[i],
                  w_up=w_up[i], b_up=b_up[i], w_down=w_down[i], b_down=b_down[i],
                  norm_ple=norm_ple[i], w_ple_gate=w_ple_gate[i], w_ple_proj=w_ple_proj[i])
        zero_state = jnp.zeros((x_prompt.shape[0], SSM_G, SSM_P), jnp.float32)
        hp, kp, vp, rp, ip = _layer(hp, p_prompt[i], None, None, zero_state, zero_state, lw)
        hs, kss, vss, rss, iss = _layer(hs, p_sample[i], cache_k_win[i], cache_v_win[i],
                                        state_ssm_re[i], state_ssm_im[i], lw)
        kp_l.append(kp); vp_l.append(vp); rp_l.append(rp); ip_l.append(ip)
        ks_l.append(kss); vs_l.append(vss); rs_l.append(rss); is_l.append(iss)
    y_prompt = _rms_norm(hp, norm_final)
    y_sample = _rms_norm(hs, norm_final)
    return (y_prompt, y_sample,
            jnp.stack(kp_l), jnp.stack(vp_l), jnp.stack(rp_l), jnp.stack(ip_l),
            jnp.stack(ks_l), jnp.stack(vs_l), jnp.stack(rs_l), jnp.stack(is_l))


_drawn_inputs = setup_inputs


def setup_inputs(seed=0):
    import zlib

    import numpy as np

    out = dict(_drawn_inputs(seed))
    spreads = {}
    factors = {'b_up': 8.0, 'b_down': 8.0, 'norm_ple': 52.268, 'norm_final': 8.17}
    for name, (base, spread) in spreads.items():
        noise = np.random.default_rng([zlib.crc32(name.encode()), seed]).standard_normal(out[name].shape)
        drawn = base * np.exp(spread * noise) if base else spread * noise
        out[name] = __import__('jax').numpy.asarray(drawn.astype(out[name].dtype))
    for name, factor in factors.items():
        out[name] = (out[name] * factor).astype(out[name].dtype)
    return out
```

```python
from contextlib import ExitStack

import numpy as np

import concourse.bass as bass
from concourse import mybir

F32 = mybir.dt.float32
I32 = mybir.dt.int32
U32 = mybir.dt.uint32
ALU = mybir.AluOpType
ACT = mybir.ActivationFunctionType
AX = mybir.AxisListType

P = 128
D = 1024
SEQ, NB = 256, 8
T = SEQ + NB
KD = D // P
HEADS, KV, HD = 8, 2, 64
D_ATTN = HEADS * HD
WIN = 128
G, H, S = 32, 16, 64
D_SSM = G * H
KM = D_SSM // P
D_IN = D_ATTN + 2 * KV * HD + D_SSM
ST = G // 2
NE, TOPK, FF = 32, 4, 1024
PLE = 256
EPS = 1e-5
LIMIT, ALPHA = 7.0, 1.702
C = 64
ROUNDS = -(-T // C)
CHUNKS = [(0, P), (P, P), (SEQ, NB)]
SLOPES = [2.0 ** (-8.0 * (h + 1.0) / HEADS) for h in range(HEADS)]
SCALE = HD ** -0.5
FAR = 1e30

K_ID, K_TRI, K_ONE = 0, P, 2 * P
K_DIST = 3 * P
K_SBIAS = K_DIST + 2 * P
K_PAR = K_SBIAS + WIN + 1
K_HALF = K_PAR + 2
K_SAME = K_HALF + 2
K_OWN = K_SAME + 64
K_IOTA = K_OWN + NB
K_N = K_IOTA + C

V_MIX, V_FFN, V_PLE, V_OUT, V_D, V_GLU, V_N = 0, 8, 16, 24, 32, 36, 40

AT_QKV, AT_KVTOK, AT_B0, AT_B0V, AT_B1, AT_B1V, AT_S, AT_SV = 1, 3, 4, 5, 7, 8, 10, 12

UP, DN = 8, 4
DVE_LOOP = 6


def shape_constants():
    k = np.zeros((P, K_N), np.float32)
    i = np.arange(P)
    k[:, K_ID:K_ID + P] = np.eye(P)
    k[:, K_TRI:K_TRI + P] = i[:, None] < i[None]
    k[:, K_ONE:K_ONE + P] = 1.0
    dist = i[:, None] + WIN - np.arange(2 * P)[None]
    k[:, K_DIST:K_DIST + 2 * P] = np.where((dist >= 0) & (dist <= WIN), dist, FAR)
    r = np.arange(64)
    slope = np.asarray(SLOPES)[r % HEADS]
    k[:64, K_SBIAS:K_SBIAS + WIN + 1] = -slope[:, None] / SCALE * (WIN - np.arange(WIN + 1))[None]
    k[:, K_PAR] = (i // H) % 2 == 0
    k[:, K_PAR + 1] = (i // H) % 2 == 1
    k[:64, K_HALF] = r % HEADS < HEADS // KV
    k[:64, K_HALF + 1] = r % HEADS >= HEADS // KV
    k[:64, K_SAME:K_SAME + 64] = r[:, None] // HEADS == r[None] // HEADS
    k[:64, K_OWN:K_OWN + NB] = r[:, None] // HEADS == np.arange(NB)[None]
    k[:, K_IOTA:K_IOTA + C] = np.arange(C)[None]
    return k


def hybrid_layer(nc, A, O):
    ctx = ExitStack()
    with ctx:
        def sb(name, shape, dt=F32):
            return ctx.enter_context(nc.sbuf_tensor(name, shape, dt))

        def sem(name):
            return ctx.enter_context(nc.semaphore(name))

        ps = ctx.enter_context(nc.psum_tensor("ps", [P, 8, 512], F32))
        ring_up = sb("ring_up", [P, UP, 2 * FF])
        ring_dn = sb("ring_dn", [P, 2 * DN, D])
        up_flat = ring_up[:].rearrange("p a b -> p (a b)")
        w_in = up_flat[:, 0:KD * D_IN].rearrange("p (k n) -> p k n", k=KD)
        w_glu = ring_up[:, 5].rearrange("p (k n) -> p k n", k=KM)
        w_out = ring_dn
        s5_mem = up_flat[:, 6 * 2 * FF:8 * 2 * FF]
        cos_t = s5_mem[:, 0:512].rearrange("p (a t) -> p a t", a=2)
        sin_t = s5_mem[:, 512:1024].rearrange("p (a t) -> p a t", a=2)
        tmp_t = s5_mem[:, 1024:1280]
        prod_p = s5_mem[:, 1280:1792].rearrange("p (r t) -> p r t", r=2)
        z_in = s5_mem[:, 1792:2304].rearrange("p (r t) -> p r t", r=2)
        rot_c = s5_mem[:, 2304:3328].rearrange("p (a r t) -> p a r t", a=2, r=2)
        w_gate = ring_up[:, 0:4].rearrange("p a (b n) -> p (a b) n", b=2)
        w_pp = ring_up[:, 4].rearrange("p (k n) -> p k n", k=2)

        kst = sb("kst", [P, K_N])
        ident = kst[:, K_ID:K_ID + P]
        tri = kst[:, K_TRI:K_TRI + P]
        ones = kst[:, K_ONE:K_ONE + P]
        x_tok = sb("x_tok", [P, 3, D])
        n_tok = sb("n_tok", [P, 3, D])
        fa = sb("fa", [P, KD, T])
        fb = sb("fb", [P, KD, T])
        vecs = sb("vecs", [P, V_N])
        final_g = sb("final_g", [P, D])
        router = sb("router", [P, KD, NE])
        router_b = sb("router_b", [P, NE])
        b_down = sb("b_down", [NE, D])
        stat = sb("stat", [P, 3, 4])
        rank = sb("rank", [P, 3, NE + 1])
        gate = sb("gate", [P, 3, NE + 1])
        n_max = sb("n_max", [P, 1])
        n_int = sb("n_int", [1, 1], I32)

        R_N = 12100
        region = sb("region", [P, R_N])
        used = [0]

        def part(n):
            used[0] += n
            assert used[0] <= R_N, used[0]
            return region[:, used[0] - n:used[0]]

        proj = part(10 * T).rearrange("p (k t) -> p k t", k=10)
        rot_s = part(1024).rearrange("p (a r t) -> p a r t", a=2, r=2)
        b_t = [part(512).rearrange("p (k n) -> p k n", k=4) for _ in range(2)]
        c_t = [part(512).rearrange("p (k n) -> p k n", k=4) for _ in range(3)]
        lo = [part(256).rearrange("p (a b) -> p a b", a=ST) for _ in range(2)]
        hi = [part(256).rearrange("p (a b) -> p a b", a=ST) for _ in range(2)]
        pt = part(16 * P).rearrange("p (k n) -> p k n", k=16)
        kc_t = part(NB * (WIN + 1)).rearrange("p (b n) -> p b n", b=NB)
        spread = part(NB * 72)
        pcols = part(7 * ST).rearrange("p (a b) -> p a b", a=7)
        x0_t = part(2 * P).rearrange("p (r n) -> p r n", r=2)
        xs_flat = part(2 * P)
        xs_new = xs_flat.rearrange("p (r b a) -> p r a b", r=2, a=ST)
        bu_s = part(2 * P).rearrange("p (r a b) -> p r a b", r=2, a=ST)
        last = part(2 * ST).rearrange("p (r a) -> p r a", r=2)
        mini = part(2 * P)
        rows = fb[:].rearrange("p a b -> p (a b)")[:, 0:16 * P]
        pt_flat = pt.rearrange("p k n -> p (k n)")
        b_raw = pt_flat[:, 0:512].rearrange("p (r a h) -> p r a h", r=2, a=ST)
        b_bd = kc_t.rearrange("p b n -> p (b n)")[:, 0:1024].rearrange("p (r a m) -> p r a m", r=2, a=ST)
        c_raw = pt_flat[:, 512:1024].rearrange("p (r a n) -> p r a n", r=2, a=4)
        c_bd = pt_flat[:, 1024:2048].rearrange("p (r a n) -> p r a n", r=2, a=4)
        n_flat = n_tok[:].rearrange("p a b -> p (a b)")
        sc = n_flat[:, 0:2048].rearrange("p (h n) -> p h n", h=HEADS)
        att = n_flat[:, 2048:3072].rearrange("p (b n) -> p b n", b=2)
        fa_flat = fa[:].rearrange("p a b -> p (a b)")
        kc = fa_flat[:, 0:1024].rearrange("p (b n) -> p b n", b=NB)
        vc = fa_flat[:, 1024:2048].rearrange("p (b n) -> p b n", b=NB)
        y_t = proj[:, 0:4]

        small = sb("small", [P, 160])
        mx, mneg, rsum, esink, rden = (small[:, 8 * i:8 * i + 8] for i in range(5))
        sink_b = small[:, 40:48]
        sink_s = small[:, 48:49]
        s_small = small[:, 49:57]
        kv_tok = sb("kv_tok", [P, 3, P])
        kv_new = sb("kv_new", [NB, 2, P])
        s_sc = sb("s_sc", [64, WIN + 1])
        s_o = sb("s_o", [64, 2, 64])
        s_own = sb("s_own", [64, NB])
        s_ownT = sb("s_ownT", [NB, 64])
        top = sb("top", [P, 3, 48])
        top_i = sb("top_i", [P, 3, 8], U32)
        pick = sb("pick", [P, TOPK, NE])

        used[0] = 0
        b_up = part(2 * FF)
        one_hot = part(C)
        sel = part(3 * C).rearrange("p (c s) -> p c s", c=3)
        sel_g = part(3 * 2 * C).rearrange("p (c a s) -> p c a s", c=3, a=2)
        xe = part(KD * C).rearrange("p (k s) -> p k s", k=KD)
        g_lim = part(512)
        u_lim = part(512)
        sig = part(512)
        act_v = part(512)
        act_t = part(512).rearrange("p (j n) -> p j n", j=4)
        out_e = part(512)
        g_t = part(3 * P)
        gates_t = part(T)
        p_tok = part(3 * PLE).rearrange("p (c n) -> p c n", c=3)
        p_t = part(2 * T).rearrange("p (k t) -> p k t", k=2)
        logits = part(3 * NE).rearrange("p (c n) -> p c n", c=3)
        mask = part(3 * NE).rearrange("p (c n) -> p c n", c=3)
        sg_t = part(2 * T).rearrange("p (a t) -> p a t", a=2)
        sq = sg_t

        def bank(b, n=512, parts=P, first=0):
            return ps[first:first + parts, b, 0:n]

        def col(t, n):
            return t.unsqueeze(2).to_broadcast([t.shape[0], t.shape[1], n])

        (ld_x, ld_win, ld_wglu, ld_wout, ld_vec, ld_par, ld_b, ld_c, ld_x0, ld_sink, ld_cache,
         ld_router, ld_bup, ld_gate_w, ld_p) = (sem(n) for n in (
            "ld_x", "ld_win", "ld_wglu", "ld_wout", "ld_vec", "ld_par", "ld_b", "ld_c", "ld_x0",
            "ld_sink", "ld_cache", "ld_router", "ld_bup", "ld_gate_w", "ld_p"))
        up_in = [sem(f"up_in{k}") for k in range(UP)]
        dn_in = [sem(f"dn_in{k}") for k in range(DN)]
        dve_step, act_step, pool_step, dve_loop = (sem(n) for n in ("dve_step", "act_step", "pool_step", "dve_loop"))
        names = ("up_rounds n_ready st_k q_ps glu_ps s5_free up_free mix_ps dn_free f_out st_y c_ready par_sb b_ready "
                 "rot_ready trig last_in region_free hot_rdy hid_ps vec_ps norm_scaled norm_ps par_rows par_ps "
                 "norm_sb u_ps c_ps x0_ps c_sb b_ps b_sb u_sb bu_read bu_ps y_read y_rot q_sb tok_ps tok_sb "
                 "att_sb att_t score_read score_ps expd p_sb p_ps o_ps att_scaled att_ps kct_ps kct_sb q_spread "
                 "ssc_ps s_expd s_oready s_pps s_pspread s_ops s_ossq s_gps s_onorm s_otps state_s ys_ps gelu "
                 "state_ps ssm_sq ssm_ssq s_ot mix_sb ssm_n back_add back_ps lg_ps mask_sb cnt_ps gtr_ps gtr_sb "
                 "bd_sb bd_ps sel_rdy xg_ps dn_sb gt_sb cmb_read cmb_ps xe_rdy act_rdy at_ps selg_rdy gt_ps at_sb "
                 "pT_ps pT_sb pp_sb pp_ps gz_mul gz_sig gz_ps par_exp par_red norm_ssq norm_root par_sin vec_sb "
                 "x0_sb m_neg att_ssq att_root s_mneg s_groot ypre ssm_y glu_sig ssm_root topv w_exp g_rdy "
                 "sig_rdy all_added rank_sb").split()
        Z = {n: sem(n) for n in names}

        block = ctx.enter_context(nc.Block())

        def after_rounds(eng, body):
            body(0)
            eng.wait_ge(Z["n_ready"], 1)
            n = eng.value_load(n_int[0:1, 0:1], min_val=0, max_val=T)
            with eng.Fori(1, ROUNDS) as r:
                with eng.If(n > r * C):
                    body(r)
                eng.nop()

        @block.sync
        def _(sp):
            x_p, x_s = A["x_prompt"][0], A["x_sample"].rearrange("b l d -> (b l) d")
            for c in range(2):
                sp.dma_start(x_tok[:, c], x_p[c * P:(c + 1) * P, :]).then_inc(ld_x, 16)
            sp.dma_start(x_tok[0:NB, 2], x_s).then_inc(ld_x, 16)
            sp.dma_start(kst[:], A["shape_constants"]).then_inc(ld_x, 16)
            w = A["w_in"][0].rearrange("(k p) n -> p k n", p=P)
            for k in range(0, KD, 4):
                sp.dma_start(w_in[:, k:k + 4], w[:, k:k + 4]).then_inc(ld_win, 16)
            sp.dma_start(w_glu, A["w_glu"][0].rearrange("(k p) n -> p k n", p=P)).then_inc(ld_wglu, 16)
            sp.dma_start(w_out[:], A["w_out"][0].rearrange("(k p) n -> p k n", p=P)).then_inc(ld_wout, 16)
            sp.dma_start(final_g[:], A["norm_final"].partition_broadcast(P)).then_inc(ld_router, 16)
            sp.dma_start(router[:], A["w_router"][0].rearrange("(k p) n -> p k n", p=P)).then_inc(ld_router, 16)
            sp.dma_start(router_b[:], A["b_router"][0].partition_broadcast(P)).then_inc(ld_router, 16)
            sp.dma_start(b_down[:], A["b_down"][0]).then_inc(ld_router, 16)
            for src, dst in ((A["cache_k_win"], O[6]), (A["cache_v_win"], O[7])):
                sp.dma_start(dst[0].rearrange("b w n d -> b (w n d)")[:, 0:(WIN - 1) * P],
                             src[0].rearrange("b w n d -> b (w n d)")[:, P:WIN * P]).then_inc(Z["st_k"], 16)

            up_w = A["w_up"][0].rearrange("e (k p) n -> e k p n", p=P)
            dn_w = A["w_down"][0].rearrange("e (s k p) n -> e s p k n", p=P, k=2)

            def expert(e, t, first=False):
                for k in range(UP):
                    if first:
                        sp.wait_ge(*((Z["q_ps"], 6) if k < 5 else (Z["glu_ps"], KM) if k == 5 else (Z["s5_free"], 1)))
                    else:
                        sp.wait_ge(Z["up_free"], t * UP + (k + 1 - UP))
                    sp.dma_start(ring_up[:, k], up_w[bass.ds(e, 1), k].rearrange("e p n -> (e p) n")
                                 ).then_inc(up_in[k], 16)
                for s in range(DN):
                    if first:
                        sp.wait_ge(Z["mix_ps"], KD)
                    else:
                        sp.wait_ge(Z["dn_free"], t * DN + (s + 1 - DN))
                    sp.dma_start(ring_dn[:, 2 * s:2 * s + 2], dn_w[bass.ds(e, 1), s].rearrange("e p k n -> (e p) k n")
                                 ).then_inc(dn_in[s], 16)

            def one_round(r):
                if isinstance(r, int):
                    expert(0, 0, first=True)
                    with sp.Fori(1, NE) as e:
                        expert(e, e)
                else:
                    with sp.Fori(0, NE) as e:
                        expert(e, r * NE + e)
                sp.wait_ge(Z["up_free"], (r * NE + NE) * UP)
                sp.sem_inc(Z["up_rounds"], 1)

            after_rounds(sp, one_round)
            for k in range(4):
                sp.dma_start(w_gate[:, 2 * k:2 * k + 2], A["w_ple_gate"][0].rearrange("(s k p) n -> s p k n", p=P, k=2)[k]
                             ).then_inc(ld_gate_w, 16)
            sp.wait_ge(Z["f_out"], 3)
            for c in range(2):
                sp.dma_start(O[0][0, c * P:(c + 1) * P, :], n_tok[:, c]).then_inc(Z["st_y"], 16)
            sp.dma_start(O[1].rearrange("b l d -> (b l) d"), n_tok[0:NB, 2]).then_inc(Z["st_y"], 16)
            sp.wait_ge(Z["st_y"], 48)
            sp.wait_ge(Z["st_k"], 32 + 16 * 8)

        @block.gpsimd
        def _(pool):
            n = [0]

            def chain(ins):
                n[0] += 1
                ins.then_inc(pool_step, 1)
                pool.wait_ge(pool_step, n[0])

            tt = nc.gpsimd.tensor_tensor

            def cmul(out, a, b, s1, sh):
                chain(tt(s1, a[1], b[1], ALU.mult))
                chain(tt(out[0], a[0], b[0], ALU.mult))
                chain(tt(out[0], out[0], s1, ALU.subtract))
                chain(tt(s1, a[1], b[0], ALU.mult))
                chain(tt(out[1], a[0], b[1], ALU.mult))
                chain(tt(out[1], out[1], s1, ALU.add))

            pool.wait_ge(ld_c, 32)
            pool.wait_ge(ld_x, 64)
            for r, sign in ((0, 1.0), (1, -1.0)):
                for par in range(2):
                    chain(nc.gpsimd.tensor_scalar(c_bd[:, r, :, par * S:par * S + S], c_raw[:, r],
                                                  kst[:, K_PAR + par:K_PAR + par + 1], sign, ALU.mult, ALU.mult))
            nc.gpsimd.nop().then_inc(Z["c_ready"], 1)
            pool.wait_ge(Z["par_sb"], 1)
            pool.wait_ge(ld_b, 32)
            chain(nc.gpsimd.memset(b_bd, 0.0))
            fr, fi = col(pcols[:, 5], H), col(pcols[:, 6], H)
            t1 = mini.rearrange("p (a h) -> p a h", h=H)
            for r, (f0, f1, op) in enumerate(((fr, fi, ALU.subtract), (fi, fr, ALU.add))):
                t2 = tmp_t.rearrange("p (a h) -> p a h", h=H)
                chain(tt(t1, b_raw[:, 0], f0, ALU.mult))
                chain(tt(t2, b_raw[:, 1], f1, ALU.mult))
                for par in range(2):
                    rows_ = slice(par * S, par * S + S)
                    chain(tt(b_bd[rows_, r, :, par * H:par * H + H], t1[rows_], t2[rows_], op))
            nc.gpsimd.nop().then_inc(Z["b_ready"], 1)
            m3 = mini.rearrange("p (a b) -> p a b", b=16)
            base = (pcols[:, 0].unsqueeze(2), pcols[:, 1].unsqueeze(2))
            for tab in (lo, hi):
                chain(nc.gpsimd.memset(tab[0][:, :, 0:1], 1.0))
                chain(nc.gpsimd.memset(tab[1][:, :, 0:1], 0.0))
                chain(nc.gpsimd.tensor_copy(tab[0][:, :, 1:2], base[0]))
                chain(nc.gpsimd.tensor_copy(tab[1][:, :, 1:2], base[1]))
                step = (tab[0][:, :, 1:2], tab[1][:, :, 1:2])
                for k in (2, 4, 8, 16):
                    sq_ = (rows[:, 32 * k:32 * k + 16].unsqueeze(2), rows[:, 32 * k + 16:32 * k + 32].unsqueeze(2))
                    cmul(sq_, step, step, m3[:, :, 0:1], 1)
                    step = sq_
                    if k < 16:
                        cmul((tab[0][:, :, k:2 * k], tab[1][:, :, k:2 * k]), (tab[0][:, :, 0:k], tab[1][:, :, 0:k]),
                             (step[0].to_broadcast([P, ST, k]), step[1].to_broadcast([P, ST, k])), m3[:, :, 0:k], k)
                base = step

            def trig(i):
                a = i % 2
                if i >= 2:
                    pool.wait_ge(Z["rot_ready"], i - 1)
                hb = [h[:, i].unsqueeze(2).to_broadcast([P, 16, 16]) for h in hi]
                lb = [l[:, i].unsqueeze(1).to_broadcast([P, 16, 16]) for l in lo]
                out = [x[:, a].rearrange("p (a b) -> p a b", a=16) for x in (cos_t, sin_t)]
                tm = tmp_t.rearrange("p (a b) -> p a b", a=16)
                cmul(out, hb, lb, tm, 256)
                nc.gpsimd.nop().then_inc(Z["trig"], 1)

            def last_state(i):
                a = i % 2
                pool.wait_ge(Z["rot_ready"], i + 1)
                chain(tt(last[:, 0, i:i + 1], rot_c[:, a, 0, 255:256], rot_s[:, a, 1, 255:256], ALU.subtract))
                tt(last[:, 1, i:i + 1], rot_s[:, a, 0, 255:256], rot_c[:, a, 1, 255:256], ALU.add
                   ).then_inc(Z["last_in"], 1)

            for i in range(ST + 2):
                if i < ST:
                    trig(i)
                if i >= 2:
                    last_state(i - 2)

            pool.wait_ge(Z["region_free"], 1)
            nc.gpsimd.memset(b_up, 0.0).then_inc(Z["hot_rdy"], 1)

            def hot(e, t, first=False):
                if not first:
                    pool.wait_ge(Z["hid_ps"], t)
                nc.gpsimd.tensor_copy(one_hot, ident[:, bass.ds(e, 1)].to_broadcast([P, C])).then_inc(Z["hot_rdy"], 1)

            def one_round(r):
                if isinstance(r, int):
                    hot(0, 0, first=True)
                    with pool.Fori(1, NE) as e:
                        hot(e, e)
                else:
                    with pool.Fori(0, NE) as e:
                        hot(e, r * NE + e)

            after_rounds(pool, one_round)

        @block.tensor
        def _(pe):
            mm, tr = nc.tensor.matmul, nc.tensor.transpose
            pe.wait_ge(ld_x, 64)
            pe.wait_ge(ld_vec, 16 * 7)
            tr(bank(7, V_N), rows[0:V_N, 0:P], ident[0:V_N, 0:V_N]).then_inc(Z["vec_ps"], 1)
            n = 0
            for c, (t0, nt) in enumerate(CHUNKS):
                pe.wait_ge(Z["norm_scaled"], c + 1)
                for half in range(2):
                    for k in range(4):
                        m = tr(ps[:, 2 * c + half, k * nt:(k + 1) * nt],
                               n_tok[0:nt, c, (4 * half + k) * P:(4 * half + k + 1) * P], ident[0:nt, 0:nt])
                    m.then_inc(Z["norm_ps"], 1)
            pe.wait_ge(Z["par_rows"], 1)
            for j in range(7):
                m = tr(ps[:, 6, j * ST:(j + 1) * ST], rows[0:ST, (2 + j) * P:(3 + j) * P], ident[0:ST, 0:ST])
            m.then_inc(Z["par_ps"], 1)

            def project(slot, b, lhs):
                for k in range(KD):
                    m = mm(bank(b, T), lhs(k), fa[:, k, :], start=(k == 0), stop=(k == KD - 1))
                return m

            pe.wait_ge(Z["norm_sb"], 6)
            pe.wait_ge(ld_win, 32)
            for j in range(4):
                project(6 + j, j, lambda k: w_in[:, k, D_IN - D_SSM + j * P:D_IN - D_SSM + (j + 1) * P]
                        ).then_inc(Z["u_ps"], 1)
            pe.wait_ge(Z["c_ready"], 1)
            for r in range(2):
                for k in range(4):
                    m = tr(ps[:, 4 + r, k * P:(k + 1) * P], c_bd[:, r, k], ident)
            m.then_inc(Z["c_ps"], 1)
            pe.wait_ge(ld_x0, 32)
            pe.wait_ge(Z["par_sb"], 1)
            for r in range(2):
                m = tr(ps[:, 6, r * P:(r + 1) * P], rows[:, (10 + r) * P:(11 + r) * P], ident)
            m.then_inc(Z["x0_ps"], 1)
            pe.wait_ge(Z["b_ready"], 1)
            pe.wait_ge(Z["c_sb"], 1)
            for r in range(2):
                for k in range(4):
                    m = tr(ps[:, 4 + r, k * P:(k + 1) * P],
                           b_bd[:, r, 4 * k:4 * k + 4].rearrange("p a m -> p (a m)"), ident)
            m.then_inc(Z["b_ps"], 1)
            pe.wait_ge(Z["b_sb"], 1)
            pe.wait_ge(Z["u_sb"], 4)

            def drive(i):
                c, j = divmod(i, 4)
                if i >= 1:
                    pe.wait_ge(Z["bu_read"], i)
                rows_ = slice(32 * j, 32 * j + 32)
                for r in range(2):
                    m = mm(bank(r, T), b_t[r][rows_, c, :], proj[rows_, 6 + c, :], start=True, stop=True)
                m.then_inc(Z["bu_ps"], 1)

            def read_out(i):
                c, j = divmod(i, 4)
                pe.wait_ge(Z["rot_ready"], i + 1)
                if j == 0 and c >= 1:
                    pe.wait_ge(Z["y_read"], c)
                a = i % 2
                out = ps[32 * j:32 * j + 32, 4, 0:SEQ]
                cols = slice(32 * j, 32 * j + 32)
                for n_, (w, v) in enumerate(((0, rot_c[:, a, 0]), (1, rot_c[:, a, 1]), (2, rot_s[:, a, 1]),
                                            (1, rot_s[:, a, 0]))):
                    m = mm(out, c_t[w][:, c, cols], v, start=(n_ == 0), stop=(n_ == 3))
                m.then_inc(Z["y_rot"], 1)

            def project_q(c, b):
                for k in range(KD):
                    for n_ in range(KV):
                        h = 4 * n_ + c
                        m = mm(ps[64 * n_:64 * n_ + 64, b, 0:T], w_in[:, k, h * HD:(h + 1) * HD], fa[:, k, :],
                               start=(k == 0), stop=(k == KD - 1))
                return m

            def project_qkv():
                for n_, slot in enumerate((4, 5, 0, 1, 2, 3)):
                    b = 5 + n_ % 3
                    if n_ >= 3:
                        pe.wait_ge(Z["q_sb"], n_ - 2)
                    if slot >= 4:
                        m = project(slot, b, lambda k: w_in[:, k, D_ATTN + (slot - 4) * P:D_ATTN + (slot - 3) * P])
                    else:
                        m = project_q(slot, b)
                    m.then_inc(Z["q_ps"], 1)

            def kv_to_tokens():
                pe.wait_ge(Z["q_sb"], 6)
                for j, (slot, c) in enumerate(((5, 0), (5, 1), (4, 1))):
                    tr(ps[:, 7, j * P:(j + 1) * P], proj[:, slot, c * P:(c + 1) * P], ident)
                for j, slot in enumerate((4, 5)):
                    m = tr(ps[0:NB, 6, j * P:(j + 1) * P], proj[:, slot, SEQ:T], ident)
                m.then_inc(Z["tok_ps"], 1)

            def scores(b):
                K = P * (b + 1)
                if b == 0:
                    pe.wait_ge(Z["tok_sb"], 1)
                else:
                    pe.wait_ge(Z["att_sb"], b)
                    pe.wait_ge(Z["att_t"], b)
                for c in range(4):
                    if b * 4 + c >= 1 and c >= 1:
                        pe.wait_ge(Z["score_read"], b * 4 + c)
                    for n_ in range(KV):
                        r = slice(64 * n_, 64 * n_ + 64)
                        m = mm(bank(5 + n_, K), proj[r, c, b * P:(b + 1) * P], proj[r, 4, 0:K], start=True, stop=True)
                    m.then_inc(Z["score_ps"], 1)

            p_fills = [0]

            def p_transposes(b):
                nk = b + 1
                pe.wait_ge(Z["expd"], b + 1)
                pe.wait_ge(Z["score_read"], 4 * (b + 1))
                for f in range(2 * nk):
                    if f >= 3:
                        pe.wait_ge(Z["p_sb"], p_fills[0] - 2)
                    for q in range(4):
                        h, kc_ = divmod(4 * f + q, nk)
                        m = tr(ps[:, 5 + f % 3, q * P:(q + 1) * P], sc[:, h, kc_ * P:(kc_ + 1) * P], ident)
                    m.then_inc(Z["p_ps"], 1)
                    p_fills[0] += 1

            def values(b):
                nk = b + 1
                pe.wait_ge(Z["p_sb"], p_fills[0])
                for h in range(HEADS):
                    for kc_ in range(nk):
                        m = mm(ps[:, 5, h * HD:(h + 1) * HD], pt[:, h * nk + kc_, :],
                               kv_tok[:, kc_, (h // 4) * HD:(h // 4 + 1) * HD], start=(kc_ == 0), stop=(kc_ == nk - 1))
                m.then_inc(Z["o_ps"], 1)

            def att_transposes(b):
                pe.wait_ge(Z["att_scaled"], b + 1)
                for k in range(4):
                    m = tr(ps[:, 6, k * P:(k + 1) * P], att[:, b, k * P:(k + 1) * P], ident)
                m.then_inc(Z["att_ps"], 1)

            def cache_transposes():
                pe.wait_ge(ld_cache, 32)
                pe.wait_ge(Z["att_sb"], 2)
                pe.wait_ge(Z["p_sb"], p_fills[0])
                for f, b_ in enumerate((5, 7)):
                    for q in range(4):
                        m = tr(ps[:, b_, q * P:(q + 1) * P], kc[:, 4 * f + q], ident)
                    m.then_inc(Z["kct_ps"], 1)

            def sample_scores():
                pe.wait_ge(Z["kct_sb"], 3)
                pe.wait_ge(Z["q_spread"], 1)
                for b_ in range(NB):
                    m = mm(ps[0:64, 5, 0:WIN + 1], spread[:, b_ * 64:(b_ + 1) * 64], kc_t[:, b_, :],
                           start=(b_ == 0), stop=(b_ == NB - 1))
                m.then_inc(Z["ssc_ps"], 1)

            def sample_values():
                pe.wait_ge(Z["s_expd"], 1)
                pe.wait_ge(Z["s_oready"], 1)
                tr(ps[:, 7, 0:64], s_sc[:, 0:WIN], ident[0:64, 0:64])
                tr(ps[0:NB, 7, 64:128], s_own[:], ident[0:64, 0:64]).then_inc(Z["s_pps"], 1)
                pe.wait_ge(Z["s_pspread"], 2)
                for b_ in range(NB):
                    mm(ps[0:64, 5, 0:P], spread[:, b_ * 64:(b_ + 1) * 64], vc[:, b_, :], start=(b_ == 0), stop=False)
                mm(ps[0:64, 5, 0:P], s_ownT[:], kv_new[:, 1, :], start=False, stop=True).then_inc(Z["s_ops"], 1)
                pe.wait_ge(Z["s_ossq"], 1)
                mm(ps[0:64, 7, 0:1], kst[0:64, K_SAME:K_SAME + 64], s_small[0:64, 5:6], start=True, stop=True
                   ).then_inc(Z["s_gps"], 1)
                pe.wait_ge(Z["s_onorm"], 1)
                tr(ps[:, 6, 0:64], s_o[:].rearrange("p a d -> p (a d)"), ident[0:64, 0:64]).then_inc(Z["s_otps"], 1)

            for i in range(ST + 1):
                if i < ST:
                    drive(i)
                if i >= 1:
                    read_out(i - 1)
                if i == AT_QKV:
                    project_qkv()
                if i == AT_KVTOK:
                    kv_to_tokens()
                if i == AT_B0:
                    scores(0)
                if i == AT_B0V:
                    p_transposes(0)
                    values(0)
                    att_transposes(0)
                if i == AT_B1:
                    scores(1)
                if i == AT_B1V:
                    p_transposes(1)
                    values(1)
                    att_transposes(1)
                if i == AT_S:
                    cache_transposes()
                    sample_scores()
                if i == AT_SV:
                    sample_values()

            pe.wait_ge(Z["state_s"], 1)
            for i in range(ST):
                c, j = divmod(i, 4)
                for n_ in range(2):
                    m = mm(ps[32 * j:32 * j + 32, 5, NB * c:NB * c + NB], c_t[n_][:, c, 32 * j:32 * j + 32],
                           xs_new[:, n_, i, :], start=(n_ == 0), stop=(n_ == 1))
            m.then_inc(Z["ys_ps"], 1)
            pe.wait_ge(ld_wglu, 16)
            pe.wait_ge(Z["gelu"], 1)
            for c in range(KM):
                for k in range(KM):
                    m = mm(bank(c, T), w_glu[:, k, c * P:(c + 1) * P], y_t[:, k, :], start=(k == 0), stop=(k == KM - 1))
                m.then_inc(Z["glu_ps"], 1)
            pe.wait_ge(Z["last_in"], ST)
            for r in range(2):
                tr(ps[:, 7, r * P:(r + 1) * P], xs_flat[:, r * P:(r + 1) * P], ident)
            for r in range(2):
                m = tr(ps[0:ST, 7, (2 + r) * P:(3 + r) * P], last[:, r], ident)
            m.then_inc(Z["state_ps"], 1)
            for c in range(KM):
                pe.wait_ge(Z["ssm_sq"], c + 1)
                m = mm(bank(6, T), ones, sq[:, c % 2], start=(c == 0), stop=(c == KM - 1))
                m.then_inc(Z["ssm_ssq"], 1)
            pe.wait_ge(ld_wout, 16)
            pe.wait_ge(Z["att_t"], 2)
            pe.wait_ge(Z["s_ot"], 1)
            for o in range(KD):
                b_ = (0, 1, 2, 3)[o % 4]
                if o >= 4:
                    pe.wait_ge(Z["mix_sb"], o - 3)
                for k in range(KD):
                    if o == 0 and k == 4:
                        pe.wait_ge(Z["ssm_n"], KM)
                    m = mm(bank(b_, T), w_out[:, k, o * P:(o + 1) * P], fb[:, k, :], start=(k == 0), stop=(k == KD - 1))
                m.then_inc(Z["mix_ps"], 1)
            n_ = 0
            for half in range(2):
                pe.wait_ge(Z["mix_sb"], 4 * (half + 1))
                for c, (t0, nt) in enumerate(CHUNKS):
                    if n_ >= 2:
                        pe.wait_ge(Z["back_add"], n_ - 1)
                    for k in range(4):
                        m = tr(ps[0:nt, 4 + n_ % 2, k * P:(k + 1) * P], fa[:, 4 * half + k, t0:t0 + nt], ident)
                    m.then_inc(Z["back_ps"], 1)
                    n_ += 1
            for c, (t0, nt) in enumerate(CHUNKS):
                pe.wait_ge(Z["norm_scaled"], 3 + c + 1)
                for half in range(2):
                    b_ = (0, 1, 2, 3, 6, 7)[2 * c + half]
                    for k in range(4):
                        m = tr(ps[:, b_, k * nt:(k + 1) * nt],
                               n_tok[0:nt, c, (4 * half + k) * P:(4 * half + k + 1) * P], ident[0:nt, 0:nt])
                    m.then_inc(Z["norm_ps"], 1)
            pe.wait_ge(Z["norm_sb"], 12)
            pe.wait_ge(ld_router, 64)
            for c, (t0, nt) in enumerate(CHUNKS):
                for k in range(KD):
                    m = mm(ps[0:nt, 4, c * NE:(c + 1) * NE], fb[:, k, t0:t0 + nt], router[:, k, :],
                           start=(k == 0), stop=(k == KD - 1))
            m.then_inc(Z["lg_ps"], 1)
            pe.wait_ge(Z["mask_sb"], 1)
            for c, (t0, nt) in enumerate(CHUNKS):
                for k in range(c):
                    mm(ps[:, 5, c * NE:(c + 1) * NE], ones, mask[:, k, :], start=(k == 0), stop=False)
                mm(ps[:, 5, c * NE:(c + 1) * NE], tri[0:nt, :], mask[0:nt, c, :], start=(c == 0), stop=True)
            for c, (t0, nt) in enumerate(CHUNKS):
                m = mm(ps[:, 5, 3 * NE:4 * NE], ones[0:nt, :], mask[0:nt, c, :], start=(c == 0), stop=(c == 2))
            m.then_inc(Z["cnt_ps"], 1)
            for c, (t0, nt) in enumerate(CHUNKS):
                m = tr(ps[0:NE, 3, t0:t0 + nt], gate[0:nt, c, 0:NE], ident[0:nt, 0:nt])
            m.then_inc(Z["gtr_ps"], 1)
            pe.wait_ge(Z["gtr_sb"], 1)
            pe.wait_ge(ld_router, 64)
            for c, (t0, nt) in enumerate(CHUNKS):
                if c == 2:
                    pe.wait_ge(Z["bd_sb"], 1)
                for half in range(2):
                    m = mm(ps[0:nt, (6, 0, 6)[c] + half, :], gates_t[0:NE, t0:t0 + nt], b_down[:, half * 512:(half + 1) * 512],
                           start=True, stop=True)
                m.then_inc(Z["bd_ps"], 1)

            G_B, U_B, X_B, T_B, O_B, GT_B = 0, 1, 2, 3, 4, 5

            def gather(g):
                pe.wait_ge(Z["sel_rdy"], g + 1)
                for k in range(KD):
                    for c, (t0, nt) in enumerate(CHUNKS):
                        m = mm(ps[:, X_B, k * C:(k + 1) * C], n_tok[0:nt, c, k * P:(k + 1) * P], sel[0:nt, c, :],
                               start=(c == 0), stop=(c == 2))
                m.then_inc(Z["xg_ps"], 1)

            def combine(t):
                pe.wait_ge(Z["dn_sb"], t + 1)
                pe.wait_ge(Z["gt_sb"], t + 1)
                for c, (t0, nt) in enumerate(CHUNKS):
                    if c == 2:
                        pe.wait_ge(Z["cmb_read"], 3 * t + 1)
                    for half in range(2):
                        r = slice(64 * half, 64 * half + 64)
                        m = mm(ps[:, ((6, 7), (G_B, U_B), (6, 7))[c][half], :], g_t[r, t0:t0 + P], out_e[r, :],
                               start=True, stop=True)
                    m.then_inc(Z["cmb_ps"], 1)

            def expert(t, g, first):
                pe.wait_ge(Z["xe_rdy"], g + 1)
                pe.wait_ge(Z["hot_rdy"], t + 2)
                if first == 0:
                    pe.wait_ge(Z["bd_sb"], 3)
                    pe.wait_ge(ld_bup, 16)
                elif first == 1:
                    pe.wait_ge(Z["cmb_read"], 3 * t)
                for k in range(UP + 1):
                    if k < UP:
                        pe.wait_ge(up_in[k], 16 * t + 16)
                    for q in range(4):
                        w = (ring_up[:, k] if k < UP else b_up)[:, q * 512:(q + 1) * 512]
                        m = mm(ps[64 * (q % 2):64 * (q % 2) + 64, q // 2, :], xe[:, k, :] if k < UP else one_hot, w,
                               start=(k == 0), stop=(k == UP))
                    m.then_inc(Z["up_free"] if k < UP else Z["hid_ps"], 1)
                gather(g + 1)
                pe.wait_ge(Z["act_rdy"], t + 1)
                for j in range(4):
                    m = tr(ps[:, T_B, j * P:(j + 1) * P], act_v[:, j * P:(j + 1) * P], ident)
                m.then_inc(Z["at_ps"], 1)
                if first == 2:
                    combine(t - 1)
                pe.wait_ge(Z["selg_rdy"], t + 1)
                for c, (t0, nt) in enumerate(CHUNKS):
                    m = tr(ps[:, GT_B, t0:t0 + nt], sel_g[0:nt, c].rearrange("p a s -> p (a s)"), ident[0:nt, 0:nt])
                m.then_inc(Z["gt_ps"], 1)
                pe.wait_ge(Z["at_sb"], t + 1)
                for f in range(FF // P):
                    if f % 2 == 0:
                        pe.wait_ge(dn_in[f // 2], 16 * t + 16)
                    for half in range(2):
                        m = mm(ps[64 * half:64 * half + 64, O_B, :], act_t[:, f % 4, 64 * (f // 4):64 * (f // 4) + 64],
                               ring_dn[:, f, 512 * half:512 * half + 512], start=(f == 0), stop=(f == FF // P - 1))
                    if f % 2 == 1:
                        m.then_inc(Z["dn_free"], 1)
                if first == 2:
                    pe.wait_ge(Z["cmb_read"], 3 * t)

            def one_round(r):
                g0, t0 = r * (NE + 1), r * NE
                gather(g0)
                expert(t0, g0, 0 if isinstance(r, int) else 1)
                with pe.Fori(1, NE) as e:
                    expert(t0 + e, g0 + e, 2)
                combine(t0 + (NE - 1))

            after_rounds(pe, one_round)

            pe.wait_ge(ld_p, 64)
            for k in range(2):
                for c, (t0, nt) in enumerate(CHUNKS):
                    m = tr(ps[:, 2 + k, t0:t0 + nt], p_tok[0:nt, c, k * P:(k + 1) * P], ident[0:nt, 0:nt])
            m.then_inc(Z["pT_ps"], 1)
            pe.wait_ge(Z["pT_sb"], 1)
            for o in range(KD):
                b_ = 2 + o % 3
                if o >= 3:
                    pe.wait_ge(Z["pp_sb"], o - 2)
                for k in range(2):
                    m = mm(bank(b_, T), w_pp[:, k, o * P:(o + 1) * P], p_t[:, k, :], start=(k == 0), stop=(k == 1))
                m.then_inc(Z["pp_ps"], 1)
            for c, (t0, nt) in enumerate(CHUNKS):
                pe.wait_ge(Z["norm_scaled"], 6 + c + 1)
                for half in range(2):
                    b_ = (0, 1, 6, 7, 5, 2)[2 * c + half]
                    if b_ == 2:
                        pe.wait_ge(Z["pp_sb"], KD)
                    for k in range(4):
                        m = tr(ps[:, b_, k * nt:(k + 1) * nt],
                               n_tok[0:nt, c, (4 * half + k) * P:(4 * half + k + 1) * P], ident[0:nt, 0:nt])
                    m.then_inc(Z["norm_ps"], 1)
            pe.wait_ge(Z["norm_sb"], 18)
            pe.wait_ge(ld_gate_w, 64)

            def back(half):
                pe.wait_ge(Z["gz_mul"], 4 * (half + 1))
                for c, (t0, nt) in enumerate(CHUNKS):
                    n_ = 3 * half + c
                    if n_ >= 2:
                        pe.wait_ge(Z["back_add"], 6 + n_ - 1)
                    for k in range(4):
                        m = tr(ps[0:nt, 4 + n_ % 2, k * P:(k + 1) * P], fa[:, 4 * half + k, t0:t0 + nt], ident)
                    m.then_inc(Z["back_ps"], 1)

            for o in range(KD):
                b_ = o % 4
                if o >= 4:
                    pe.wait_ge(Z["gz_sig"], o - 3)
                for k in range(KD):
                    m = mm(bank(b_, T), w_gate[:, k, o * P:(o + 1) * P], fb[:, k, :], start=(k == 0), stop=(k == KD - 1))
                m.then_inc(Z["gz_ps"], 1)
                if o == 5:
                    back(0)
            back(1)

        @block.scalar
        def _(act):
            f = nc.scalar.activation
            n = [0]

            def chain(ins):
                n[0] += 1
                ins.then_inc(act_step, 1)
                act.wait_ge(act_step, n[0])

            r0 = 0
            for name, k in (("norm_mix", 8), ("norm_ffn", 8), ("norm_ple", 8), ("norm_attn_out", 4),
                            ("norm_ssm_out", 4)):
                act.dma_start(rows[r0:r0 + k, 0:P], A[name][0].rearrange("(k p) -> k p", p=P)).then_inc(ld_vec, 16)
                r0 += k
            act.dma_start(rows[r0:r0 + 4, 0:P], A["ssm_d"][0].rearrange("(k g) h -> k (g h)", k=4)).then_inc(ld_vec, 16)
            act.dma_start(rows[r0 + 4:r0 + 8, 0:P], A["b_glu"][0].rearrange("(k p) -> k p", p=P)).then_inc(ld_vec, 16)
            for j, name in enumerate(("ssm_lam_re", "ssm_lam_im")):
                act.dma_start(rows[0:ST, (12 + j) * P:(13 + j) * P], A[name][0].rearrange("(k g) p -> k (g p)", g=2)
                              ).then_inc(ld_par, 16)
            act.dma_start(rows[0:ST, 14 * P:14 * P + 2], A["ssm_log_step"][0].rearrange("(k g) -> k g", g=2)
                          ).then_inc(ld_par, 16)
            for r, name in enumerate(("ssm_c_re", "ssm_c_im")):
                act.dma_start(c_raw[:, r], A[name][0].rearrange("(k g) h p -> (g h) k p", k=4)).then_inc(ld_c, 16)
            for r, name in enumerate(("ssm_b_re", "ssm_b_im")):
                act.dma_start(b_raw[:, r], A[name][0].rearrange("(k g) p h -> (g p) k h", g=2)).then_inc(ld_b, 16)
            for r, name in enumerate(("state_ssm_re", "state_ssm_im")):
                act.dma_start(rows[:, (10 + r) * P:(11 + r) * P],
                              A[name][0].rearrange("b (k g) p -> (b k) (g p)", g=2)).then_inc(ld_x0, 16)
            act.dma_start(sink_b, A["sinks"][0].partition_broadcast(P)).then_inc(ld_sink, 16)
            for b_ in range(NB):
                act.dma_start(sink_s[HEADS * b_:HEADS * (b_ + 1), :], A["sinks"][0].unsqueeze(1)).then_inc(ld_sink, 16)

            R = [rows[0:ST, j * P:(j + 1) * P] for j in range(16)]
            act.wait_ge(ld_par, 48)
            f(rows[0:ST, 14 * P + 2:14 * P + 4], rows[0:ST, 14 * P:14 * P + 2], ACT.Exp).then_inc(Z["par_exp"], 1)
            act.wait_ge(Z["par_red"], 1)
            f(R[4], R[15], ACT.Exp).then_inc(Z["par_exp"], 1)
            for c, (t0, nt) in enumerate(CHUNKS):
                if c == 0:
                    act.wait_ge(ld_x, 64)
                f(n_tok[0:nt, c], x_tok[0:nt, c], ACT.Square, accum_out=stat[0:nt, c, 0:1]).then_inc(Z["norm_ssq"], 1)
            act.wait_ge(Z["norm_ssq"], 6)
            for c, (t0, nt) in enumerate(CHUNKS):
                f(stat[0:nt, c, 1:2], stat[0:nt, c, 0:1], ACT.Sqrt).then_inc(Z["norm_root"], 1)
            act.wait_ge(Z["par_red"], 3)
            f(R[3], R[9], ACT.Sin)
            f(R[15], R[9], ACT.Sin, scale=0.5).then_inc(Z["par_sin"], 1)

            act.wait_ge(Z["vec_ps"], 1)
            f(vecs[:], bank(7, V_N), ACT.Copy).then_inc(Z["vec_sb"], 1)
            act.wait_ge(Z["par_ps"], 1)
            f(pcols, ps[:, 6, 0:7 * ST].rearrange("p (a b) -> p a b", a=7), ACT.Copy).then_inc(Z["par_sb"], 1)
            for j in range(4):
                act.wait_ge(Z["u_ps"], j + 1)
                f(proj[:, 6 + j, :], bank(j, T), ACT.Copy).then_inc(Z["u_sb"], 1)
            act.wait_ge(Z["c_ps"], 1)
            f(c_t[0], ps[:, 4].rearrange("p (k n) -> p k n", k=4), ACT.Copy)
            f(c_t[1], ps[:, 5].rearrange("p (k n) -> p k n", k=4), ACT.Copy)
            f(c_t[2], ps[:, 4].rearrange("p (k n) -> p k n", k=4), ACT.Copy, scale=-1.0).then_inc(Z["c_sb"], 1)
            act.wait_ge(Z["x0_ps"], 1)
            f(x0_t, ps[:, 6, 0:2 * P].rearrange("p (r n) -> p r n", r=2), ACT.Copy).then_inc(Z["x0_sb"], 1)
            act.wait_ge(Z["b_ps"], 1)
            f(b_t[0], ps[:, 4].rearrange("p (k n) -> p k n", k=4), ACT.Copy)
            f(b_t[1], ps[:, 5].rearrange("p (k n) -> p k n", k=4), ACT.Copy).then_inc(Z["b_sb"], 1)

            def qkv():
                for n_, slot in enumerate((4, 5, 0, 1, 2, 3)):
                    act.wait_ge(Z["q_ps"], n_ + 1)
                    m = f(proj[:, slot, :], bank(5 + n_ % 3, T), ACT.Copy)
                    m.then_inc(Z["q_sb"], 1)
                act.dma_start(kc, A["cache_k_win"][0].rearrange("b w n d -> w b (n d)")).then_inc(ld_cache, 16)
                act.dma_start(vc, A["cache_v_win"][0].rearrange("b w n d -> w b (n d)")).then_inc(ld_cache, 16)

            def kv_tokens():
                act.wait_ge(Z["tok_ps"], 1)
                chain(f(kv_tok[:], ps[:, 7, 0:3 * P].rearrange("p (a n) -> p a n", a=3), ACT.Copy))
                chain(f(kv_new[:], ps[0:NB, 6, 0:2 * P].rearrange("p (a n) -> p a n", a=2), ACT.Copy))
                nc.scalar.nop().then_inc(Z["tok_sb"], 1)
                act.dma_start(O[2][0, 0].rearrange("w n d -> w (n d)"), kv_tok[:, 2]).then_inc(Z["st_k"], 16)
                act.dma_start(O[3][0, 0].rearrange("w n d -> w (n d)"), kv_tok[:, 1]).then_inc(Z["st_k"], 16)
                for j in range(2):
                    act.dma_start(O[6 + j][0].rearrange("b w n d -> b w (n d)")[:, WIN - 1], kv_new[:, j]
                                  ).then_inc(Z["st_k"], 16)

            def exps(b):
                K = P * (b + 1)
                act.wait_ge(Z["m_neg"], b + 1)
                for h in range(HEADS):
                    f(sc[:, h, 0:K], sc[:, h, 0:K], ACT.Exp, bias=mneg[:, h:h + 1], scale=SCALE,
                      accum_out=rsum[:, h:h + 1])
                f(esink, esink, ACT.Exp).then_inc(Z["expd"], 1)

            fills = [0]

            def p_copies(b):
                for q in range(2 * (b + 1)):
                    fills[0] += 1
                    act.wait_ge(Z["p_ps"], fills[0])
                    f(pt[:, 4 * q:4 * q + 4], ps[:, 5 + q % 3].rearrange("p (k n) -> p k n", k=4), ACT.Copy
                      ).then_inc(Z["p_sb"], 1)

            def att_root(b):
                act.wait_ge(Z["att_sb"], b + 1)
                f(pt_flat[:, 0:D_ATTN], att[:, b], ACT.Square,
                  accum_out=small[:, 80 + b:81 + b]).then_inc(Z["att_ssq"], 1)
                act.wait_ge(Z["att_ssq"], 2 * b + 2)
                f(small[:, 84 + b:85 + b], small[:, 82 + b:83 + b], ACT.Sqrt).then_inc(Z["att_root"], 1)

            def cache_copies():
                for q, b_ in enumerate((5, 7)):
                    act.wait_ge(Z["kct_ps"], q + 1)
                    f(kc_t[:, 4 * q:4 * q + 4, 0:WIN], ps[:, b_].rearrange("p (k n) -> p k n", k=4), ACT.Copy
                      ).then_inc(Z["kct_sb"], 1)
                f(kc_t[:, :, WIN:WIN + 1], proj[:, 4, SEQ:T].unsqueeze(2), ACT.Copy).then_inc(Z["kct_sb"], 1)

            def sample_exp():
                act.wait_ge(Z["s_mneg"], 1)
                f(s_sc[:], s_sc[:], ACT.Exp, bias=s_small[0:64, 1:2], scale=SCALE, accum_out=s_small[0:64, 2:3])
                f(s_small[0:64, 3:4], s_small[0:64, 3:4], ACT.Exp).then_inc(Z["s_expd"], 1)

            def sample_root():
                act.wait_ge(Z["s_ops"], 1)
                act.wait_ge(Z["s_groot"], 1)
                f(s_small[0:64, 6:7], s_small[0:64, 5:6], ACT.Sqrt).then_inc(Z["s_groot"], 1)

            for i in range(ST):
                if i == AT_QKV:
                    qkv()
                if i == AT_KVTOK:
                    kv_tokens()
                if i == AT_B0:
                    exps(0)
                if i == AT_B0V:
                    p_copies(0)
                    att_root(0)
                if i == AT_B1:
                    exps(1)
                if i == AT_B1V:
                    p_copies(1)
                    att_root(1)
                if i == AT_S:
                    cache_copies()
                    sample_exp()
                if i == AT_SV:
                    sample_root()

            act.wait_ge(Z["ypre"], 1)
            f(y_t, proj[:, 6:10], ACT.Gelu_apprx_tanh).then_inc(Z["gelu"], 1)
            for c in range(KM):
                act.wait_ge(Z["glu_ps"], c + 1)
                if c >= 2:
                    act.wait_ge(Z["ssm_y"], c - 1)
                f(kc_t.rearrange("p b n -> p (b n)")[:, (c % 2) * T:(c % 2 + 1) * T], bank(c, T), ACT.Sigmoid,
                  bias=vecs[:, V_GLU + c:V_GLU + c + 1]).then_inc(Z["glu_sig"], 1)
            act.wait_ge(Z["state_ps"], 1)
            f(x0_t, ps[:, 7, 0:2 * P].rearrange("p (r n) -> p r n", r=2), ACT.Copy)
            chain(f(mini[0:ST, :].rearrange("p (r n) -> p r n", r=2),
                    ps[0:ST, 7, 2 * P:4 * P].rearrange("p (r n) -> p r n", r=2), ACT.Copy))
            for c in range(KM):
                act.wait_ge(Z["ssm_y"], c + 1)
                if c >= 2:
                    act.wait_ge(Z["ssm_ssq"], c - 1)
                f(sq[:, c % 2], fb[:, 4 + c, :], ACT.Square).then_inc(Z["ssm_sq"], 1)
            act.wait_ge(Z["ssm_ssq"], KM)
            act.wait_ge(Z["ssm_root"], 1)
            f(sq[:, 1], sq[:, 0], ACT.Sqrt).then_inc(Z["ssm_root"], 1)
            for r in range(2):
                act.dma_start(O[8 + r][0].rearrange("b (k g) p -> (b k) (g p)", g=2), x0_t[:, r]).then_inc(Z["st_k"], 16)
                act.dma_start(O[4 + r][0, 0].rearrange("(k g) p -> k (g p)", g=2), mini[0:ST, r * P:(r + 1) * P]
                              ).then_inc(Z["st_k"], 16)
            for o in range(KD):
                act.wait_ge(Z["mix_ps"], o + 1)
                f(fa[:, o, :], bank(o % 4, T), ACT.Copy).then_inc(Z["mix_sb"], 1)
            for c, (t0, nt) in enumerate(CHUNKS):
                act.wait_ge(Z["back_add"], 4 + c)
                f(n_tok[0:nt, c], x_tok[0:nt, c], ACT.Square, accum_out=stat[0:nt, c, 0:1]).then_inc(Z["norm_ssq"], 1)
            act.wait_ge(Z["norm_ssq"], 12)
            for c, (t0, nt) in enumerate(CHUNKS):
                f(stat[0:nt, c, 1:2], stat[0:nt, c, 0:1], ACT.Sqrt).then_inc(Z["norm_root"], 1)
            act.wait_ge(Z["topv"], 1)
            for c, (t0, nt) in enumerate(CHUNKS):
                f(top[0:nt, c, 16:20], top[0:nt, c, 0:4], ACT.Exp, bias=top[0:nt, c, 12:13],
                  accum_out=top[0:nt, c, 20:21]).then_inc(Z["w_exp"], 1)
            act.wait_ge(Z["gtr_ps"], 1)
            f(gates_t[0:NE, :], ps[0:NE, 3, 0:T], ACT.Copy).then_inc(Z["gtr_sb"], 1)
            act.wait_ge(Z["hot_rdy"], 1)
            act.dma_start(b_up[0:NE, :], A["b_up"][0]).then_inc(ld_bup, 16)
            act.dma_start(p_tok[:, 0:2], A["p_prompt"][0, 0].rearrange("(c p) n -> p c n", p=P)).then_inc(ld_p, 16)
            act.dma_start(p_tok[0:NB, 2], A["p_sample"][0].rearrange("b l n -> (b l) n")).then_inc(ld_p, 16)

            def expert(t):
                act.wait_ge(Z["g_rdy"], t + 1)
                f(sig, g_lim, ACT.Sigmoid, scale=ALPHA).then_inc(Z["sig_rdy"], 1)
                act.wait_ge(Z["at_ps"], t + 1)
                f(act_t, ps[:, 3].rearrange("p (j n) -> p j n", j=4), ACT.Copy).then_inc(Z["at_sb"], 1)
                act.wait_ge(Z["gt_ps"], t + 1)
                f(g_t[:, 0:T], ps[:, 5, 0:T], ACT.Copy).then_inc(Z["gt_sb"], 1)
                act.wait_ge(Z["dn_free"], DN * t + DN)
                f(out_e, ps[:, 4], ACT.Copy).then_inc(Z["dn_sb"], 1)

            def one_round(r):
                with act.Fori(0, NE) as e:
                    expert(r * NE + e)

            after_rounds(act, one_round)

            for k in range(2):
                act.dma_start(w_pp[:, k], A["w_ple_proj"][0, k * P:(k + 1) * P, :]).then_inc(ld_p, 16)
            act.wait_ge(Z["pT_ps"], 1)
            f(p_t, ps[:, 2:4, 0:T], ACT.Copy).then_inc(Z["pT_sb"], 1)
            for c, (t0, nt) in enumerate(CHUNKS):
                if c == 0:
                    act.wait_ge(Z["all_added"], 1)
                f(n_tok[0:nt, c], x_tok[0:nt, c], ACT.Square, accum_out=stat[0:nt, c, 0:1]).then_inc(Z["norm_ssq"], 1)
            act.wait_ge(Z["norm_ssq"], 18)
            for c, (t0, nt) in enumerate(CHUNKS):
                f(stat[0:nt, c, 1:2], stat[0:nt, c, 0:1], ACT.Sqrt).then_inc(Z["norm_root"], 1)
            for o in range(KD):
                act.wait_ge(Z["pp_ps"], o + 1)
                f(fa[:, o, :], bank(2 + o % 3, T), ACT.Copy).then_inc(Z["pp_sb"], 1)
            for o in range(KD):
                act.wait_ge(Z["gz_ps"], o + 1)
                if o >= 2:
                    act.wait_ge(Z["gz_mul"], o - 1)
                f(sg_t[:, o % 2], bank(o % 4, T), ACT.Sigmoid).then_inc(Z["gz_sig"], 1)
            for c, (t0, nt) in enumerate(CHUNKS):
                act.wait_ge(Z["back_add"], 6 + 4 + c)
                f(n_tok[0:nt, c], x_tok[0:nt, c], ACT.Square, accum_out=stat[0:nt, c, 0:1]).then_inc(Z["norm_ssq"], 1)
            act.wait_ge(Z["norm_ssq"], 24)
            for c, (t0, nt) in enumerate(CHUNKS):
                f(stat[0:nt, c, 1:2], stat[0:nt, c, 0:1], ACT.Sqrt).then_inc(Z["norm_root"], 1)
            act.wait_ge(Z["st_k"], 32 + 16 * 8)

        @block.vector
        def _(dve):
            V = nc.vector
            n = [0]

            def chain(ins):
                n[0] += 1
                ins.then_inc(dve_step, 1)
                dve.wait_ge(dve_step, n[0])

            def norm_rows(n_):
                dve.wait_ge(Z["norm_ssq"], 6 * n_ + 3)
                for c, (t0, nt) in enumerate(CHUNKS):
                    V.tensor_scalar(stat[0:nt, c, 0:1], stat[0:nt, c, 0:1], 1.0 / D, EPS, ALU.mult, ALU.add
                                    ).then_inc(Z["norm_ssq"], 1)
                for c, (t0, nt) in enumerate(CHUNKS):
                    dve.wait_ge(Z["norm_root"], 3 * n_ + c + 1)
                    chain(V.reciprocal(stat[0:nt, c, 2:3], stat[0:nt, c, 1:2]))
                    if n_ < 3:
                        V.tensor_scalar(n_tok[0:nt, c], x_tok[0:nt, c], stat[0:nt, c, 2:3], None, ALU.mult
                                        ).then_inc(Z["norm_scaled"], 1)

            R = [rows[0:ST, j * P:(j + 1) * P] for j in range(16)]
            l_re, l_im = R[12], R[13]
            dt = rows[0:ST, 14 * P + 2:14 * P + 4].unsqueeze(2).to_broadcast([ST, 2, S])

            def halves(x):
                return x.rearrange("k (g p) -> k g p", g=2)

            dve.wait_ge(Z["par_exp"], 1)
            V.tensor_tensor(halves(R[15]), halves(l_re), dt, ALU.mult).then_inc(Z["par_red"], 1)
            chain(V.tensor_tensor(halves(R[9]), halves(l_im), dt, ALU.mult))
            two_pi_hi, magic = 6.28125, 12582912.0
            two_pi_lo = 2.0 * np.pi - two_pi_hi
            chain(V.tensor_scalar(R[8], R[9], 1.0 / (2.0 * np.pi), magic, ALU.mult, ALU.add))
            chain(V.tensor_scalar(R[8], R[8], -magic, None, ALU.add))
            chain(V.scalar_tensor_tensor(R[9], R[8], -two_pi_hi, R[9], ALU.mult, ALU.add))
            chain(V.scalar_tensor_tensor(R[9], R[8], -float(two_pi_lo), R[9], ALU.mult, ALU.add))
            dve.wait_ge(Z["par_exp"], 2)
            V.tensor_scalar(R[9], R[9], 3.1415925, -3.1415925, ALU.min, ALU.max).then_inc(Z["par_red"], 2)
            norm_rows(0)
            chain(V.tensor_tensor(R[8], l_re, l_re, ALU.mult))
            chain(V.tensor_tensor(R[7], l_im, l_im, ALU.mult))
            chain(V.tensor_tensor(R[8], R[8], R[7], ALU.add))
            chain(V.reciprocal(R[8], R[8]))
            dve.wait_ge(Z["par_sin"], 1)
            chain(V.tensor_tensor(R[2], R[15], R[15], ALU.mult))
            chain(V.tensor_scalar(R[2], R[2], -2.0, 1.0, ALU.mult, ALU.add))
            chain(V.tensor_tensor(R[5], R[4], R[2], ALU.mult))
            chain(V.tensor_tensor(R[6], R[4], R[3], ALU.mult))
            chain(V.tensor_scalar(R[9], R[5], -1.0, None, ALU.add))
            chain(V.tensor_tensor(R[7], R[9], l_re, ALU.mult))
            chain(V.tensor_tensor(R[15], R[6], l_im, ALU.mult))
            chain(V.tensor_tensor(R[7], R[7], R[15], ALU.add))
            chain(V.tensor_tensor(R[7], R[7], R[8], ALU.mult))
            chain(V.tensor_tensor(R[15], R[9], l_im, ALU.mult))
            chain(V.tensor_tensor(R[9], R[6], l_re, ALU.mult))
            chain(V.tensor_tensor(R[9], R[9], R[15], ALU.subtract))
            V.tensor_tensor(R[8], R[9], R[8], ALU.mult).then_inc(Z["par_rows"], 1)
            dve.wait_ge(Z["vec_sb"], 1)
            for c, (t0, nt) in enumerate(CHUNKS):
                for half in range(2):
                    dve.wait_ge(Z["norm_ps"], 0 + 2 * c + half + 1)
                    V.tensor_tensor(fa[:, 4 * half:4 * half + 4, t0:t0 + nt],
                                    ps[:, 2 * c + half, 0:4 * nt].rearrange("p (k n) -> p k n", k=4),
                                    col(vecs[:, V_MIX + 4 * half:V_MIX + 4 * half + 4], nt), ALU.mult
                                    ).then_inc(Z["norm_sb"], 1)
            dve.wait_ge(Z["par_sb"], 1)

            def scan(i):
                a = i % 2
                cs = cos_t[:, a].unsqueeze(1).to_broadcast([P, 2, SEQ])
                sn = sin_t[:, a].unsqueeze(1).to_broadcast([P, 2, SEQ])
                decay = pcols[:, 2, i:i + 1].to_broadcast([P, SEQ])
                dve.wait_ge(Z["trig"], i + 1)
                dve.wait_ge(Z["bu_ps"], i + 1)
                V.tensor_copy(bu_s[:, :, i, :], ps[:, 0:2, SEQ:T])
                V.tensor_tensor(prod_p, ps[:, 0:2, 0:SEQ], cs, ALU.mult)
                q = ps[:, 2].rearrange("p (r t) -> p r t", r=2)
                z = ps[:, 3].rearrange("p (r t) -> p r t", r=2)
                m = V.tensor_tensor(q, ps[:, 0:2, 0:SEQ], sn, ALU.mult)
                m.then_inc(Z["bu_read"], 1)
                dve.wait_ge(Z["bu_read"], i + 1)
                V.tensor_tensor(z_in[:, 0], prod_p[:, 0], q[:, 1], ALU.add)
                chain(V.tensor_tensor(z_in[:, 1], prod_p[:, 1], q[:, 0], ALU.subtract))
                V.tensor_tensor_scan(z[:, 0], decay, z_in[:, 0], 0.0, ALU.mult, ALU.add)
                chain(V.tensor_tensor_scan(z[:, 1], decay, z_in[:, 1], 0.0, ALU.mult, ALU.add))
                if i >= 2:
                    dve.wait_ge(Z["y_rot"], i - 1)
                    dve.wait_ge(Z["last_in"], i - 1)
                V.tensor_tensor(rot_c[:, a], z, cs, ALU.mult)
                V.tensor_tensor(rot_s[:, a], z, sn, ALU.mult).then_inc(Z["rot_ready"], 1)

            def biases(b):
                K = P * (b + 1)
                for c in range(4):
                    dve.wait_ge(Z["score_ps"], 4 * b + c + 1)
                    for n_ in range(KV):
                        h = 4 * n_ + c
                        m = V.scalar_tensor_tensor(sc[:, h, 0:K], kst[:, K_DIST + 2 * P - K:K_DIST + 2 * P],
                                                   -SLOPES[h] / SCALE, bank(5 + n_, K), ALU.mult, ALU.add)
                    m.then_inc(Z["score_read"], 1)
                if b == 0:
                    dve.wait_ge(ld_sink, 16 * (NB + 1))
                dve.wait_ge(Z["score_read"], 4 * b + 4)
                chain(V.tensor_reduce(mx, sc[:, :, 0:K], AX.X, ALU.max))
                chain(V.scalar_tensor_tensor(mx, mx, SCALE, sink_b, ALU.mult, ALU.max))
                chain(V.tensor_scalar(mneg, mx, -1.0, None, ALU.mult))
                V.tensor_tensor(esink, sink_b, mneg, ALU.add).then_inc(Z["m_neg"], 1)

            def attended(b):
                dve.wait_ge(Z["expd"], b + 1)
                chain(V.tensor_tensor(rden, rsum, esink, ALU.add))
                chain(V.reciprocal(rden, rden))
                dve.wait_ge(Z["o_ps"], b + 1)
                V.tensor_tensor(att[:, b].rearrange("p (h d) -> p h d", h=HEADS),
                                ps[:, 5].rearrange("p (h d) -> p h d", h=HEADS), col(rden, HD), ALU.mult
                                ).then_inc(Z["att_sb"], 1)
                dve.wait_ge(Z["att_ssq"], 2 * b + 1)
                V.tensor_scalar(small[:, 82 + b:83 + b], small[:, 80 + b:81 + b], 1.0 / D_ATTN, EPS, ALU.mult, ALU.add
                                ).then_inc(Z["att_ssq"], 1)
                dve.wait_ge(Z["att_root"], b + 1)
                chain(V.reciprocal(small[:, 86 + b:87 + b], small[:, 84 + b:85 + b]))
                V.tensor_scalar(att[:, b], att[:, b], small[:, 86 + b:87 + b], None, ALU.mult
                                ).then_inc(Z["att_scaled"], 1)
                dve.wait_ge(Z["att_ps"], b + 1)
                V.tensor_tensor(fb[:, 0:4, b * P:(b + 1) * P], ps[:, 6].rearrange("p (k n) -> p k n", k=4),
                                col(vecs[:, V_OUT:V_OUT + 4], P), ALU.mult).then_inc(Z["att_t"], 1)

            sp72 = spread.rearrange("p (b s) -> p b s", s=72)

            def sample_bias():
                chain(V.memset(spread, 0.0))
                for c in range(4):
                    for n_ in range(KV):
                        r = slice(64 * n_, 64 * n_ + 64)
                        m = V.tensor_copy(sp72[r, :, 4 * n_ + c:4 * n_ + c + 1], proj[r, c, SEQ:T].unsqueeze(2))
                m.then_inc(Z["q_spread"], 1)
                dve.wait_ge(Z["ssc_ps"], 1)
                chain(V.tensor_tensor(s_sc[:], ps[0:64, 5, 0:WIN + 1], kst[0:64, K_SBIAS:K_SBIAS + WIN + 1], ALU.add))
                chain(V.tensor_reduce(s_small[0:64, 0:1], s_sc[:], AX.X, ALU.max))
                chain(V.scalar_tensor_tensor(s_small[0:64, 0:1], s_small[0:64, 0:1], SCALE, sink_s[0:64], ALU.mult, ALU.max))
                chain(V.tensor_scalar(s_small[0:64, 1:2], s_small[0:64, 0:1], -1.0, None, ALU.mult))
                V.tensor_tensor(s_small[0:64, 3:4], sink_s[0:64], s_small[0:64, 1:2], ALU.add).then_inc(Z["s_mneg"], 1)

            def sample_out():
                dve.wait_ge(Z["s_expd"], 1)
                V.tensor_scalar(s_own[:], kst[0:64, K_OWN:K_OWN + NB], s_sc[:, WIN:WIN + 1], None, ALU.mult
                                ).then_inc(Z["s_oready"], 1)
                chain(V.tensor_tensor(s_small[0:64, 4:5], s_small[0:64, 2:3], s_small[0:64, 3:4], ALU.add))
                chain(V.reciprocal(s_small[0:64, 4:5], s_small[0:64, 4:5]))
                dve.wait_ge(Z["s_pps"], 1)
                V.tensor_copy(s_ownT[:], ps[0:NB, 7, 64:128]).then_inc(Z["s_pspread"], 1)
                V.tensor_copy(sp72[:, :, 0:HEADS], ps[:, 7, 0:64].rearrange("p (b h) -> p b h", b=NB)
                              ).then_inc(Z["s_pspread"], 1)
                dve.wait_ge(Z["s_ops"], 1)
                chain(V.tensor_scalar(s_o[:, 0], ps[0:64, 5, 0:64], kst[0:64, K_HALF:K_HALF + 1], s_small[0:64, 4:5],
                                      ALU.mult, ALU.mult))
                chain(V.tensor_scalar(s_o[:, 1], ps[0:64, 5, 64:128], kst[0:64, K_HALF + 1:K_HALF + 2],
                                      s_small[0:64, 4:5], ALU.mult, ALU.mult))
                chain(V.tensor_tensor(s_o[:, 0], s_o[:, 0], s_o[:, 1], ALU.add))
                chain(V.tensor_tensor(s_o[:, 1], s_o[:, 0], s_o[:, 0], ALU.mult))
                V.tensor_reduce(s_small[0:64, 5:6], s_o[:, 1], AX.X, ALU.add).then_inc(Z["s_ossq"], 1)
                dve.wait_ge(Z["s_gps"], 1)
                V.tensor_scalar(s_small[0:64, 5:6], ps[0:64, 7, 0:1], 1.0 / D_ATTN, EPS, ALU.mult, ALU.add
                                ).then_inc(Z["s_groot"], 1)
                dve.wait_ge(Z["s_groot"], 2)
                chain(V.reciprocal(s_small[0:64, 7:8], s_small[0:64, 6:7]))
                chain(V.tensor_scalar(s_o[:, 0], s_o[:, 0], s_small[0:64, 7:8], None, ALU.mult))
                V.tensor_copy(s_o[:, 1], s_o[:, 0]).then_inc(Z["s_onorm"], 1)
                dve.wait_ge(Z["s_otps"], 1)
                for par in range(2):
                    r = slice(64 * par, 64 * par + 64)
                    m = V.tensor_tensor(fb[r, 0:4, SEQ:T],
                                        ps[r, 6, 0:64].rearrange("p (b c a) -> p a c b", b=NB, a=2)[:, par],
                                        col(vecs[r, V_OUT:V_OUT + 4], NB), ALU.mult)
                m.then_inc(Z["s_ot"], 1)

            for i in range(ST + 1):
                if i < ST:
                    scan(i)
                if i == AT_B0:
                    biases(0)
                if i == AT_B0V:
                    attended(0)
                if i == AT_B1:
                    biases(1)
                if i == AT_B1V:
                    attended(1)
                if i == AT_S:
                    sample_bias()
                if i == AT_SV:
                    sample_out()
                if i >= 4 and i % 4 == 0:
                    c = i // 4 - 1
                    dve.wait_ge(Z["y_rot"], 4 * c + 4)
                    dve.wait_ge(Z["bu_ps"], 4 * c + 4)
                    V.scalar_tensor_tensor(proj[:, 6 + c, 0:SEQ], proj[:, 6 + c, 0:SEQ], vecs[:, V_D + c:V_D + c + 1],
                                           ps[:, 4, 0:SEQ], ALU.mult, ALU.add).then_inc(Z["y_read"], 1)
            dve.wait_ge(Z["x0_sb"], 1)
            x0 = [x0_t[:, r].rearrange("p (b a) -> p a b", a=ST) for r in range(2)]
            lr, li = col(pcols[:, 3], NB), col(pcols[:, 4], NB)
            t1 = s5_mem[:, 1280:1408].rearrange("p (a b) -> p a b", a=ST)
            for r, (f0, f1, op) in enumerate(((lr, li, ALU.subtract), (li, lr, ALU.add))):
                chain(V.tensor_tensor(xs_new[:, r], x0[0], f0, ALU.mult))
                chain(V.tensor_tensor(t1, x0[1], f1, ALU.mult))
                chain(V.tensor_tensor(xs_new[:, r], xs_new[:, r], t1, op))
                chain(V.tensor_tensor(xs_new[:, r], xs_new[:, r], bu_s[:, r], ALU.add))
            V.engine_nop().then_inc(Z["state_s"], 1)
            dve.wait_ge(Z["ys_ps"], 1)
            for c in range(KM):
                chain(V.scalar_tensor_tensor(proj[:, 6 + c, SEQ:T], proj[:, 6 + c, SEQ:T], vecs[:, V_D + c:V_D + c + 1],
                                             ps[:, 5, NB * c:NB * c + NB], ALU.mult, ALU.add))
            V.engine_nop().then_inc(Z["ypre"], 1)
            dve.wait_ge(Z["last_in"], ST)
            V.engine_nop().then_inc(Z["s5_free"], 1)
            for c in range(KM):
                dve.wait_ge(Z["glu_sig"], c + 1)
                V.tensor_tensor(fb[:, 4 + c, :], y_t[:, c, :],
                                kc_t.rearrange("p b n -> p (b n)")[:, (c % 2) * T:(c % 2 + 1) * T], ALU.mult
                                ).then_inc(Z["ssm_y"], 1)
            dve.wait_ge(Z["ssm_ssq"], KM)
            V.tensor_scalar(sq[:, 0], bank(6, T), 1.0 / D_SSM, EPS, ALU.mult, ALU.add).then_inc(Z["ssm_root"], 1)
            dve.wait_ge(Z["ssm_root"], 2)
            chain(V.reciprocal(sq[:, 0], sq[:, 1]))
            for c in range(KM):
                V.scalar_tensor_tensor(fb[:, 4 + c, :], fb[:, 4 + c, :], vecs[:, V_OUT + 4 + c:V_OUT + 5 + c], sq[:, 0],
                                       ALU.mult, ALU.mult).then_inc(Z["ssm_n"], 1)
            n_ = 0
            for half in range(2):
                for c, (t0, nt) in enumerate(CHUNKS):
                    n_ += 1
                    dve.wait_ge(Z["back_ps"], n_)
                    xh = x_tok[0:nt, c, 512 * half:512 * half + 512]
                    V.tensor_tensor(xh, xh, ps[0:nt, 4 + (n_ - 1) % 2, :], ALU.add).then_inc(Z["back_add"], 1)
            norm_rows(1)
            for c, (t0, nt) in enumerate(CHUNKS):
                for half in range(2):
                    dve.wait_ge(Z["norm_ps"], 6 + 2 * c + half + 1)
                    b_ = (0, 1, 2, 3, 6, 7)[2 * c + half]
                    V.tensor_tensor(fb[:, 4 * half:4 * half + 4, t0:t0 + nt],
                                    ps[:, b_, 0:4 * nt].rearrange("p (k n) -> p k n", k=4),
                                    col(vecs[:, V_FFN + 4 * half:V_FFN + 4 * half + 4], nt), ALU.mult
                                    ).then_inc(Z["norm_sb"], 1)
            V.memset(mask, 0.0)
            V.memset(gate[:], 0.0)
            chain(V.memset(rank[:], -1.0))
            chain(V.memset(g_t, 0.0))
            V.engine_nop().then_inc(Z["region_free"], 1)
            dve.wait_ge(Z["lg_ps"], 1)
            dve.wait_ge(ld_router, 64)
            for c, (t0, nt) in enumerate(CHUNKS):
                r = slice(0, nt)
                chain(V.tensor_tensor(logits[r, c], ps[r, 4, c * NE:(c + 1) * NE], router_b[r], ALU.add))
                chain(V.max(top[r, c, 0:8], logits[r, c]))
                V.tensor_scalar(top[r, c, 12:13], top[r, c, 0:1], -1.0, None, ALU.mult)
                chain(V.max_index(top_i[r, c], top[r, c, 0:8], logits[r, c]))
                chain(V.tensor_copy(top[r, c, 24:32], top_i[r, c]))
            V.engine_nop().then_inc(Z["topv"], 1)
            for c, (t0, nt) in enumerate(CHUNKS):
                r = slice(0, nt)
                iota = kst[r, K_IOTA:K_IOTA + NE].unsqueeze(1).to_broadcast([nt, TOPK, NE])
                chain(V.tensor_tensor(pick[r], iota, col(top[r, c, 24:28], NE), ALU.is_equal))
                chain(V.tensor_reduce(mask[r, c], pick[r].rearrange("p k e -> p e k"), AX.X, ALU.add))
                dve.wait_ge(Z["w_exp"], c + 1)
                chain(V.reciprocal(top[r, c, 21:22], top[r, c, 20:21]))
                chain(V.tensor_scalar(top[r, c, 16:20], top[r, c, 16:20], top[r, c, 21:22], None, ALU.mult))
                chain(V.tensor_tensor(pick[r], pick[r], col(top[r, c, 16:20], NE), ALU.mult))
                chain(V.tensor_reduce(gate[r, c, 0:NE], pick[r].rearrange("p k e -> p e k"), AX.X, ALU.add))
            V.engine_nop().then_inc(Z["mask_sb"], 1)
            dve.wait_ge(Z["cnt_ps"], 1)
            chain(V.scalar_tensor_tensor(rank[:, :, 0:NE], ps[:, 5, 0:3 * NE].rearrange("p (c n) -> p c n", c=3), 1.0, mask,
                                         ALU.add, ALU.mult))
            chain(V.tensor_scalar(rank[:, :, 0:NE], rank[:, :, 0:NE], -1.0, None, ALU.add))
            chain(V.tensor_reduce(n_max[:], ps[:, 5, 3 * NE:4 * NE], AX.X, ALU.max))
            V.tensor_copy(n_int[:], n_max[0:1]).then_inc(Z["n_ready"], 1)
            for c, (t0, nt) in enumerate(CHUNKS):
                dve.wait_ge(Z["bd_ps"], c + 1)
                V.tensor_tensor(x_tok[0:nt, c].rearrange("p (a n) -> p a n", a=2),
                                x_tok[0:nt, c].rearrange("p (a n) -> p a n", a=2),
                                ps[0:nt, (6, 0, 6)[c]:(6, 0, 6)[c] + 2, :], ALU.add).then_inc(Z["bd_sb"], 1)

            dve.wait_ge(Z["bd_sb"], 3)

            def select(e):
                iota = kst[:, K_IOTA:K_IOTA + C].unsqueeze(1).to_broadcast([P, 3, C])
                return V.tensor_tensor(sel, iota, rank[:, :, bass.ds(e, 1)].to_broadcast([P, 3, C]), ALU.is_equal)

            def gathered(g):
                dve.wait_ge(Z["xg_ps"], g + 1)
                V.tensor_tensor(xe, ps[:, 2].rearrange("p (k s) -> p k s", k=KD), col(vecs[:, V_FFN:V_FFN + KD], C),
                                ALU.mult).then_inc(Z["xe_rdy"], 1)

            def added(t):
                for c, (t0, nt) in enumerate(CHUNKS):
                    dve.wait_ge(Z["cmb_ps"], 3 * t + c + 1)
                    xh = x_tok[0:nt, c].rearrange("p (a n) -> p a n", a=2)
                    b_ = (6, 0, 6)[c]
                    V.tensor_tensor(xh, xh, ps[0:nt, b_:b_ + 2, :], ALU.add).then_inc(Z["cmb_read"], 1)
                dve.wait_ge(Z["cmb_read"], 3 * t + 3)

            def expert(e, t, g, first):
                dve.wait_ge(Z["sel_rdy"], g + 1)
                if not first:
                    dve.wait_ge(Z["gt_ps"], t)
                for a in range(2):
                    m = V.tensor_tensor(sel_g[:, :, a], sel, gate[:, :, bass.ds(e, 1)].to_broadcast([P, 3, C]), ALU.mult)
                m.then_inc(Z["selg_rdy"], 1)
                dve.wait_ge(Z["selg_rdy"], t + 1)
                select(e + 1).then_inc(Z["sel_rdy"], 1)
                dve.wait_ge(Z["hid_ps"], t + 1)
                V.tensor_scalar(g_lim, bank(0), LIMIT, None, ALU.min).then_inc(Z["g_rdy"], 1)
                V.tensor_scalar(u_lim, bank(1), -LIMIT, LIMIT, ALU.max, ALU.min).then_inc(dve_loop, 1)
                dve.wait_ge(dve_loop, 2 * t + 1)
                dve.wait_ge(Z["g_rdy"], t + 1)
                V.scalar_tensor_tensor(u_lim, u_lim, 1.0, g_lim, ALU.add, ALU.mult).then_inc(dve_loop, 1)
                dve.wait_ge(dve_loop, 2 * t + 2)
                dve.wait_ge(Z["sig_rdy"], t + 1)
                V.tensor_tensor(act_v, u_lim, sig, ALU.mult).then_inc(Z["act_rdy"], 1)
                if not first:
                    added(t - 1)
                gathered(g + 1)

            def one_round(r):
                g0, t0 = r * (NE + 1), r * NE
                if not isinstance(r, int):
                    dve.wait_ge(Z["rank_sb"], r)
                select(0).then_inc(Z["sel_rdy"], 1)
                gathered(g0)
                expert(0, t0, g0, True)
                with dve.Fori(1, NE) as e:
                    expert(e, t0 + e, g0 + e, False)
                added(t0 + (NE - 1))
                V.tensor_scalar(rank[:], rank[:], -float(C), None, ALU.add).then_inc(Z["rank_sb"], 1)

            after_rounds(dve, one_round)
            V.engine_nop().then_inc(Z["all_added"], 1)

            norm_rows(2)
            for c, (t0, nt) in enumerate(CHUNKS):
                for half in range(2):
                    dve.wait_ge(Z["norm_ps"], 12 + 2 * c + half + 1)
                    b_ = (0, 1, 6, 7, 5, 2)[2 * c + half]
                    V.tensor_tensor(fb[:, 4 * half:4 * half + 4, t0:t0 + nt],
                                    ps[:, b_, 0:4 * nt].rearrange("p (k n) -> p k n", k=4),
                                    col(vecs[:, V_PLE + 4 * half:V_PLE + 4 * half + 4], nt), ALU.mult
                                    ).then_inc(Z["norm_sb"], 1)

            def residual(half):
                for c, (t0, nt) in enumerate(CHUNKS):
                    n_ = 3 * half + c
                    dve.wait_ge(Z["back_ps"], 6 + n_ + 1)
                    xh = x_tok[0:nt, c, 512 * half:512 * half + 512]
                    V.tensor_tensor(xh, xh, ps[0:nt, 4 + n_ % 2, :], ALU.add).then_inc(Z["back_add"], 1)

            dve.wait_ge(Z["pp_sb"], KD)
            for o in range(KD):
                dve.wait_ge(Z["gz_sig"], o + 1)
                V.tensor_tensor(fa[:, o, :], fa[:, o, :], sg_t[:, o % 2], ALU.mult).then_inc(Z["gz_mul"], 1)
                if o == 5:
                    residual(0)
            residual(1)
            norm_rows(3)
            dve.wait_ge(ld_router, 64)
            for c, (t0, nt) in enumerate(CHUNKS):
                V.scalar_tensor_tensor(n_tok[0:nt, c], x_tok[0:nt, c], stat[0:nt, c, 2:3], final_g[0:nt, :], ALU.mult,
                                       ALU.mult).then_inc(Z["f_out"], 1)


_INS = ['x_prompt', 'x_sample', 'cache_k_win', 'cache_v_win', 'state_ssm_re', 'state_ssm_im', 'p_prompt', 'p_sample',
        'norm_mix', 'w_in', 'sinks', 'ssm_lam_re', 'ssm_lam_im', 'ssm_log_step', 'ssm_b_re', 'ssm_b_im', 'ssm_c_re',
        'ssm_c_im', 'ssm_d', 'w_glu', 'b_glu', 'norm_attn_out', 'norm_ssm_out', 'w_out', 'norm_ffn', 'w_router',
        'b_router', 'w_up', 'b_up', 'w_down', 'b_down', 'norm_ple', 'w_ple_gate', 'w_ple_proj', 'norm_final']
_OUTS = [(1, SEQ, D), (NB, 1, D), (1, 1, WIN, KV, HD), (1, 1, WIN, KV, HD), (1, 1, G, S), (1, 1, G, S),
         (1, NB, WIN, KV, HD), (1, NB, WIN, KV, HD), (1, NB, G, S), (1, NB, G, S)]


def kernel(**inputs):
    import numpy as _np
    import concourse.bacc as _bacc
    from concourse import mybir as _mybir
    from concourse.bass_utils import run_bass_kernel_spmd as _run

    nc = _bacc.Bacc("TRN2", target_bir_lowering=False, num_devices=1)
    arrays, aps = {}, {}
    for name in _INS + ["shape_constants"]:
        a = shape_constants() if name == "shape_constants" else _np.ascontiguousarray(inputs[name])
        arrays[f"in_{name}_dram"] = a
        aps[name] = nc.dram_tensor(f"in_{name}_dram", a.shape, _mybir.dt.from_np(a.dtype), kind="ExternalInput").ap()
    outs = [nc.dram_tensor(f"out_{i}_dram", shape, F32, kind="ExternalOutput").ap() for i, shape in enumerate(_OUTS)]
    hybrid_layer(nc, aps, outs)
    r = _run(nc, [arrays], core_ids=[0])
    return tuple(r.results[0][f"out_{i}_dram"] for i in range(len(_OUTS)))
```

```python
from contextlib import ExitStack

import numpy as np

import concourse.bass as bass
from concourse import mybir

F32 = mybir.dt.float32
I32 = mybir.dt.int32
U32 = mybir.dt.uint32
ALU = mybir.AluOpType
ACT = mybir.ActivationFunctionType
AX = mybir.AxisListType

P = 128
D = 1024
SEQ, NB = 256, 8
T = SEQ + NB
KD = D // P
HEADS, KV, HD = 8, 2, 64
D_ATTN = HEADS * HD
WIN = 128
G, H, S = 32, 16, 64
D_SSM = G * H
KM = D_SSM // P
D_IN = D_ATTN + 2 * KV * HD + D_SSM
ST = G // 2
NE, TOPK, FF = 32, 4, 1024
PLE = 256
EPS = 1e-5
LIMIT, ALPHA = 7.0, 1.702
C = 64
PAIRS = NE // 2
VISITS = T * TOPK // (C + 1)
CHUNKS = [(0, P), (P, P), (SEQ, NB)]
SLOPES = [2.0 ** (-8.0 * (h + 1.0) / HEADS) for h in range(HEADS)]
SCALE = HD ** -0.5
FAR = 1e30

K_ID, K_TRI, K_ONE = 0, P, 2 * P
K_DIST = 3 * P
K_SBIAS = K_DIST + 2 * P
K_PAR = K_SBIAS + WIN + 1
K_HALF = K_PAR + 2
K_SAME = K_HALF + 2
K_OWN = K_SAME + 64
K_IOTA = K_OWN + NB
K_NTH = K_IOTA + C
K_OF = K_NTH + NE
K_N = K_OF + 4

V_MIX, V_FFN, V_PLE, V_OUT, V_D, V_GLU, V_N = 0, 8, 16, 24, 32, 36, 40

AT_QKV, AT_KVTOK, AT_B0, AT_B0V, AT_B1, AT_B1V, AT_S, AT_SV = 1, 3, 4, 5, 7, 8, 10, 12

UP, DN = 8, 4


def shape_constants():
    k = np.zeros((P, K_N), np.float32)
    i = np.arange(P)
    k[:, K_ID:K_ID + P] = np.eye(P)
    k[:, K_TRI:K_TRI + P] = i[:, None] < i[None]
    k[:, K_ONE:K_ONE + P] = 1.0
    dist = i[:, None] + WIN - np.arange(2 * P)[None]
    k[:, K_DIST:K_DIST + 2 * P] = np.where((dist >= 0) & (dist <= WIN), dist, FAR)
    r = np.arange(64)
    slope = np.asarray(SLOPES)[r % HEADS]
    k[:64, K_SBIAS:K_SBIAS + WIN + 1] = -slope[:, None] / SCALE * (WIN - np.arange(WIN + 1))[None]
    k[:, K_PAR] = (i // H) % 2 == 0
    k[:, K_PAR + 1] = (i // H) % 2 == 1
    k[:64, K_HALF] = r % HEADS < HEADS // KV
    k[:64, K_HALF + 1] = r % HEADS >= HEADS // KV
    k[:64, K_SAME:K_SAME + 64] = r[:, None] // HEADS == r[None] // HEADS
    k[:64, K_OWN:K_OWN + NB] = r[:, None] // HEADS == np.arange(NB)[None]
    k[:, K_IOTA:K_IOTA + C] = np.arange(C)[None]
    k[:, K_NTH:K_NTH + NE] = i[:, None] % NE == np.arange(NE)[None]
    k[:, K_OF] = C * (i // NE + 1)
    k[:, K_OF + 1] = i % NE
    return k


def hybrid_layer(nc, A, O):
    ctx = ExitStack()
    with ctx:
        def sb(name, shape, dt=F32):
            return ctx.enter_context(nc.sbuf_tensor(name, shape, dt))

        def sem(name):
            return ctx.enter_context(nc.semaphore(name))

        ps = ctx.enter_context(nc.psum_tensor("ps", [P, 8, 512], F32))
        ring_up = sb("ring_up", [P, UP, 2 * FF])
        ring_dn = sb("ring_dn", [P, 2 * DN, D])
        up_flat = ring_up[:].rearrange("p a b -> p (a b)")
        w_in = up_flat[:, 0:KD * D_IN].rearrange("p (k n) -> p k n", k=KD)
        w_glu = ring_up[:, 5].rearrange("p (k n) -> p k n", k=KM)
        w_out = ring_dn
        s5_mem = up_flat[:, 6 * 2 * FF:8 * 2 * FF]
        cos_t = s5_mem[:, 0:512].rearrange("p (a t) -> p a t", a=2)
        sin_t = s5_mem[:, 512:1024].rearrange("p (a t) -> p a t", a=2)
        tmp_t = s5_mem[:, 1024:1280]
        prod_p = s5_mem[:, 1280:1792].rearrange("p (r t) -> p r t", r=2)
        z_in = s5_mem[:, 1792:2304].rearrange("p (r t) -> p r t", r=2)
        rot_c = s5_mem[:, 2304:3328].rearrange("p (a r t) -> p a r t", a=2, r=2)
        w_gate = ring_up[:, 0:4].rearrange("p a (b n) -> p (a b) n", b=2)
        w_pp = ring_up[:, 4].rearrange("p (k n) -> p k n", k=2)

        kst = sb("kst", [P, K_N])
        ident = kst[:, K_ID:K_ID + P]
        tri = kst[:, K_TRI:K_TRI + P]
        ones = kst[:, K_ONE:K_ONE + P]
        x_tok = sb("x_tok", [P, 3, D])
        n_tok = sb("n_tok", [P, 3, D])
        fa = sb("fa", [P, KD, T])
        fb = sb("fb", [P, KD, T])
        vecs = sb("vecs", [P, V_N])
        final_g = sb("final_g", [P, D])
        router = sb("router", [P, KD, NE])
        router_b = sb("router_b", [P, NE])
        b_down = sb("b_down", [P, D])
        stat = sb("stat", [P, 3, 4])
        rank = sb("rank", [P, 3, NE + 1])
        gate = sb("gate", [P, 3, NE + 1])
        vis = sb("vis", [P, NE + 8 + 3 * VISITS])
        v_cnt, v_flag, v_pos = vis[:, 0:NE], vis[:, NE:NE + 1], vis[:, NE + 1:NE + 2]
        v_hot = vis[:, NE + 4:NE + 4 + VISITS]
        v_first = vis[:, NE + 4 + VISITS:NE + 4 + 2 * VISITS]
        v_from = vis[:, NE + 4 + 2 * VISITS:NE + 4 + 3 * VISITS]
        v_rank = vis[:, NE + 4 + 3 * VISITS:NE + 4 + 3 * VISITS + 3]
        vis_int = sb("vis_int", [1, VISITS + 1], I32)

        R_N = 12100
        region = sb("region", [P, R_N])
        used = [0]

        def part(n):
            used[0] += n
            assert used[0] <= R_N, used[0]
            return region[:, used[0] - n:used[0]]

        proj = part(10 * T).rearrange("p (k t) -> p k t", k=10)
        rot_s = part(1024).rearrange("p (a r t) -> p a r t", a=2, r=2)
        b_t = [part(512).rearrange("p (k n) -> p k n", k=4) for _ in range(2)]
        c_t = [part(512).rearrange("p (k n) -> p k n", k=4) for _ in range(3)]
        lo = [part(256).rearrange("p (a b) -> p a b", a=ST) for _ in range(2)]
        hi = [part(256).rearrange("p (a b) -> p a b", a=ST) for _ in range(2)]
        pt = part(16 * P).rearrange("p (k n) -> p k n", k=16)
        kc_t = part(NB * (WIN + 1)).rearrange("p (b n) -> p b n", b=NB)
        spread = part(NB * 72)
        pcols = part(7 * ST).rearrange("p (a b) -> p a b", a=7)
        x0_t = part(2 * P).rearrange("p (r n) -> p r n", r=2)
        xs_flat = part(2 * P)
        xs_new = xs_flat.rearrange("p (r b a) -> p r a b", r=2, a=ST)
        bu_s = part(2 * P).rearrange("p (r a b) -> p r a b", r=2, a=ST)
        last = part(2 * ST).rearrange("p (r a) -> p r a", r=2)
        mini = part(2 * P)
        rows = fb[:].rearrange("p a b -> p (a b)")[:, 0:16 * P]
        pt_flat = pt.rearrange("p k n -> p (k n)")
        b_raw = pt_flat[:, 0:512].rearrange("p (r a h) -> p r a h", r=2, a=ST)
        b_bd = kc_t.rearrange("p b n -> p (b n)")[:, 0:1024].rearrange("p (r a m) -> p r a m", r=2, a=ST)
        c_raw = pt_flat[:, 512:1024].rearrange("p (r a n) -> p r a n", r=2, a=4)
        c_bd = pt_flat[:, 1024:2048].rearrange("p (r a n) -> p r a n", r=2, a=4)
        n_flat = n_tok[:].rearrange("p a b -> p (a b)")
        sc = n_flat[:, 0:2048].rearrange("p (h n) -> p h n", h=HEADS)
        att = n_flat[:, 2048:3072].rearrange("p (b n) -> p b n", b=2)
        fa_flat = fa[:].rearrange("p a b -> p (a b)")
        kc = fa_flat[:, 0:1024].rearrange("p (b n) -> p b n", b=NB)
        vc = fa_flat[:, 1024:2048].rearrange("p (b n) -> p b n", b=NB)
        y_t = proj[:, 0:4]

        small = sb("small", [P, 160])
        mx, mneg, rsum, esink, rden = (small[:, 8 * i:8 * i + 8] for i in range(5))
        sink_b = small[:, 40:48]
        sink_s = small[:, 48:49]
        s_small = small[:, 49:57]
        kv_tok = sb("kv_tok", [P, 3, P])
        kv_new = sb("kv_new", [NB, 2, P])
        s_sc = sb("s_sc", [64, WIN + 1])
        s_o = sb("s_o", [64, 2, 64])
        s_own = sb("s_own", [64, NB])
        s_ownT = sb("s_ownT", [NB, 64])
        top = sb("top", [P, 3, 48])
        top_i = sb("top_i", [P, 3, 8], U32)
        pick = sb("pick", [P, TOPK, NE])

        used[0] = 0
        b_up = part(2 * FF)
        one_hot = part(C)
        sel = part(3 * 2 * C).rearrange("p (c a s) -> p c a s", c=3, a=2)
        sel_g = part(3 * 2 * C).rearrange("p (c a s) -> p c a s", c=3, a=2)
        xe = part(KD * 2 * C).rearrange("p (k s) -> p k s", k=KD)
        g_lim = part(512)
        u_lim = part(512)
        sig = part(512)
        act_v = part(512)
        act_t = part(512).rearrange("p (j n) -> p j n", j=4)
        out_e = part(D).rearrange("p (h n) -> p h n", h=2)
        g_t = part(3 * P)
        gates_t = part(T + C)
        p_tok = part(3 * PLE).rearrange("p (c n) -> p c n", c=3)
        p_t = part(2 * T).rearrange("p (k t) -> p k t", k=2)
        logits = part(3 * NE).rearrange("p (c n) -> p c n", c=3)
        mask = part(3 * NE).rearrange("p (c n) -> p c n", c=3)
        sg_t = part(2 * T).rearrange("p (a t) -> p a t", a=2)
        sq = proj[:, 6:8]

        def bank(b, n=512, parts=P, first=0):
            return ps[first:first + parts, b, 0:n]

        def col(t, n):
            return t.unsqueeze(2).to_broadcast([t.shape[0], t.shape[1], n])

        (ld_x, ld_win, ld_wglu, ld_wout, ld_vec, ld_par, ld_b, ld_c, ld_x0, ld_sink, ld_cache,
         ld_router, ld_bup, ld_gate_w, ld_p) = (sem(n) for n in (
            "ld_x", "ld_win", "ld_wglu", "ld_wout", "ld_vec", "ld_par", "ld_b", "ld_c", "ld_x0",
            "ld_sink", "ld_cache", "ld_router", "ld_bup", "ld_gate_w", "ld_p"))
        up_in = [sem(f"up_in{k}") for k in range(UP)]
        dn_in = [sem(f"dn_in{k}") for k in range(DN)]
        dve_step, act_step, pool_step, dve_loop = (sem(n) for n in ("dve_step", "act_step", "pool_step", "dve_loop"))
        names = ("n_ready st_k q_ps glu_ps s5_free up_free mix_ps dn_free f_out st_y c_ready par_sb b_ready "
                 "rot_ready trig last_in region_free hot_rdy hid_ps vec_ps norm_scaled norm_ps par_rows par_ps "
                 "norm_sb u_ps c_ps x0_ps c_sb b_ps b_sb u_sb bu_read bu_ps y_read y_rot q_sb tok_ps tok_sb "
                 "att_sb att_t score_read score_ps expd p_sb p_ps o_ps att_scaled att_ps kct_ps kct_sb q_spread "
                 "ssc_ps s_expd s_oready s_pps s_pspread s_ops s_ossq s_gps s_onorm s_otps state_s ys_ps gelu "
                 "state_ps ssm_sq ssm_ssq s_ot mix_sb ssm_n back_add back_ps lg_ps mask_sb cnt_ps gtr_ps gtr_sb "
                 "sel_rdy xg_ps dn_sb gt_sb cmb_read cmb_ps xe_rdy act_rdy at_ps selg_rdy gt_ps at_sb "
                 "pT_ps pT_sb pp_sb pp_ps gz_mul gz_sig gz_ps par_exp par_red norm_ssq norm_root par_sin vec_sb "
                 "x0_sb m_neg att_ssq att_root s_mneg s_groot ypre ssm_y glu_sig ssm_root topv w_exp g_rdy "
                 "sig_rdy all_added vis_flag vis_pos vis_hot vis_ps v_rank").split()
        Z = {n: sem(n) for n in names}

        block = ctx.enter_context(nc.Block())

        def further_visits(eng, body, expert_of=False):
            eng.wait_ge(Z["n_ready"], 1)
            n = eng.value_load(vis_int[0:1, VISITS:VISITS + 1], min_val=0, max_val=VISITS)
            with eng.Fori(0, VISITS) as v:
                with eng.If(n > v):
                    body(v, eng.value_load(vis_int[0:1, bass.ds(v, 1)], min_val=0, max_val=NE - 1)
                         if expert_of else None)
                eng.nop()
            return n

        @block.sync
        def _(sp):
            x_p, x_s = A["x_prompt"][0], A["x_sample"].rearrange("b l d -> (b l) d")
            for c in range(2):
                sp.dma_start(x_tok[:, c], x_p[c * P:(c + 1) * P, :]).then_inc(ld_x, 16)
            sp.dma_start(x_tok[0:NB, 2], x_s).then_inc(ld_x, 16)
            sp.dma_start(kst[:], A["shape_constants"]).then_inc(ld_x, 16)
            w = A["w_in"][0].rearrange("(k p) n -> p k n", p=P)
            for k in range(0, KD, 4):
                sp.dma_start(w_in[:, k:k + 4], w[:, k:k + 4]).then_inc(ld_win, 16)
            sp.dma_start(w_glu, A["w_glu"][0].rearrange("(k p) n -> p k n", p=P)).then_inc(ld_wglu, 16)
            sp.dma_start(w_out[:], A["w_out"][0].rearrange("(k p) n -> p k n", p=P)).then_inc(ld_wout, 16)
            sp.dma_start(final_g[:], A["norm_final"].partition_broadcast(P)).then_inc(ld_router, 16)
            sp.dma_start(router[:], A["w_router"][0].rearrange("(k p) n -> p k n", p=P)).then_inc(ld_router, 16)
            sp.dma_start(router_b[:], A["b_router"][0].partition_broadcast(P)).then_inc(ld_router, 16)
            sp.dma_start(b_down[0:NE], A["b_down"][0]).then_inc(ld_router, 16)
            for src, dst in ((A["cache_k_win"], O[6]), (A["cache_v_win"], O[7])):
                sp.dma_start(dst[0].rearrange("b w n d -> b (w n d)")[:, 0:(WIN - 1) * P],
                             src[0].rearrange("b w n d -> b (w n d)")[:, P:WIN * P]).then_inc(Z["st_k"], 16)

            up_w = A["w_up"][0].rearrange("e (k p) n -> e k p n", p=P)
            dn_w = A["w_down"][0].rearrange("e (s k p) n -> e s p k n", p=P, k=2)

            def expert(e, t, first=False):
                for k in range(UP):
                    if first:
                        sp.wait_ge(*((Z["q_ps"], 6) if k < 5 else (Z["glu_ps"], KM) if k == 5 else (Z["s5_free"], 1)))
                    else:
                        sp.wait_ge(Z["up_free"], t * UP + (k + 1 - UP))
                    sp.dma_start(ring_up[:, k], up_w[bass.ds(e, 1), k].rearrange("e p n -> (e p) n")
                                 ).then_inc(up_in[k], 16)
                for s in range(DN):
                    if first:
                        sp.wait_ge(Z["mix_ps"], KD)
                    else:
                        sp.wait_ge(Z["dn_free"], t * DN + (s + 1 - DN))
                    sp.dma_start(ring_dn[:, 2 * s:2 * s + 2], dn_w[bass.ds(e, 1), s].rearrange("e p k n -> (e p) k n")
                                 ).then_inc(dn_in[s], 16)

            expert(0, 0, first=True)
            with sp.Fori(1, NE) as e:
                expert(e, e)
            n = further_visits(sp, lambda v, e: expert(e, NE + v), expert_of=True)
            for k in range(4):
                sp.wait_ge(Z["up_free"], (n + (NE - 1)) * UP + (k + 1))
                sp.dma_start(w_gate[:, 2 * k:2 * k + 2], A["w_ple_gate"][0].rearrange("(s k p) n -> s p k n", p=P, k=2)[k]
                             ).then_inc(ld_gate_w, 16)
            sp.wait_ge(Z["up_free"], (n + (NE - 1)) * UP + 5)
            sp.dma_start(w_pp, A["w_ple_proj"][0].rearrange("(k p) n -> p k n", p=P)).then_inc(ld_p, 16)
            sp.wait_ge(Z["f_out"], 3)
            for c in range(2):
                sp.dma_start(O[0][0, c * P:(c + 1) * P, :], n_tok[:, c]).then_inc(Z["st_y"], 16)
            sp.dma_start(O[1].rearrange("b l d -> (b l) d"), n_tok[0:NB, 2]).then_inc(Z["st_y"], 16)
            sp.wait_ge(Z["st_y"], 48)
            sp.wait_ge(Z["st_k"], 32 + 16 * 8)

        @block.gpsimd
        def _(pool):
            n = [0]

            def chain(ins):
                n[0] += 1
                ins.then_inc(pool_step, 1)
                pool.wait_ge(pool_step, n[0])

            tt = nc.gpsimd.tensor_tensor

            def cmul(out, a, b, s1, sh):
                chain(tt(s1, a[1], b[1], ALU.mult))
                chain(tt(out[0], a[0], b[0], ALU.mult))
                chain(tt(out[0], out[0], s1, ALU.subtract))
                chain(tt(s1, a[1], b[0], ALU.mult))
                chain(tt(out[1], a[0], b[1], ALU.mult))
                chain(tt(out[1], out[1], s1, ALU.add))

            nc.gpsimd.memset(b_down[NE:2 * NE], 0.0)
            chain(nc.gpsimd.memset(b_down[2 * NE:P], 0.0))
            pool.wait_ge(ld_c, 32)
            pool.wait_ge(ld_x, 64)
            for r, sign in ((0, 1.0), (1, -1.0)):
                for par in range(2):
                    chain(nc.gpsimd.tensor_scalar(c_bd[:, r, :, par * S:par * S + S], c_raw[:, r],
                                                  kst[:, K_PAR + par:K_PAR + par + 1], sign, ALU.mult, ALU.mult))
            nc.gpsimd.nop().then_inc(Z["c_ready"], 1)
            pool.wait_ge(Z["par_sb"], 1)
            pool.wait_ge(ld_b, 32)
            chain(nc.gpsimd.memset(b_bd, 0.0))
            fr, fi = col(pcols[:, 5], H), col(pcols[:, 6], H)
            t1 = mini.rearrange("p (a h) -> p a h", h=H)
            for r, (f0, f1, op) in enumerate(((fr, fi, ALU.subtract), (fi, fr, ALU.add))):
                t2 = tmp_t.rearrange("p (a h) -> p a h", h=H)
                chain(tt(t1, b_raw[:, 0], f0, ALU.mult))
                chain(tt(t2, b_raw[:, 1], f1, ALU.mult))
                for par in range(2):
                    rows_ = slice(par * S, par * S + S)
                    chain(tt(b_bd[rows_, r, :, par * H:par * H + H], t1[rows_], t2[rows_], op))
            nc.gpsimd.nop().then_inc(Z["b_ready"], 1)
            m3 = mini.rearrange("p (a b) -> p a b", b=16)
            base = (pcols[:, 0].unsqueeze(2), pcols[:, 1].unsqueeze(2))
            for tab in (lo, hi):
                chain(nc.gpsimd.memset(tab[0][:, :, 0:1], 1.0))
                chain(nc.gpsimd.memset(tab[1][:, :, 0:1], 0.0))
                chain(nc.gpsimd.tensor_copy(tab[0][:, :, 1:2], base[0]))
                chain(nc.gpsimd.tensor_copy(tab[1][:, :, 1:2], base[1]))
                step = (tab[0][:, :, 1:2], tab[1][:, :, 1:2])
                for k in (2, 4, 8, 16):
                    sq_ = (rows[:, 32 * k:32 * k + 16].unsqueeze(2), rows[:, 32 * k + 16:32 * k + 32].unsqueeze(2))
                    cmul(sq_, step, step, m3[:, :, 0:1], 1)
                    step = sq_
                    if k < 16:
                        cmul((tab[0][:, :, k:2 * k], tab[1][:, :, k:2 * k]), (tab[0][:, :, 0:k], tab[1][:, :, 0:k]),
                             (step[0].to_broadcast([P, ST, k]), step[1].to_broadcast([P, ST, k])), m3[:, :, 0:k], k)
                base = step

            def trig(i):
                a = i % 2
                if i >= 2:
                    pool.wait_ge(Z["rot_ready"], i - 1)
                hb = [h[:, i].unsqueeze(2).to_broadcast([P, 16, 16]) for h in hi]
                lb = [l[:, i].unsqueeze(1).to_broadcast([P, 16, 16]) for l in lo]
                out = [x[:, a].rearrange("p (a b) -> p a b", a=16) for x in (cos_t, sin_t)]
                tm = tmp_t.rearrange("p (a b) -> p a b", a=16)
                cmul(out, hb, lb, tm, 256)
                nc.gpsimd.nop().then_inc(Z["trig"], 1)

            def last_state(i):
                a = i % 2
                pool.wait_ge(Z["rot_ready"], i + 1)
                chain(tt(last[:, 0, i:i + 1], rot_c[:, a, 0, 255:256], rot_s[:, a, 1, 255:256], ALU.subtract))
                tt(last[:, 1, i:i + 1], rot_s[:, a, 0, 255:256], rot_c[:, a, 1, 255:256], ALU.add
                   ).then_inc(Z["last_in"], 1)

            for i in range(ST + 2):
                if i < ST:
                    trig(i)
                if i >= 2:
                    last_state(i - 2)

            pool.wait_ge(Z["region_free"], 1)
            nc.gpsimd.memset(b_up, 0.0).then_inc(Z["hot_rdy"], 1)

            def hot(e, t, first=False):
                if not first:
                    pool.wait_ge(Z["hid_ps"], t)
                nc.gpsimd.tensor_copy(one_hot, ident[:, bass.ds(e, 1)].to_broadcast([P, C])).then_inc(Z["hot_rdy"], 1)

            hot(0, 0, first=True)
            with pool.Fori(1, NE) as e:
                hot(e, e)
            further_visits(pool, lambda v, e: hot(e, NE + v), expert_of=True)

        @block.tensor
        def _(pe):
            mm, tr = nc.tensor.matmul, nc.tensor.transpose
            pe.wait_ge(ld_x, 64)
            pe.wait_ge(ld_vec, 16 * 7)
            tr(bank(7, V_N), rows[0:V_N, 0:P], ident[0:V_N, 0:V_N]).then_inc(Z["vec_ps"], 1)
            n = 0
            for c, (t0, nt) in enumerate(CHUNKS):
                pe.wait_ge(Z["norm_scaled"], c + 1)
                for half in range(2):
                    for k in range(4):
                        m = tr(ps[:, 2 * c + half, k * nt:(k + 1) * nt],
                               n_tok[0:nt, c, (4 * half + k) * P:(4 * half + k + 1) * P], ident[0:nt, 0:nt])
                    m.then_inc(Z["norm_ps"], 1)
            pe.wait_ge(Z["par_rows"], 1)
            for j in range(7):
                m = tr(ps[:, 6, j * ST:(j + 1) * ST], rows[0:ST, (2 + j) * P:(3 + j) * P], ident[0:ST, 0:ST])
            m.then_inc(Z["par_ps"], 1)

            def project(slot, b, lhs):
                for k in range(KD):
                    m = mm(bank(b, T), lhs(k), fa[:, k, :], start=(k == 0), stop=(k == KD - 1))
                return m

            pe.wait_ge(Z["norm_sb"], 6)
            pe.wait_ge(ld_win, 32)
            for j in range(4):
                project(6 + j, j, lambda k: w_in[:, k, D_IN - D_SSM + j * P:D_IN - D_SSM + (j + 1) * P]
                        ).then_inc(Z["u_ps"], 1)
            pe.wait_ge(Z["c_ready"], 1)
            for r in range(2):
                for k in range(4):
                    m = tr(ps[:, 4 + r, k * P:(k + 1) * P], c_bd[:, r, k], ident)
            m.then_inc(Z["c_ps"], 1)
            pe.wait_ge(ld_x0, 32)
            pe.wait_ge(Z["par_sb"], 1)
            for r in range(2):
                m = tr(ps[:, 6, r * P:(r + 1) * P], rows[:, (10 + r) * P:(11 + r) * P], ident)
            m.then_inc(Z["x0_ps"], 1)
            pe.wait_ge(Z["b_ready"], 1)
            pe.wait_ge(Z["c_sb"], 1)
            for r in range(2):
                for k in range(4):
                    m = tr(ps[:, 4 + r, k * P:(k + 1) * P],
                           b_bd[:, r, 4 * k:4 * k + 4].rearrange("p a m -> p (a m)"), ident)
            m.then_inc(Z["b_ps"], 1)
            pe.wait_ge(Z["b_sb"], 1)
            pe.wait_ge(Z["u_sb"], 4)

            def drive(i):
                c, j = divmod(i, 4)
                if i >= 1:
                    pe.wait_ge(Z["bu_read"], i)
                rows_ = slice(32 * j, 32 * j + 32)
                for r in range(2):
                    m = mm(bank(r, T), b_t[r][rows_, c, :], proj[rows_, 6 + c, :], start=True, stop=True)
                m.then_inc(Z["bu_ps"], 1)

            def read_out(i):
                c, j = divmod(i, 4)
                pe.wait_ge(Z["rot_ready"], i + 1)
                if j == 0 and c >= 1:
                    pe.wait_ge(Z["y_read"], c)
                a = i % 2
                out = ps[32 * j:32 * j + 32, 4, 0:SEQ]
                cols = slice(32 * j, 32 * j + 32)
                for n_, (w, v) in enumerate(((0, rot_c[:, a, 0]), (1, rot_c[:, a, 1]), (2, rot_s[:, a, 1]),
                                            (1, rot_s[:, a, 0]))):
                    m = mm(out, c_t[w][:, c, cols], v, start=(n_ == 0), stop=(n_ == 3))
                m.then_inc(Z["y_rot"], 1)

            def project_q(c, b):
                for k in range(KD):
                    for n_ in range(KV):
                        h = 4 * n_ + c
                        m = mm(ps[64 * n_:64 * n_ + 64, b, 0:T], w_in[:, k, h * HD:(h + 1) * HD], fa[:, k, :],
                               start=(k == 0), stop=(k == KD - 1))
                return m

            def project_qkv():
                for n_, slot in enumerate((4, 5, 0, 1, 2, 3)):
                    b = 5 + n_ % 3
                    if n_ >= 3:
                        pe.wait_ge(Z["q_sb"], n_ - 2)
                    if slot >= 4:
                        m = project(slot, b, lambda k: w_in[:, k, D_ATTN + (slot - 4) * P:D_ATTN + (slot - 3) * P])
                    else:
                        m = project_q(slot, b)
                    m.then_inc(Z["q_ps"], 1)

            def kv_to_tokens():
                pe.wait_ge(Z["q_sb"], 6)
                for j, (slot, c) in enumerate(((5, 0), (5, 1), (4, 1))):
                    tr(ps[:, 7, j * P:(j + 1) * P], proj[:, slot, c * P:(c + 1) * P], ident)
                for j, slot in enumerate((4, 5)):
                    m = tr(ps[0:NB, 6, j * P:(j + 1) * P], proj[:, slot, SEQ:T], ident)
                m.then_inc(Z["tok_ps"], 1)

            def scores(b):
                K = P * (b + 1)
                if b == 0:
                    pe.wait_ge(Z["tok_sb"], 1)
                else:
                    pe.wait_ge(Z["att_sb"], b)
                    pe.wait_ge(Z["att_t"], b)
                for c in range(4):
                    if b * 4 + c >= 1 and c >= 1:
                        pe.wait_ge(Z["score_read"], b * 4 + c)
                    for n_ in range(KV):
                        r = slice(64 * n_, 64 * n_ + 64)
                        m = mm(bank(5 + n_, K), proj[r, c, b * P:(b + 1) * P], proj[r, 4, 0:K], start=True, stop=True)
                    m.then_inc(Z["score_ps"], 1)

            p_fills = [0]

            def p_transposes(b):
                nk = b + 1
                pe.wait_ge(Z["expd"], b + 1)
                pe.wait_ge(Z["score_read"], 4 * (b + 1))
                for f in range(2 * nk):
                    if f >= 3:
                        pe.wait_ge(Z["p_sb"], p_fills[0] - 2)
                    for q in range(4):
                        h, kc_ = divmod(4 * f + q, nk)
                        m = tr(ps[:, 5 + f % 3, q * P:(q + 1) * P], sc[:, h, kc_ * P:(kc_ + 1) * P], ident)
                    m.then_inc(Z["p_ps"], 1)
                    p_fills[0] += 1

            def values(b):
                nk = b + 1
                pe.wait_ge(Z["p_sb"], p_fills[0])
                for h in range(HEADS):
                    for kc_ in range(nk):
                        m = mm(ps[:, 5, h * HD:(h + 1) * HD], pt[:, h * nk + kc_, :],
                               kv_tok[:, kc_, (h // 4) * HD:(h // 4 + 1) * HD], start=(kc_ == 0), stop=(kc_ == nk - 1))
                m.then_inc(Z["o_ps"], 1)

            def att_transposes(b):
                pe.wait_ge(Z["att_scaled"], b + 1)
                for k in range(4):
                    m = tr(ps[:, 6, k * P:(k + 1) * P], att[:, b, k * P:(k + 1) * P], ident)
                m.then_inc(Z["att_ps"], 1)

            def cache_transposes():
                pe.wait_ge(ld_cache, 32)
                pe.wait_ge(Z["att_sb"], 2)
                pe.wait_ge(Z["p_sb"], p_fills[0])
                for f, b_ in enumerate((5, 7)):
                    for q in range(4):
                        m = tr(ps[:, b_, q * P:(q + 1) * P], kc[:, 4 * f + q], ident)
                    m.then_inc(Z["kct_ps"], 1)

            def sample_scores():
                pe.wait_ge(Z["kct_sb"], 3)
                pe.wait_ge(Z["q_spread"], 1)
                for b_ in range(NB):
                    m = mm(ps[0:64, 5, 0:WIN + 1], spread[:, b_ * 64:(b_ + 1) * 64], kc_t[:, b_, :],
                           start=(b_ == 0), stop=(b_ == NB - 1))
                m.then_inc(Z["ssc_ps"], 1)

            def sample_values():
                pe.wait_ge(Z["s_expd"], 1)
                pe.wait_ge(Z["s_oready"], 1)
                tr(ps[:, 7, 0:64], s_sc[:, 0:WIN], ident[0:64, 0:64])
                tr(ps[0:NB, 7, 64:128], s_own[:], ident[0:64, 0:64]).then_inc(Z["s_pps"], 1)
                pe.wait_ge(Z["s_pspread"], 2)
                for b_ in range(NB):
                    mm(ps[0:64, 5, 0:P], spread[:, b_ * 64:(b_ + 1) * 64], vc[:, b_, :], start=(b_ == 0), stop=False)
                mm(ps[0:64, 5, 0:P], s_ownT[:], kv_new[:, 1, :], start=False, stop=True).then_inc(Z["s_ops"], 1)
                pe.wait_ge(Z["s_ossq"], 1)
                mm(ps[0:64, 7, 0:1], kst[0:64, K_SAME:K_SAME + 64], s_small[0:64, 5:6], start=True, stop=True
                   ).then_inc(Z["s_gps"], 1)
                pe.wait_ge(Z["s_onorm"], 1)
                tr(ps[:, 6, 0:64], s_o[:].rearrange("p a d -> p (a d)"), ident[0:64, 0:64]).then_inc(Z["s_otps"], 1)

            for i in range(ST + 1):
                if i < ST:
                    drive(i)
                if i >= 1:
                    read_out(i - 1)
                if i == AT_QKV:
                    project_qkv()
                if i == AT_KVTOK:
                    kv_to_tokens()
                if i == AT_B0:
                    scores(0)
                if i == AT_B0V:
                    p_transposes(0)
                    values(0)
                    att_transposes(0)
                if i == AT_B1:
                    scores(1)
                if i == AT_B1V:
                    p_transposes(1)
                    values(1)
                    att_transposes(1)
                if i == AT_S:
                    cache_transposes()
                    sample_scores()
                if i == AT_SV:
                    sample_values()

            pe.wait_ge(Z["state_s"], 1)
            for i in range(ST):
                c, j = divmod(i, 4)
                for n_ in range(2):
                    m = mm(ps[32 * j:32 * j + 32, 5, NB * c:NB * c + NB], c_t[n_][:, c, 32 * j:32 * j + 32],
                           xs_new[:, n_, i, :], start=(n_ == 0), stop=(n_ == 1))
            m.then_inc(Z["ys_ps"], 1)
            pe.wait_ge(ld_wglu, 16)
            pe.wait_ge(Z["gelu"], 1)
            for c in range(KM):
                for k in range(KM):
                    m = mm(bank(c, T), w_glu[:, k, c * P:(c + 1) * P], y_t[:, k, :], start=(k == 0), stop=(k == KM - 1))
                m.then_inc(Z["glu_ps"], 1)
            pe.wait_ge(Z["last_in"], ST)
            for r in range(2):
                tr(ps[:, 7, r * P:(r + 1) * P], xs_flat[:, r * P:(r + 1) * P], ident)
            for r in range(2):
                m = tr(ps[0:ST, 7, (2 + r) * P:(3 + r) * P], last[:, r], ident)
            m.then_inc(Z["state_ps"], 1)
            for c in range(KM):
                pe.wait_ge(Z["ssm_sq"], c + 1)
                m = mm(bank(6, T), ones, sq[:, c % 2], start=(c == 0), stop=(c == KM - 1))
                m.then_inc(Z["ssm_ssq"], 1)
            pe.wait_ge(ld_wout, 16)
            pe.wait_ge(Z["att_t"], 2)
            pe.wait_ge(Z["s_ot"], 1)
            for o in range(KD):
                b_ = (0, 1, 2, 3)[o % 4]
                if o >= 4:
                    pe.wait_ge(Z["mix_sb"], o - 3)
                for k in range(KD):
                    if o == 0 and k == 4:
                        pe.wait_ge(Z["ssm_n"], KM)
                    m = mm(bank(b_, T), w_out[:, k, o * P:(o + 1) * P], fb[:, k, :], start=(k == 0), stop=(k == KD - 1))
                m.then_inc(Z["mix_ps"], 1)
            n_ = 0
            for half in range(2):
                pe.wait_ge(Z["mix_sb"], 4 * (half + 1))
                for c, (t0, nt) in enumerate(CHUNKS):
                    if n_ >= 2:
                        pe.wait_ge(Z["back_add"], n_ - 1)
                    for k in range(4):
                        m = tr(ps[0:nt, 4 + n_ % 2, k * P:(k + 1) * P], fa[:, 4 * half + k, t0:t0 + nt], ident)
                    m.then_inc(Z["back_ps"], 1)
                    n_ += 1
            for c, (t0, nt) in enumerate(CHUNKS):
                pe.wait_ge(Z["norm_scaled"], 3 + c + 1)
                for half in range(2):
                    b_ = (0, 1, 2, 3, 6, 7)[2 * c + half]
                    for k in range(4):
                        m = tr(ps[:, b_, k * nt:(k + 1) * nt],
                               n_tok[0:nt, c, (4 * half + k) * P:(4 * half + k + 1) * P], ident[0:nt, 0:nt])
                    m.then_inc(Z["norm_ps"], 1)
            pe.wait_ge(Z["norm_sb"], 12)
            pe.wait_ge(ld_router, 64)
            for c, (t0, nt) in enumerate(CHUNKS):
                for k in range(KD):
                    m = mm(ps[0:nt, 4, c * NE:(c + 1) * NE], fb[:, k, t0:t0 + nt], router[:, k, :],
                           start=(k == 0), stop=(k == KD - 1))
            m.then_inc(Z["lg_ps"], 1)
            pe.wait_ge(Z["mask_sb"], 1)
            for c, (t0, nt) in enumerate(CHUNKS):
                for k in range(c):
                    mm(ps[:, 5, c * NE:(c + 1) * NE], ones, mask[:, k, :], start=(k == 0), stop=False)
                mm(ps[:, 5, c * NE:(c + 1) * NE], tri[0:nt, :], mask[0:nt, c, :], start=(c == 0), stop=True)
            for c, (t0, nt) in enumerate(CHUNKS):
                m = mm(ps[:, 5, 3 * NE:4 * NE], ones[0:nt, :], mask[0:nt, c, :], start=(c == 0), stop=(c == 2))
            m.then_inc(Z["cnt_ps"], 1)
            for c, (t0, nt) in enumerate(CHUNKS):
                m = tr(ps[0:NE, 3, t0:t0 + nt], gate[0:nt, c, 0:NE], ident[0:nt, 0:nt])
            m.then_inc(Z["gtr_ps"], 1)

            G_B, U_B, T_B, O_B, X_B = 0, 1, 3, 4, (2, 5)
            SHARE_B = ((6, 7), (G_B, U_B), (2, 2))

            def shares(weights, outputs, rows_=slice(0, P)):
                for c, (t0, nt) in enumerate(CHUNKS):
                    for half in range(2):
                        if c < 2:
                            m = mm(ps[:, SHARE_B[c][half], :], weights[rows_, t0:t0 + P], outputs(half),
                                   start=True, stop=True)
                        else:
                            m = mm(ps[64 * half:64 * half + 64, SHARE_B[c][half], :], weights[rows_, t0:t0 + 64], outputs(half),
                                   start=True, stop=True)
                    m.then_inc(Z["cmb_ps"], 1)

            def output_biases():
                pe.wait_ge(Z["gtr_sb"], 1)
                shares(gates_t, lambda half: b_down[:, half * 512:(half + 1) * 512])

            def visit_list():
                pe.wait_ge(Z["vis_flag"], 1)
                mm(ps[:, 5, 0:1], tri, v_flag, start=True, stop=True).then_inc(Z["vis_pos"], 1)
                pe.wait_ge(Z["vis_hot"], 1)
                mm(ps[:, 5, 0:VISITS], ones, v_from, start=True, stop=True)
                mm(ps[0:1, 5, 64:64 + VISITS], kst[:, K_OF + 1:K_OF + 2], v_hot, start=True, stop=True)
                mm(ps[0:1, 5, 64 + VISITS:65 + VISITS], ones[:, 0:1], v_flag, start=True, stop=True
                   ).then_inc(Z["vis_ps"], 1)
                pe.wait_ge(Z["n_ready"], 1)

            def gather(p):
                pe.wait_ge(Z["sel_rdy"], p + 1)
                for k in range(KD):
                    for c, (t0, nt) in enumerate(CHUNKS):
                        m = mm(ps[:, X_B[k // 4], (k % 4) * P:(k % 4 + 1) * P], n_tok[0:nt, c, k * P:(k + 1) * P],
                               sel[0:nt, c].rearrange("p a s -> p (a s)"), start=(c == 0), stop=(c == 2))
                    if k % 4 == 3:
                        m.then_inc(Z["xg_ps"], 1)

            def up(t, slots):
                for k in range(UP + 1):
                    if k < UP:
                        pe.wait_ge(up_in[k], 16 * t + 16)
                    else:
                        pe.wait_ge(Z["hot_rdy"], t + 2)
                    for q in range(4):
                        w = (ring_up[:, k] if k < UP else b_up)[:, q * 512:(q + 1) * 512]
                        m = mm(ps[64 * (q % 2):64 * (q % 2) + 64, q // 2, :], xe[:, k, slots] if k < UP else one_hot, w,
                               start=(k == 0), stop=(k == UP))
                    m.then_inc(Z["up_free"] if k < UP else Z["hid_ps"], 1)

            def turn_activations(t):
                pe.wait_ge(Z["act_rdy"], t + 1)
                for j in range(4):
                    m = tr(ps[:, T_B, j * P:(j + 1) * P], act_v[:, j * P:(j + 1) * P], ident)
                m.then_inc(Z["at_ps"], 1)

            def down(t):
                pe.wait_ge(Z["at_sb"], t + 1)
                for f in range(FF // P):
                    if f % 2 == 0:
                        pe.wait_ge(dn_in[f // 2], 16 * t + 16)
                    for half in range(2):
                        m = mm(ps[64 * half:64 * half + 64, O_B, :], act_t[:, f % 4, 64 * (f // 4):64 * (f // 4) + 64],
                               ring_dn[:, f, 512 * half:512 * half + 512], start=(f == 0), stop=(f == FF // P - 1))
                    if f % 2 == 1:
                        m.then_inc(Z["dn_free"], 1)

            def turn_selection(n_):
                pe.wait_ge(Z["selg_rdy"], n_ + 1)
                for c, (t0, nt) in enumerate(CHUNKS):
                    m = tr(ps[:, T_B, t0:t0 + nt], sel_g[0:nt, c].rearrange("p a s -> p (a s)"), ident[0:nt, 0:nt])
                m.then_inc(Z["gt_ps"], 1)

            def combine(p):
                pe.wait_ge(Z["dn_sb"], 2 * p + 2)
                pe.wait_ge(Z["gt_sb"], p + 1)
                shares(g_t, lambda half: out_e[:, half])

            def pair(p, place=None):
                t = 2 * p
                if place == "first":
                    pe.wait_ge(ld_bup, 16)
                pe.wait_ge(Z["xe_rdy"], 2 * p + 2)
                up(t, slice(0, C))
                turn_activations(t)
                if place == "first":
                    output_biases()
                    visit_list()
                else:
                    combine(p - 1)
                down(t)
                turn_selection(p)
                pe.wait_ge(Z["cmb_read"], 4 * p + 4)
                up(t + 1, slice(C, 2 * C))
                if place != "last":
                    gather(p + 1)
                pe.wait_ge(Z["gt_sb"], p + 1)
                turn_activations(t + 1)
                pe.wait_ge(Z["dn_sb"], t + 1)
                down(t + 1)

            def visit(v, _):
                t = NE + v
                pe.wait_ge(Z["cmb_read"], 4 * (PAIRS + 1) + 4 * v)
                pe.wait_ge(Z["sel_rdy"], PAIRS + 1 + v)
                for k in range(KD):
                    for c, (t0, nt) in enumerate(CHUNKS):
                        m = mm(ps[:, 2, k * C:(k + 1) * C], n_tok[0:nt, c, k * P:(k + 1) * P], sel[0:nt, c, 0],
                               start=(c == 0), stop=(c == 2))
                m.then_inc(Z["xg_ps"], 1)
                pe.wait_ge(Z["xe_rdy"], 2 * PAIRS + 1 + v)
                up(t, slice(0, C))
                turn_activations(t)
                down(t)
                turn_selection(PAIRS + v)
                pe.wait_ge(Z["dn_sb"], t + 1)
                pe.wait_ge(Z["gt_sb"], PAIRS + 1 + v)
                shares(g_t, lambda half: out_e[0:C, half], slice(0, C))

            gather(0)
            pair(0, "first")
            with pe.Fori(1, PAIRS - 1) as p:
                pair(p)
            pair(PAIRS - 1, "last")
            combine(PAIRS - 1)
            further_visits(pe, visit)

            pe.wait_ge(ld_p, 48)
            for k in range(2):
                for c, (t0, nt) in enumerate(CHUNKS):
                    m = tr(ps[:, 3 + k, t0:t0 + nt], p_tok[0:nt, c, k * P:(k + 1) * P], ident[0:nt, 0:nt])
            m.then_inc(Z["pT_ps"], 1)
            pe.wait_ge(Z["pT_sb"], 1)
            for o in range(KD):
                b_ = 3 + o % 3
                if o >= 3:
                    pe.wait_ge(Z["pp_sb"], o - 2)
                for k in range(2):
                    m = mm(bank(b_, T), w_pp[:, k, o * P:(o + 1) * P], p_t[:, k, :], start=(k == 0), stop=(k == 1))
                m.then_inc(Z["pp_ps"], 1)
            for c, (t0, nt) in enumerate(CHUNKS):
                pe.wait_ge(Z["norm_scaled"], 6 + c + 1)
                for half in range(2):
                    b_ = (0, 1, 6, 7, 2, 5)[2 * c + half]
                    if b_ == 5:
                        pe.wait_ge(Z["pp_sb"], KD)
                    for k in range(4):
                        m = tr(ps[:, b_, k * nt:(k + 1) * nt],
                               n_tok[0:nt, c, (4 * half + k) * P:(4 * half + k + 1) * P], ident[0:nt, 0:nt])
                    m.then_inc(Z["norm_ps"], 1)
            pe.wait_ge(Z["norm_sb"], 18)
            pe.wait_ge(ld_gate_w, 64)

            def back(half):
                pe.wait_ge(Z["gz_mul"], 4 * (half + 1))
                for c, (t0, nt) in enumerate(CHUNKS):
                    n_ = 3 * half + c
                    if n_ >= 2:
                        pe.wait_ge(Z["back_add"], 6 + n_ - 1)
                    for k in range(4):
                        m = tr(ps[0:nt, 4 + n_ % 2, k * P:(k + 1) * P], fa[:, 4 * half + k, t0:t0 + nt], ident)
                    m.then_inc(Z["back_ps"], 1)

            for o in range(KD):
                b_ = o % 4
                if o >= 4:
                    pe.wait_ge(Z["gz_sig"], o - 3)
                for k in range(KD):
                    m = mm(bank(b_, T), w_gate[:, k, o * P:(o + 1) * P], fb[:, k, :], start=(k == 0), stop=(k == KD - 1))
                m.then_inc(Z["gz_ps"], 1)
                if o == 5:
                    back(0)
            back(1)

        @block.scalar
        def _(act):
            f = nc.scalar.activation
            n = [0]

            def chain(ins):
                n[0] += 1
                ins.then_inc(act_step, 1)
                act.wait_ge(act_step, n[0])

            r0 = 0
            for name, k in (("norm_mix", 8), ("norm_ffn", 8), ("norm_ple", 8), ("norm_attn_out", 4),
                            ("norm_ssm_out", 4)):
                act.dma_start(rows[r0:r0 + k, 0:P], A[name][0].rearrange("(k p) -> k p", p=P)).then_inc(ld_vec, 16)
                r0 += k
            act.dma_start(rows[r0:r0 + 4, 0:P], A["ssm_d"][0].rearrange("(k g) h -> k (g h)", k=4)).then_inc(ld_vec, 16)
            act.dma_start(rows[r0 + 4:r0 + 8, 0:P], A["b_glu"][0].rearrange("(k p) -> k p", p=P)).then_inc(ld_vec, 16)
            for j, name in enumerate(("ssm_lam_re", "ssm_lam_im")):
                act.dma_start(rows[0:ST, (12 + j) * P:(13 + j) * P], A[name][0].rearrange("(k g) p -> k (g p)", g=2)
                              ).then_inc(ld_par, 16)
            act.dma_start(rows[0:ST, 14 * P:14 * P + 2], A["ssm_log_step"][0].rearrange("(k g) -> k g", g=2)
                          ).then_inc(ld_par, 16)
            for r, name in enumerate(("ssm_c_re", "ssm_c_im")):
                act.dma_start(c_raw[:, r], A[name][0].rearrange("(k g) h p -> (g h) k p", k=4)).then_inc(ld_c, 16)
            for r, name in enumerate(("ssm_b_re", "ssm_b_im")):
                act.dma_start(b_raw[:, r], A[name][0].rearrange("(k g) p h -> (g p) k h", g=2)).then_inc(ld_b, 16)
            for r, name in enumerate(("state_ssm_re", "state_ssm_im")):
                act.dma_start(rows[:, (10 + r) * P:(11 + r) * P],
                              A[name][0].rearrange("b (k g) p -> (b k) (g p)", g=2)).then_inc(ld_x0, 16)
            act.dma_start(sink_b, A["sinks"][0].partition_broadcast(P)).then_inc(ld_sink, 16)
            for b_ in range(NB):
                act.dma_start(sink_s[HEADS * b_:HEADS * (b_ + 1), :], A["sinks"][0].unsqueeze(1)).then_inc(ld_sink, 16)

            R = [rows[0:ST, j * P:(j + 1) * P] for j in range(16)]
            act.wait_ge(ld_par, 48)
            f(rows[0:ST, 14 * P + 2:14 * P + 4], rows[0:ST, 14 * P:14 * P + 2], ACT.Exp).then_inc(Z["par_exp"], 1)
            act.wait_ge(Z["par_red"], 1)
            f(R[4], R[15], ACT.Exp).then_inc(Z["par_exp"], 1)
            for c, (t0, nt) in enumerate(CHUNKS):
                if c == 0:
                    act.wait_ge(ld_x, 64)
                f(n_tok[0:nt, c], x_tok[0:nt, c], ACT.Square, accum_out=stat[0:nt, c, 0:1]).then_inc(Z["norm_ssq"], 1)
            act.wait_ge(Z["norm_ssq"], 6)
            for c, (t0, nt) in enumerate(CHUNKS):
                f(stat[0:nt, c, 1:2], stat[0:nt, c, 0:1], ACT.Sqrt).then_inc(Z["norm_root"], 1)
            act.wait_ge(Z["par_red"], 3)
            f(R[3], R[9], ACT.Sin)
            f(R[15], R[9], ACT.Sin, scale=0.5).then_inc(Z["par_sin"], 1)

            act.wait_ge(Z["vec_ps"], 1)
            f(vecs[:], bank(7, V_N), ACT.Copy).then_inc(Z["vec_sb"], 1)
            act.wait_ge(Z["par_ps"], 1)
            f(pcols, ps[:, 6, 0:7 * ST].rearrange("p (a b) -> p a b", a=7), ACT.Copy).then_inc(Z["par_sb"], 1)
            for j in range(4):
                act.wait_ge(Z["u_ps"], j + 1)
                f(proj[:, 6 + j, :], bank(j, T), ACT.Copy).then_inc(Z["u_sb"], 1)
            act.wait_ge(Z["c_ps"], 1)
            f(c_t[0], ps[:, 4].rearrange("p (k n) -> p k n", k=4), ACT.Copy)
            f(c_t[1], ps[:, 5].rearrange("p (k n) -> p k n", k=4), ACT.Copy)
            f(c_t[2], ps[:, 4].rearrange("p (k n) -> p k n", k=4), ACT.Copy, scale=-1.0).then_inc(Z["c_sb"], 1)
            act.wait_ge(Z["x0_ps"], 1)
            f(x0_t, ps[:, 6, 0:2 * P].rearrange("p (r n) -> p r n", r=2), ACT.Copy).then_inc(Z["x0_sb"], 1)
            act.wait_ge(Z["b_ps"], 1)
            f(b_t[0], ps[:, 4].rearrange("p (k n) -> p k n", k=4), ACT.Copy)
            f(b_t[1], ps[:, 5].rearrange("p (k n) -> p k n", k=4), ACT.Copy).then_inc(Z["b_sb"], 1)

            def qkv():
                for n_, slot in enumerate((4, 5, 0, 1, 2, 3)):
                    act.wait_ge(Z["q_ps"], n_ + 1)
                    m = f(proj[:, slot, :], bank(5 + n_ % 3, T), ACT.Copy)
                    m.then_inc(Z["q_sb"], 1)
                act.dma_start(kc, A["cache_k_win"][0].rearrange("b w n d -> w b (n d)")).then_inc(ld_cache, 16)
                act.dma_start(vc, A["cache_v_win"][0].rearrange("b w n d -> w b (n d)")).then_inc(ld_cache, 16)

            def kv_tokens():
                act.wait_ge(Z["tok_ps"], 1)
                chain(f(kv_tok[:], ps[:, 7, 0:3 * P].rearrange("p (a n) -> p a n", a=3), ACT.Copy))
                chain(f(kv_new[:], ps[0:NB, 6, 0:2 * P].rearrange("p (a n) -> p a n", a=2), ACT.Copy))
                nc.scalar.nop().then_inc(Z["tok_sb"], 1)
                act.dma_start(O[2][0, 0].rearrange("w n d -> w (n d)"), kv_tok[:, 2]).then_inc(Z["st_k"], 16)
                act.dma_start(O[3][0, 0].rearrange("w n d -> w (n d)"), kv_tok[:, 1]).then_inc(Z["st_k"], 16)
                for j in range(2):
                    act.dma_start(O[6 + j][0].rearrange("b w n d -> b w (n d)")[:, WIN - 1], kv_new[:, j]
                                  ).then_inc(Z["st_k"], 16)

            def exps(b):
                K = P * (b + 1)
                act.wait_ge(Z["m_neg"], b + 1)
                for h in range(HEADS):
                    f(sc[:, h, 0:K], sc[:, h, 0:K], ACT.Exp, bias=mneg[:, h:h + 1], scale=SCALE,
                      accum_out=rsum[:, h:h + 1])
                f(esink, esink, ACT.Exp).then_inc(Z["expd"], 1)

            fills = [0]

            def p_copies(b):
                for q in range(2 * (b + 1)):
                    fills[0] += 1
                    act.wait_ge(Z["p_ps"], fills[0])
                    f(pt[:, 4 * q:4 * q + 4], ps[:, 5 + q % 3].rearrange("p (k n) -> p k n", k=4), ACT.Copy
                      ).then_inc(Z["p_sb"], 1)

            def att_root(b):
                act.wait_ge(Z["att_sb"], b + 1)
                f(pt_flat[:, 0:D_ATTN], att[:, b], ACT.Square,
                  accum_out=small[:, 80 + b:81 + b]).then_inc(Z["att_ssq"], 1)
                act.wait_ge(Z["att_ssq"], 2 * b + 2)
                f(small[:, 84 + b:85 + b], small[:, 82 + b:83 + b], ACT.Sqrt).then_inc(Z["att_root"], 1)

            def cache_copies():
                for q, b_ in enumerate((5, 7)):
                    act.wait_ge(Z["kct_ps"], q + 1)
                    f(kc_t[:, 4 * q:4 * q + 4, 0:WIN], ps[:, b_].rearrange("p (k n) -> p k n", k=4), ACT.Copy
                      ).then_inc(Z["kct_sb"], 1)
                f(kc_t[:, :, WIN:WIN + 1], proj[:, 4, SEQ:T].unsqueeze(2), ACT.Copy).then_inc(Z["kct_sb"], 1)

            def sample_exp():
                act.wait_ge(Z["s_mneg"], 1)
                f(s_sc[:], s_sc[:], ACT.Exp, bias=s_small[0:64, 1:2], scale=SCALE, accum_out=s_small[0:64, 2:3])
                f(s_small[0:64, 3:4], s_small[0:64, 3:4], ACT.Exp).then_inc(Z["s_expd"], 1)

            def sample_root():
                act.wait_ge(Z["s_ops"], 1)
                act.wait_ge(Z["s_groot"], 1)
                f(s_small[0:64, 6:7], s_small[0:64, 5:6], ACT.Sqrt).then_inc(Z["s_groot"], 1)

            for i in range(ST):
                if i == AT_QKV:
                    qkv()
                if i == AT_KVTOK:
                    kv_tokens()
                if i == AT_B0:
                    exps(0)
                if i == AT_B0V:
                    p_copies(0)
                    att_root(0)
                if i == AT_B1:
                    exps(1)
                if i == AT_B1V:
                    p_copies(1)
                    att_root(1)
                if i == AT_S:
                    cache_copies()
                    sample_exp()
                if i == AT_SV:
                    sample_root()

            act.wait_ge(Z["ypre"], 1)
            f(y_t, proj[:, 6:10], ACT.Gelu_apprx_tanh).then_inc(Z["gelu"], 1)
            for c in range(KM):
                act.wait_ge(Z["glu_ps"], c + 1)
                if c >= 2:
                    act.wait_ge(Z["ssm_y"], c - 1)
                f(kc_t.rearrange("p b n -> p (b n)")[:, (c % 2) * T:(c % 2 + 1) * T], bank(c, T), ACT.Sigmoid,
                  bias=vecs[:, V_GLU + c:V_GLU + c + 1]).then_inc(Z["glu_sig"], 1)
            act.wait_ge(Z["state_ps"], 1)
            f(x0_t, ps[:, 7, 0:2 * P].rearrange("p (r n) -> p r n", r=2), ACT.Copy)
            chain(f(mini[0:ST, :].rearrange("p (r n) -> p r n", r=2),
                    ps[0:ST, 7, 2 * P:4 * P].rearrange("p (r n) -> p r n", r=2), ACT.Copy))
            for c in range(KM):
                act.wait_ge(Z["ssm_y"], c + 1)
                if c >= 2:
                    act.wait_ge(Z["ssm_ssq"], c - 1)
                f(sq[:, c % 2], fb[:, 4 + c, :], ACT.Square).then_inc(Z["ssm_sq"], 1)
            act.wait_ge(Z["ssm_ssq"], KM)
            act.wait_ge(Z["ssm_root"], 1)
            f(sq[:, 1], sq[:, 0], ACT.Sqrt).then_inc(Z["ssm_root"], 1)
            for r in range(2):
                act.dma_start(O[8 + r][0].rearrange("b (k g) p -> (b k) (g p)", g=2), x0_t[:, r]).then_inc(Z["st_k"], 16)
                act.dma_start(O[4 + r][0, 0].rearrange("(k g) p -> k (g p)", g=2), mini[0:ST, r * P:(r + 1) * P]
                              ).then_inc(Z["st_k"], 16)
            for o in range(KD):
                act.wait_ge(Z["mix_ps"], o + 1)
                f(fa[:, o, :], bank(o % 4, T), ACT.Copy).then_inc(Z["mix_sb"], 1)
            for c, (t0, nt) in enumerate(CHUNKS):
                act.wait_ge(Z["back_add"], 4 + c)
                f(n_tok[0:nt, c], x_tok[0:nt, c], ACT.Square, accum_out=stat[0:nt, c, 0:1]).then_inc(Z["norm_ssq"], 1)
            act.wait_ge(Z["norm_ssq"], 12)
            for c, (t0, nt) in enumerate(CHUNKS):
                f(stat[0:nt, c, 1:2], stat[0:nt, c, 0:1], ACT.Sqrt).then_inc(Z["norm_root"], 1)
            act.wait_ge(Z["topv"], 1)
            for c, (t0, nt) in enumerate(CHUNKS):
                f(top[0:nt, c, 16:20], top[0:nt, c, 0:4], ACT.Exp, bias=top[0:nt, c, 12:13],
                  accum_out=top[0:nt, c, 20:21]).then_inc(Z["w_exp"], 1)
            act.wait_ge(Z["gtr_ps"], 1)
            f(gates_t[0:NE, 0:T], ps[0:NE, 3, 0:T], ACT.Copy).then_inc(Z["gtr_sb"], 1)
            act.wait_ge(Z["hot_rdy"], 1)
            act.dma_start(b_up[0:NE, :], A["b_up"][0]).then_inc(ld_bup, 16)
            act.dma_start(p_tok[:, 0:2], A["p_prompt"][0, 0].rearrange("(c p) n -> p c n", p=P)).then_inc(ld_p, 16)
            act.dma_start(p_tok[0:NB, 2], A["p_sample"][0].rearrange("b l n -> (b l) n")).then_inc(ld_p, 16)

            def activation(t):
                act.wait_ge(Z["g_rdy"], t + 1)
                f(sig, g_lim, ACT.Sigmoid, scale=ALPHA).then_inc(Z["sig_rdy"], 1)
                act.wait_ge(Z["at_ps"], t + 1)
                f(act_t, ps[:, 3].rearrange("p (j n) -> p j n", j=4), ACT.Copy).then_inc(Z["at_sb"], 1)

            def selection(n_):
                act.wait_ge(Z["gt_ps"], n_ + 1)
                f(g_t[:, 0:T], ps[:, 3, 0:T], ACT.Copy).then_inc(Z["gt_sb"], 1)

            def outputs(t, a):
                act.wait_ge(Z["dn_free"], DN * t + DN)
                for half in range(2):
                    m = f(out_e[C * a:C * a + C, half], ps[64 * half:64 * half + 64, 4], ACT.Copy)
                m.then_inc(Z["dn_sb"], 1)

            with act.Fori(0, PAIRS) as p:
                activation(2 * p)
                outputs(2 * p, 0)
                selection(p)
                activation(2 * p + 1)
                outputs(2 * p + 1, 1)

            def visit(v, _):
                activation(NE + v)
                outputs(NE + v, 0)
                selection(PAIRS + v)

            further_visits(act, visit)

            act.wait_ge(Z["pT_ps"], 1)
            f(p_t, ps[:, 3:5, 0:T], ACT.Copy).then_inc(Z["pT_sb"], 1)
            for c, (t0, nt) in enumerate(CHUNKS):
                if c == 0:
                    act.wait_ge(Z["all_added"], 1)
                f(n_tok[0:nt, c], x_tok[0:nt, c], ACT.Square, accum_out=stat[0:nt, c, 0:1]).then_inc(Z["norm_ssq"], 1)
            act.wait_ge(Z["norm_ssq"], 18)
            for c, (t0, nt) in enumerate(CHUNKS):
                f(stat[0:nt, c, 1:2], stat[0:nt, c, 0:1], ACT.Sqrt).then_inc(Z["norm_root"], 1)
            for o in range(KD):
                act.wait_ge(Z["pp_ps"], o + 1)
                f(fa[:, o, :], bank(3 + o % 3, T), ACT.Copy).then_inc(Z["pp_sb"], 1)
            for o in range(KD):
                act.wait_ge(Z["gz_ps"], o + 1)
                if o >= 2:
                    act.wait_ge(Z["gz_mul"], o - 1)
                f(sg_t[:, o % 2], bank(o % 4, T), ACT.Sigmoid).then_inc(Z["gz_sig"], 1)
            for c, (t0, nt) in enumerate(CHUNKS):
                act.wait_ge(Z["back_add"], 6 + 4 + c)
                f(n_tok[0:nt, c], x_tok[0:nt, c], ACT.Square, accum_out=stat[0:nt, c, 0:1]).then_inc(Z["norm_ssq"], 1)
            act.wait_ge(Z["norm_ssq"], 24)
            for c, (t0, nt) in enumerate(CHUNKS):
                f(stat[0:nt, c, 1:2], stat[0:nt, c, 0:1], ACT.Sqrt).then_inc(Z["norm_root"], 1)
            act.wait_ge(Z["st_k"], 32 + 16 * 8)

        @block.vector
        def _(dve):
            V = nc.vector
            n = [0]

            def chain(ins):
                n[0] += 1
                ins.then_inc(dve_step, 1)
                dve.wait_ge(dve_step, n[0])

            def norm_rows(n_):
                dve.wait_ge(Z["norm_ssq"], 6 * n_ + 3)
                for c, (t0, nt) in enumerate(CHUNKS):
                    V.tensor_scalar(stat[0:nt, c, 0:1], stat[0:nt, c, 0:1], 1.0 / D, EPS, ALU.mult, ALU.add
                                    ).then_inc(Z["norm_ssq"], 1)
                for c, (t0, nt) in enumerate(CHUNKS):
                    dve.wait_ge(Z["norm_root"], 3 * n_ + c + 1)
                    chain(V.reciprocal(stat[0:nt, c, 2:3], stat[0:nt, c, 1:2]))
                    if n_ < 3:
                        V.tensor_scalar(n_tok[0:nt, c], x_tok[0:nt, c], stat[0:nt, c, 2:3], None, ALU.mult
                                        ).then_inc(Z["norm_scaled"], 1)

            R = [rows[0:ST, j * P:(j + 1) * P] for j in range(16)]
            l_re, l_im = R[12], R[13]
            dt = rows[0:ST, 14 * P + 2:14 * P + 4].unsqueeze(2).to_broadcast([ST, 2, S])

            def halves(x):
                return x.rearrange("k (g p) -> k g p", g=2)

            dve.wait_ge(Z["par_exp"], 1)
            V.tensor_tensor(halves(R[15]), halves(l_re), dt, ALU.mult).then_inc(Z["par_red"], 1)
            chain(V.tensor_tensor(halves(R[9]), halves(l_im), dt, ALU.mult))
            two_pi_hi, magic = 6.28125, 12582912.0
            two_pi_lo = 2.0 * np.pi - two_pi_hi
            chain(V.tensor_scalar(R[8], R[9], 1.0 / (2.0 * np.pi), magic, ALU.mult, ALU.add))
            chain(V.tensor_scalar(R[8], R[8], -magic, None, ALU.add))
            chain(V.scalar_tensor_tensor(R[9], R[8], -two_pi_hi, R[9], ALU.mult, ALU.add))
            chain(V.scalar_tensor_tensor(R[9], R[8], -float(two_pi_lo), R[9], ALU.mult, ALU.add))
            dve.wait_ge(Z["par_exp"], 2)
            V.tensor_scalar(R[9], R[9], 3.1415925, -3.1415925, ALU.min, ALU.max).then_inc(Z["par_red"], 2)
            norm_rows(0)
            chain(V.tensor_tensor(R[8], l_re, l_re, ALU.mult))
            chain(V.tensor_tensor(R[7], l_im, l_im, ALU.mult))
            chain(V.tensor_tensor(R[8], R[8], R[7], ALU.add))
            chain(V.reciprocal(R[8], R[8]))
            dve.wait_ge(Z["par_sin"], 1)
            chain(V.tensor_tensor(R[2], R[15], R[15], ALU.mult))
            chain(V.tensor_scalar(R[2], R[2], -2.0, 1.0, ALU.mult, ALU.add))
            chain(V.tensor_tensor(R[5], R[4], R[2], ALU.mult))
            chain(V.tensor_tensor(R[6], R[4], R[3], ALU.mult))
            chain(V.tensor_scalar(R[9], R[5], -1.0, None, ALU.add))
            chain(V.tensor_tensor(R[7], R[9], l_re, ALU.mult))
            chain(V.tensor_tensor(R[15], R[6], l_im, ALU.mult))
            chain(V.tensor_tensor(R[7], R[7], R[15], ALU.add))
            chain(V.tensor_tensor(R[7], R[7], R[8], ALU.mult))
            chain(V.tensor_tensor(R[15], R[9], l_im, ALU.mult))
            chain(V.tensor_tensor(R[9], R[6], l_re, ALU.mult))
            chain(V.tensor_tensor(R[9], R[9], R[15], ALU.subtract))
            V.tensor_tensor(R[8], R[9], R[8], ALU.mult).then_inc(Z["par_rows"], 1)
            dve.wait_ge(Z["vec_sb"], 1)
            for c, (t0, nt) in enumerate(CHUNKS):
                for half in range(2):
                    dve.wait_ge(Z["norm_ps"], 0 + 2 * c + half + 1)
                    V.tensor_tensor(fa[:, 4 * half:4 * half + 4, t0:t0 + nt],
                                    ps[:, 2 * c + half, 0:4 * nt].rearrange("p (k n) -> p k n", k=4),
                                    col(vecs[:, V_MIX + 4 * half:V_MIX + 4 * half + 4], nt), ALU.mult
                                    ).then_inc(Z["norm_sb"], 1)
            dve.wait_ge(Z["par_sb"], 1)

            def scan(i):
                a = i % 2
                cs = cos_t[:, a].unsqueeze(1).to_broadcast([P, 2, SEQ])
                sn = sin_t[:, a].unsqueeze(1).to_broadcast([P, 2, SEQ])
                decay = pcols[:, 2, i:i + 1].to_broadcast([P, SEQ])
                dve.wait_ge(Z["trig"], i + 1)
                dve.wait_ge(Z["bu_ps"], i + 1)
                V.tensor_copy(bu_s[:, :, i, :], ps[:, 0:2, SEQ:T])
                V.tensor_tensor(prod_p, ps[:, 0:2, 0:SEQ], cs, ALU.mult)
                q = ps[:, 2].rearrange("p (r t) -> p r t", r=2)
                z = ps[:, 3].rearrange("p (r t) -> p r t", r=2)
                m = V.tensor_tensor(q, ps[:, 0:2, 0:SEQ], sn, ALU.mult)
                m.then_inc(Z["bu_read"], 1)
                dve.wait_ge(Z["bu_read"], i + 1)
                V.tensor_tensor(z_in[:, 0], prod_p[:, 0], q[:, 1], ALU.add)
                chain(V.tensor_tensor(z_in[:, 1], prod_p[:, 1], q[:, 0], ALU.subtract))
                V.tensor_tensor_scan(z[:, 0], decay, z_in[:, 0], 0.0, ALU.mult, ALU.add)
                chain(V.tensor_tensor_scan(z[:, 1], decay, z_in[:, 1], 0.0, ALU.mult, ALU.add))
                if i >= 2:
                    dve.wait_ge(Z["y_rot"], i - 1)
                    dve.wait_ge(Z["last_in"], i - 1)
                V.tensor_tensor(rot_c[:, a], z, cs, ALU.mult)
                V.tensor_tensor(rot_s[:, a], z, sn, ALU.mult).then_inc(Z["rot_ready"], 1)

            def biases(b):
                K = P * (b + 1)
                for c in range(4):
                    dve.wait_ge(Z["score_ps"], 4 * b + c + 1)
                    for n_ in range(KV):
                        h = 4 * n_ + c
                        m = V.scalar_tensor_tensor(sc[:, h, 0:K], kst[:, K_DIST + 2 * P - K:K_DIST + 2 * P],
                                                   -SLOPES[h] / SCALE, bank(5 + n_, K), ALU.mult, ALU.add)
                    m.then_inc(Z["score_read"], 1)
                if b == 0:
                    dve.wait_ge(ld_sink, 16 * (NB + 1))
                dve.wait_ge(Z["score_read"], 4 * b + 4)
                chain(V.tensor_reduce(mx, sc[:, :, 0:K], AX.X, ALU.max))
                chain(V.scalar_tensor_tensor(mx, mx, SCALE, sink_b, ALU.mult, ALU.max))
                chain(V.tensor_scalar(mneg, mx, -1.0, None, ALU.mult))
                V.tensor_tensor(esink, sink_b, mneg, ALU.add).then_inc(Z["m_neg"], 1)

            def attended(b):
                dve.wait_ge(Z["expd"], b + 1)
                chain(V.tensor_tensor(rden, rsum, esink, ALU.add))
                chain(V.reciprocal(rden, rden))
                dve.wait_ge(Z["o_ps"], b + 1)
                V.tensor_tensor(att[:, b].rearrange("p (h d) -> p h d", h=HEADS),
                                ps[:, 5].rearrange("p (h d) -> p h d", h=HEADS), col(rden, HD), ALU.mult
                                ).then_inc(Z["att_sb"], 1)
                dve.wait_ge(Z["att_ssq"], 2 * b + 1)
                V.tensor_scalar(small[:, 82 + b:83 + b], small[:, 80 + b:81 + b], 1.0 / D_ATTN, EPS, ALU.mult, ALU.add
                                ).then_inc(Z["att_ssq"], 1)
                dve.wait_ge(Z["att_root"], b + 1)
                chain(V.reciprocal(small[:, 86 + b:87 + b], small[:, 84 + b:85 + b]))
                V.tensor_scalar(att[:, b], att[:, b], small[:, 86 + b:87 + b], None, ALU.mult
                                ).then_inc(Z["att_scaled"], 1)
                dve.wait_ge(Z["att_ps"], b + 1)
                V.tensor_tensor(fb[:, 0:4, b * P:(b + 1) * P], ps[:, 6].rearrange("p (k n) -> p k n", k=4),
                                col(vecs[:, V_OUT:V_OUT + 4], P), ALU.mult).then_inc(Z["att_t"], 1)

            sp72 = spread.rearrange("p (b s) -> p b s", s=72)

            def sample_bias():
                chain(V.memset(spread, 0.0))
                for c in range(4):
                    for n_ in range(KV):
                        r = slice(64 * n_, 64 * n_ + 64)
                        m = V.tensor_copy(sp72[r, :, 4 * n_ + c:4 * n_ + c + 1], proj[r, c, SEQ:T].unsqueeze(2))
                m.then_inc(Z["q_spread"], 1)
                dve.wait_ge(Z["ssc_ps"], 1)
                chain(V.tensor_tensor(s_sc[:], ps[0:64, 5, 0:WIN + 1], kst[0:64, K_SBIAS:K_SBIAS + WIN + 1], ALU.add))
                chain(V.tensor_reduce(s_small[0:64, 0:1], s_sc[:], AX.X, ALU.max))
                chain(V.scalar_tensor_tensor(s_small[0:64, 0:1], s_small[0:64, 0:1], SCALE, sink_s[0:64], ALU.mult, ALU.max))
                chain(V.tensor_scalar(s_small[0:64, 1:2], s_small[0:64, 0:1], -1.0, None, ALU.mult))
                V.tensor_tensor(s_small[0:64, 3:4], sink_s[0:64], s_small[0:64, 1:2], ALU.add).then_inc(Z["s_mneg"], 1)

            def sample_out():
                dve.wait_ge(Z["s_expd"], 1)
                V.tensor_scalar(s_own[:], kst[0:64, K_OWN:K_OWN + NB], s_sc[:, WIN:WIN + 1], None, ALU.mult
                                ).then_inc(Z["s_oready"], 1)
                chain(V.tensor_tensor(s_small[0:64, 4:5], s_small[0:64, 2:3], s_small[0:64, 3:4], ALU.add))
                chain(V.reciprocal(s_small[0:64, 4:5], s_small[0:64, 4:5]))
                dve.wait_ge(Z["s_pps"], 1)
                V.tensor_copy(s_ownT[:], ps[0:NB, 7, 64:128]).then_inc(Z["s_pspread"], 1)
                V.tensor_copy(sp72[:, :, 0:HEADS], ps[:, 7, 0:64].rearrange("p (b h) -> p b h", b=NB)
                              ).then_inc(Z["s_pspread"], 1)
                dve.wait_ge(Z["s_ops"], 1)
                chain(V.tensor_scalar(s_o[:, 0], ps[0:64, 5, 0:64], kst[0:64, K_HALF:K_HALF + 1], s_small[0:64, 4:5],
                                      ALU.mult, ALU.mult))
                chain(V.tensor_scalar(s_o[:, 1], ps[0:64, 5, 64:128], kst[0:64, K_HALF + 1:K_HALF + 2],
                                      s_small[0:64, 4:5], ALU.mult, ALU.mult))
                chain(V.tensor_tensor(s_o[:, 0], s_o[:, 0], s_o[:, 1], ALU.add))
                chain(V.tensor_tensor(s_o[:, 1], s_o[:, 0], s_o[:, 0], ALU.mult))
                V.tensor_reduce(s_small[0:64, 5:6], s_o[:, 1], AX.X, ALU.add).then_inc(Z["s_ossq"], 1)
                dve.wait_ge(Z["s_gps"], 1)
                V.tensor_scalar(s_small[0:64, 5:6], ps[0:64, 7, 0:1], 1.0 / D_ATTN, EPS, ALU.mult, ALU.add
                                ).then_inc(Z["s_groot"], 1)
                dve.wait_ge(Z["s_groot"], 2)
                chain(V.reciprocal(s_small[0:64, 7:8], s_small[0:64, 6:7]))
                chain(V.tensor_scalar(s_o[:, 0], s_o[:, 0], s_small[0:64, 7:8], None, ALU.mult))
                V.tensor_copy(s_o[:, 1], s_o[:, 0]).then_inc(Z["s_onorm"], 1)
                dve.wait_ge(Z["s_otps"], 1)
                for par in range(2):
                    r = slice(64 * par, 64 * par + 64)
                    m = V.tensor_tensor(fb[r, 0:4, SEQ:T],
                                        ps[r, 6, 0:64].rearrange("p (b c a) -> p a c b", b=NB, a=2)[:, par],
                                        col(vecs[r, V_OUT:V_OUT + 4], NB), ALU.mult)
                m.then_inc(Z["s_ot"], 1)

            for i in range(ST + 1):
                if i < ST:
                    scan(i)
                if i == AT_B0:
                    biases(0)
                if i == AT_B0V:
                    attended(0)
                if i == AT_B1:
                    biases(1)
                if i == AT_B1V:
                    attended(1)
                if i == AT_S:
                    sample_bias()
                if i == AT_SV:
                    sample_out()
                if i >= 4 and i % 4 == 0:
                    c = i // 4 - 1
                    dve.wait_ge(Z["y_rot"], 4 * c + 4)
                    dve.wait_ge(Z["bu_ps"], 4 * c + 4)
                    V.scalar_tensor_tensor(proj[:, 6 + c, 0:SEQ], proj[:, 6 + c, 0:SEQ], vecs[:, V_D + c:V_D + c + 1],
                                           ps[:, 4, 0:SEQ], ALU.mult, ALU.add).then_inc(Z["y_read"], 1)
            dve.wait_ge(Z["x0_sb"], 1)
            x0 = [x0_t[:, r].rearrange("p (b a) -> p a b", a=ST) for r in range(2)]
            lr, li = col(pcols[:, 3], NB), col(pcols[:, 4], NB)
            t1 = s5_mem[:, 1280:1408].rearrange("p (a b) -> p a b", a=ST)
            for r, (f0, f1, op) in enumerate(((lr, li, ALU.subtract), (li, lr, ALU.add))):
                chain(V.tensor_tensor(xs_new[:, r], x0[0], f0, ALU.mult))
                chain(V.tensor_tensor(t1, x0[1], f1, ALU.mult))
                chain(V.tensor_tensor(xs_new[:, r], xs_new[:, r], t1, op))
                chain(V.tensor_tensor(xs_new[:, r], xs_new[:, r], bu_s[:, r], ALU.add))
            V.engine_nop().then_inc(Z["state_s"], 1)
            dve.wait_ge(Z["ys_ps"], 1)
            for c in range(KM):
                chain(V.scalar_tensor_tensor(proj[:, 6 + c, SEQ:T], proj[:, 6 + c, SEQ:T], vecs[:, V_D + c:V_D + c + 1],
                                             ps[:, 5, NB * c:NB * c + NB], ALU.mult, ALU.add))
            V.engine_nop().then_inc(Z["ypre"], 1)
            dve.wait_ge(Z["last_in"], ST)
            V.engine_nop().then_inc(Z["s5_free"], 1)
            for c in range(KM):
                dve.wait_ge(Z["glu_sig"], c + 1)
                V.tensor_tensor(fb[:, 4 + c, :], y_t[:, c, :],
                                kc_t.rearrange("p b n -> p (b n)")[:, (c % 2) * T:(c % 2 + 1) * T], ALU.mult
                                ).then_inc(Z["ssm_y"], 1)
            dve.wait_ge(Z["ssm_ssq"], KM)
            V.tensor_scalar(sq[:, 0], bank(6, T), 1.0 / D_SSM, EPS, ALU.mult, ALU.add).then_inc(Z["ssm_root"], 1)
            dve.wait_ge(Z["ssm_root"], 2)
            chain(V.reciprocal(sq[:, 0], sq[:, 1]))
            for c in range(KM):
                V.scalar_tensor_tensor(fb[:, 4 + c, :], fb[:, 4 + c, :], vecs[:, V_OUT + 4 + c:V_OUT + 5 + c], sq[:, 0],
                                       ALU.mult, ALU.mult).then_inc(Z["ssm_n"], 1)
            n_ = 0
            for half in range(2):
                for c, (t0, nt) in enumerate(CHUNKS):
                    n_ += 1
                    dve.wait_ge(Z["back_ps"], n_)
                    xh = x_tok[0:nt, c, 512 * half:512 * half + 512]
                    V.tensor_tensor(xh, xh, ps[0:nt, 4 + (n_ - 1) % 2, :], ALU.add).then_inc(Z["back_add"], 1)
            norm_rows(1)
            for c, (t0, nt) in enumerate(CHUNKS):
                for half in range(2):
                    dve.wait_ge(Z["norm_ps"], 6 + 2 * c + half + 1)
                    b_ = (0, 1, 2, 3, 6, 7)[2 * c + half]
                    V.tensor_tensor(fb[:, 4 * half:4 * half + 4, t0:t0 + nt],
                                    ps[:, b_, 0:4 * nt].rearrange("p (k n) -> p k n", k=4),
                                    col(vecs[:, V_FFN + 4 * half:V_FFN + 4 * half + 4], nt), ALU.mult
                                    ).then_inc(Z["norm_sb"], 1)
            V.memset(mask, 0.0)
            V.memset(gate[:], 0.0)
            chain(V.memset(rank[:], -1.0))
            chain(V.memset(sel_g, 0.0))
            chain(V.memset(g_t, 0.0))
            chain(V.memset(gates_t, 0.0))
            V.engine_nop().then_inc(Z["region_free"], 1)
            dve.wait_ge(Z["lg_ps"], 1)
            dve.wait_ge(ld_router, 64)
            for c, (t0, nt) in enumerate(CHUNKS):
                r = slice(0, nt)
                chain(V.tensor_tensor(logits[r, c], ps[r, 4, c * NE:(c + 1) * NE], router_b[r], ALU.add))
                chain(V.max(top[r, c, 0:8], logits[r, c]))
                V.tensor_scalar(top[r, c, 12:13], top[r, c, 0:1], -1.0, None, ALU.mult)
                chain(V.max_index(top_i[r, c], top[r, c, 0:8], logits[r, c]))
                chain(V.tensor_copy(top[r, c, 24:32], top_i[r, c]))
            V.engine_nop().then_inc(Z["topv"], 1)
            for c, (t0, nt) in enumerate(CHUNKS):
                r = slice(0, nt)
                iota = kst[r, K_IOTA:K_IOTA + NE].unsqueeze(1).to_broadcast([nt, TOPK, NE])
                chain(V.tensor_tensor(pick[r], iota, col(top[r, c, 24:28], NE), ALU.is_equal))
                chain(V.tensor_reduce(mask[r, c], pick[r].rearrange("p k e -> p e k"), AX.X, ALU.add))
                dve.wait_ge(Z["w_exp"], c + 1)
                chain(V.reciprocal(top[r, c, 21:22], top[r, c, 20:21]))
                chain(V.tensor_scalar(top[r, c, 16:20], top[r, c, 16:20], top[r, c, 21:22], None, ALU.mult))
                chain(V.tensor_tensor(pick[r], pick[r], col(top[r, c, 16:20], NE), ALU.mult))
                chain(V.tensor_reduce(gate[r, c, 0:NE], pick[r].rearrange("p k e -> p e k"), AX.X, ALU.add))
            V.engine_nop().then_inc(Z["mask_sb"], 1)
            dve.wait_ge(Z["cnt_ps"], 1)
            chain(V.scalar_tensor_tensor(rank[:, :, 0:NE], ps[:, 5, 0:3 * NE].rearrange("p (c n) -> p c n", c=3), 1.0, mask,
                                         ALU.add, ALU.mult))
            chain(V.tensor_scalar(rank[:, :, 0:NE], rank[:, :, 0:NE], -1.0, None, ALU.add))
            chain(V.tensor_tensor(v_cnt, ps[:, 5, 3 * NE:4 * NE], kst[:, K_NTH:K_NTH + NE], ALU.mult))

            iota2 = kst[:, K_IOTA:K_IOTA + C].unsqueeze(1).unsqueeze(1).to_broadcast([P, 3, 2, C])

            def of_pair(table, p):
                return table[:, :, bass.ds(2 * p, 2)].unsqueeze(3).to_broadcast([P, 3, 2, C])

            def select(p):
                V.tensor_tensor(sel, iota2, of_pair(rank, p), ALU.is_equal).then_inc(Z["sel_rdy"], 1)

            def visit_list():
                chain(V.tensor_reduce(v_flag, v_cnt, AX.X, ALU.add))
                V.tensor_tensor(v_flag, v_flag, kst[:, K_OF:K_OF + 1], ALU.is_gt).then_inc(Z["vis_flag"], 1)
                dve.wait_ge(Z["vis_pos"], 1)
                dve.wait_ge(Z["vis_flag"], 1)
                chain(V.tensor_copy(v_pos, ps[:, 5, 0:1]))
                chain(V.tensor_scalar(v_hot, kst[:, K_IOTA:K_IOTA + VISITS], v_pos, None, ALU.is_equal))
                chain(V.tensor_scalar(v_hot, v_hot, v_flag, None, ALU.mult))
                V.tensor_scalar(v_from, v_hot, kst[:, K_OF:K_OF + 1], None, ALU.mult).then_inc(Z["vis_hot"], 1)
                dve.wait_ge(Z["vis_ps"], 1)
                chain(V.tensor_copy(v_first, ps[:, 5, 0:VISITS]))
                V.tensor_copy(vis_int[:], ps[0:1, 5, 64:65 + VISITS]).then_inc(Z["n_ready"], 1)

            def gathered(p):
                for h in range(2):
                    dve.wait_ge(Z["xg_ps"], 2 * p + h + 1)
                    V.tensor_tensor(xe[:, 4 * h:4 * h + 4], ps[:, (2, 5)[h]].rearrange("p (k s) -> p k s", k=4),
                                    col(vecs[:, V_FFN + 4 * h:V_FFN + 4 * h + 4], 2 * C), ALU.mult
                                    ).then_inc(Z["xe_rdy"], 1)

            def added(n_):
                if not (isinstance(n_, int) and n_ == 0):
                    dve.wait_ge(Z["cmb_read"], 4 * n_)
                for c, (t0, nt) in enumerate(CHUNKS):
                    dve.wait_ge(Z["cmb_ps"], 3 * n_ + c + 1)
                    xh = x_tok[0:nt, c].rearrange("p (a n) -> p a n", a=2)
                    if c < 2:
                        b_ = (6, 0)[c]
                        V.tensor_tensor(xh, xh, ps[0:nt, b_:b_ + 2, :], ALU.add).then_inc(Z["cmb_read"], 1)
                    else:
                        V.tensor_tensor(xh[:, 0], xh[:, 0], ps[0:nt, 2, :], ALU.add).then_inc(Z["cmb_read"], 1)
                        V.tensor_tensor(xh[:, 1], xh[:, 1], ps[64:64 + nt, 2, :], ALU.add).then_inc(Z["cmb_read"], 1)

            def activation(t):
                dve.wait_ge(Z["hid_ps"], t + 1)
                V.tensor_scalar(g_lim, bank(0), LIMIT, None, ALU.min).then_inc(Z["g_rdy"], 1)
                V.tensor_scalar(u_lim, bank(1), -LIMIT, LIMIT, ALU.max, ALU.min).then_inc(dve_loop, 1)
                dve.wait_ge(dve_loop, 2 * t + 1)
                dve.wait_ge(Z["g_rdy"], t + 1)
                V.scalar_tensor_tensor(u_lim, u_lim, 1.0, g_lim, ALU.add, ALU.mult).then_inc(dve_loop, 1)
                dve.wait_ge(dve_loop, 2 * t + 2)
                dve.wait_ge(Z["sig_rdy"], t + 1)
                V.tensor_tensor(act_v, u_lim, sig, ALU.mult).then_inc(Z["act_rdy"], 1)

            def pair(p, place=None):
                dve.wait_ge(Z["sel_rdy"], p + 1)
                if place != "first":
                    dve.wait_ge(Z["gt_ps"], p)
                V.tensor_tensor(sel_g, sel, of_pair(gate, p), ALU.mult).then_inc(Z["selg_rdy"], 1)
                if place != "last":
                    dve.wait_ge(Z["selg_rdy"], p + 1)
                    select(p + 1)
                activation(2 * p)
                if place == "first":
                    added(0)
                    visit_list()
                else:
                    added(p)
                activation(2 * p + 1)
                if place != "last":
                    gathered(p + 1)

            def visit(v, e):
                dve.wait_ge(Z["sel_rdy"], PAIRS + v)
                V.tensor_tensor(v_rank.unsqueeze(2), rank[:, :, bass.ds(e, 1)],
                                v_first[:, bass.ds(v, 1)].unsqueeze(1).to_broadcast([P, 3, 1]), ALU.subtract
                                ).then_inc(Z["v_rank"], 1)
                dve.wait_ge(Z["v_rank"], v + 1)
                V.tensor_tensor(sel[:, :, 0], kst[:, K_IOTA:K_IOTA + C].unsqueeze(1).to_broadcast([P, 3, C]),
                                v_rank.unsqueeze(2).to_broadcast([P, 3, C]), ALU.is_equal).then_inc(Z["sel_rdy"], 1)
                dve.wait_ge(Z["sel_rdy"], PAIRS + 1 + v)
                dve.wait_ge(Z["gt_ps"], PAIRS + v)
                V.tensor_tensor(sel_g[:, :, 0], sel[:, :, 0], gate[:, :, bass.ds(e, 1)].to_broadcast([P, 3, C]), ALU.mult
                                ).then_inc(Z["selg_rdy"], 1)
                dve.wait_ge(Z["xg_ps"], 2 * PAIRS + 1 + v)
                V.tensor_tensor(xe[:, :, 0:C], ps[:, 2].rearrange("p (k s) -> p k s", k=KD),
                                col(vecs[:, V_FFN:V_FFN + KD], C), ALU.mult).then_inc(Z["xe_rdy"], 1)
                activation(NE + v)
                added(PAIRS + 1 + v)

            select(0)
            gathered(0)
            pair(0, "first")
            with dve.Fori(1, PAIRS - 1) as p:
                pair(p)
            pair(PAIRS - 1, "last")
            added(PAIRS)
            n_visits = further_visits(dve, visit, expert_of=True)
            dve.wait_ge(Z["cmb_read"], (n_visits + (PAIRS + 1)) * 4)
            V.memset(stat[:], 0.0).then_inc(Z["all_added"], 1)

            norm_rows(2)
            for c, (t0, nt) in enumerate(CHUNKS):
                for half in range(2):
                    dve.wait_ge(Z["norm_ps"], 12 + 2 * c + half + 1)
                    b_ = (0, 1, 6, 7, 2, 5)[2 * c + half]
                    V.tensor_tensor(fb[:, 4 * half:4 * half + 4, t0:t0 + nt],
                                    ps[:, b_, 0:4 * nt].rearrange("p (k n) -> p k n", k=4),
                                    col(vecs[:, V_PLE + 4 * half:V_PLE + 4 * half + 4], nt), ALU.mult
                                    ).then_inc(Z["norm_sb"], 1)

            def residual(half):
                for c, (t0, nt) in enumerate(CHUNKS):
                    n_ = 3 * half + c
                    dve.wait_ge(Z["back_ps"], 6 + n_ + 1)
                    xh = x_tok[0:nt, c, 512 * half:512 * half + 512]
                    V.tensor_tensor(xh, xh, ps[0:nt, 4 + n_ % 2, :], ALU.add).then_inc(Z["back_add"], 1)

            dve.wait_ge(Z["pp_sb"], KD)
            for o in range(KD):
                dve.wait_ge(Z["gz_sig"], o + 1)
                V.tensor_tensor(fa[:, o, :], fa[:, o, :], sg_t[:, o % 2], ALU.mult).then_inc(Z["gz_mul"], 1)
                if o == 5:
                    residual(0)
            residual(1)
            norm_rows(3)
            dve.wait_ge(ld_router, 64)
            for c, (t0, nt) in enumerate(CHUNKS):
                V.scalar_tensor_tensor(n_tok[0:nt, c], x_tok[0:nt, c], stat[0:nt, c, 2:3], final_g[0:nt, :], ALU.mult,
                                       ALU.mult).then_inc(Z["f_out"], 1)


_INS = ['x_prompt', 'x_sample', 'cache_k_win', 'cache_v_win', 'state_ssm_re', 'state_ssm_im', 'p_prompt', 'p_sample',
        'norm_mix', 'w_in', 'sinks', 'ssm_lam_re', 'ssm_lam_im', 'ssm_log_step', 'ssm_b_re', 'ssm_b_im', 'ssm_c_re',
        'ssm_c_im', 'ssm_d', 'w_glu', 'b_glu', 'norm_attn_out', 'norm_ssm_out', 'w_out', 'norm_ffn', 'w_router',
        'b_router', 'w_up', 'b_up', 'w_down', 'b_down', 'norm_ple', 'w_ple_gate', 'w_ple_proj', 'norm_final']
_OUTS = [(1, SEQ, D), (NB, 1, D), (1, 1, WIN, KV, HD), (1, 1, WIN, KV, HD), (1, 1, G, S), (1, 1, G, S),
         (1, NB, WIN, KV, HD), (1, NB, WIN, KV, HD), (1, NB, G, S), (1, NB, G, S)]


def kernel(**inputs):
    import numpy as _np
    import concourse.bacc as _bacc
    from concourse import mybir as _mybir
    from concourse.bass_utils import run_bass_kernel_spmd as _run

    nc = _bacc.Bacc("TRN2", target_bir_lowering=False, num_devices=1)
    arrays, aps = {}, {}
    for name in _INS + ["shape_constants"]:
        a = shape_constants() if name == "shape_constants" else _np.ascontiguousarray(inputs[name])
        arrays[f"in_{name}_dram"] = a
        aps[name] = nc.dram_tensor(f"in_{name}_dram", a.shape, _mybir.dt.from_np(a.dtype), kind="ExternalInput").ap()
    outs = [nc.dram_tensor(f"out_{i}_dram", shape, F32, kind="ExternalOutput").ap() for i, shape in enumerate(_OUTS)]
    hybrid_layer(nc, aps, outs)
    r = _run(nc, [arrays], core_ids=[0])
    return tuple(r.results[0][f"out_{i}_dram"] for i in range(len(_OUTS)))
```

```python
from contextlib import ExitStack

import numpy as np

import concourse.bass as bass
from concourse import mybir

F32 = mybir.dt.float32
I32 = mybir.dt.int32
U32 = mybir.dt.uint32
ALU = mybir.AluOpType
ACT = mybir.ActivationFunctionType
AX = mybir.AxisListType

P = 128
D = 1024
SEQ, NB = 256, 8
T = SEQ + NB
KD = D // P
HEADS, KV, HD = 8, 2, 64
D_ATTN = HEADS * HD
WIN = 128
G, H, S = 32, 16, 64
D_SSM = G * H
KM = D_SSM // P
D_IN = D_ATTN + 2 * KV * HD + D_SSM
ST = G // 2
NE, TOPK, FF = 32, 4, 1024
PLE = 256
EPS = 1e-5
LIMIT, ALPHA = 7.0, 1.702
C = 64
PAIRS = NE // 2
VISITS = T * TOPK // (C + 1)
CHUNKS = [(0, P), (P, P), (SEQ, NB)]
SLOPES = [2.0 ** (-8.0 * (h + 1.0) / HEADS) for h in range(HEADS)]
SCALE = HD ** -0.5
FAR = 1e30

K_ID, K_TRI, K_ONE = 0, P, 2 * P
K_DIST = 3 * P
K_SBIAS = K_DIST + 2 * P
K_PAR = K_SBIAS + WIN + 1
K_HALF = K_PAR + 2
K_SAME = K_HALF + 2
K_OWN = K_SAME + 64
K_IOTA = K_OWN + NB
K_NTH = K_IOTA + C
K_OF = K_NTH + NE
K_EPS = K_OF + 2
K_N = K_OF + 4

V_MIX, V_FFN, V_PLE, V_OUT, V_D, V_GLU, V_N = 0, 8, 16, 24, 32, 36, 40

AT_KVTOK, AT_SCORES, AT_VALUES, AT_TURN = 6, (6, 9), (8, 12), (11, 15)
AT_S_SCORES, AT_S_TURN, AT_S_VALUES = 13, 15, 16
AT_SPREAD, AT_BIAS, AT_ATTENDED, AT_SCALE, AT_TURNED = 7, (7, 10), (9, 13), (10, 14), (11, 15)
AT_S_BIAS, AT_S_OWN = 14, 15

U_BANK = (0, 1, 2, 7)
PP_BANK = (6, 7, 0, 1, 2, 6, 7, 0)
P_BANK = ((5, 6), (5, 7))
V_BANK = (7, 6)
UP, DN = 8, 4


def shape_constants():
    k = np.zeros((P, K_N), np.float32)
    i = np.arange(P)
    k[:, K_ID:K_ID + P] = np.eye(P)
    k[:, K_TRI:K_TRI + P] = i[:, None] < i[None]
    k[:, K_ONE:K_ONE + P] = 1.0
    dist = i[:, None] + WIN - np.arange(2 * P)[None]
    k[:, K_DIST:K_DIST + 2 * P] = np.where((dist >= 0) & (dist <= WIN), dist, FAR)
    r = np.arange(64)
    slope = np.asarray(SLOPES)[r % HEADS]
    k[:64, K_SBIAS:K_SBIAS + WIN + 1] = -slope[:, None] / SCALE * (WIN - np.arange(WIN + 1))[None]
    k[:, K_PAR] = (i // H) % 2 == 0
    k[:, K_PAR + 1] = (i // H) % 2 == 1
    k[:64, K_HALF] = r % HEADS < HEADS // KV
    k[:64, K_HALF + 1] = r % HEADS >= HEADS // KV
    k[:64, K_SAME:K_SAME + 64] = r[:, None] // HEADS == r[None] // HEADS
    k[:64, K_OWN:K_OWN + NB] = r[:, None] // HEADS == np.arange(NB)[None]
    k[:, K_IOTA:K_IOTA + C] = np.arange(C)[None]
    k[:, K_NTH:K_NTH + NE] = i[:, None] % NE == np.arange(NE)[None]
    k[:, K_OF] = C * (i // NE + 1)
    k[:, K_OF + 1] = i % NE
    k[:, K_EPS] = EPS
    return k


def hybrid_layer(nc, A, O):
    ctx = ExitStack()
    with ctx:
        def sb(name, shape, dt=F32):
            return ctx.enter_context(nc.sbuf_tensor(name, shape, dt))

        def sem(name):
            return ctx.enter_context(nc.semaphore(name))

        ps = ctx.enter_context(nc.psum_tensor("ps", [P, 8, 512], F32))
        ring_up = sb("ring_up", [P, UP, 2 * FF])
        ring_dn = sb("ring_dn", [P, 2 * DN, D])
        up_flat = ring_up[:].rearrange("p a b -> p (a b)")
        w_in = up_flat[:, 0:KD * D_IN].rearrange("p (k n) -> p k n", k=KD)
        w_glu = ring_up[:, 5].rearrange("p (k n) -> p k n", k=KM)
        w_out = ring_dn
        s5_mem = up_flat[:, 6 * 2 * FF:8 * 2 * FF]
        cos_t = s5_mem[:, 0:512].rearrange("p (a t) -> p a t", a=2)
        sin_t = s5_mem[:, 512:1024].rearrange("p (a t) -> p a t", a=2)
        tmp_t = s5_mem[:, 1024:1280]
        prod_p = s5_mem[:, 1280:1792].rearrange("p (r t) -> p r t", r=2)
        z_in = s5_mem[:, 1792:2304].rearrange("p (r t) -> p r t", r=2)
        rot_c = s5_mem[:, 2304:3328].rearrange("p (a r t) -> p a r t", a=2, r=2)
        w_gate = ring_up[:, 0:4].rearrange("p a (b n) -> p (a b) n", b=2)

        kst = sb("kst", [P, K_N])
        ident = kst[:, K_ID:K_ID + P]
        tri = kst[:, K_TRI:K_TRI + P]
        ones = kst[:, K_ONE:K_ONE + P]
        eps = kst[:, K_EPS:K_EPS + 1]
        x_tok = sb("x_tok", [P, 3, D])
        n_tok = sb("n_tok", [P, 3, D])
        fa = sb("fa", [P, KD, T])
        fb = sb("fb", [P, KD, T])
        vecs = sb("vecs", [P, V_N])
        final_g = sb("final_g", [P, D])
        router = sb("router", [P, KD, NE])
        router_b = sb("router_b", [P, NE])
        b_down = sb("b_down", [P, D])
        stat = sb("stat", [P, 3, 4])
        rank = sb("rank", [P, 3, NE])
        gate = sb("gate", [P, 3, NE])
        vis = sb("vis", [P, NE + 8 + 3 * VISITS])
        v_cnt, v_flag, v_pos = vis[:, 0:NE], vis[:, NE:NE + 1], vis[:, NE + 1:NE + 2]
        v_hot = vis[:, NE + 4:NE + 4 + VISITS]
        v_first = vis[:, NE + 4 + VISITS:NE + 4 + 2 * VISITS]
        v_from = vis[:, NE + 4 + 2 * VISITS:NE + 4 + 3 * VISITS]
        v_rank = vis[:, NE + 4 + 3 * VISITS:NE + 4 + 3 * VISITS + 3]
        vis_int = sb("vis_int", [1, VISITS + 1], I32)

        R_N = 12100
        region = sb("region", [P, R_N])
        used = [0]

        def part(n):
            used[0] += n
            assert used[0] <= R_N, used[0]
            return region[:, used[0] - n:used[0]]

        proj = part(10 * T).rearrange("p (k t) -> p k t", k=10)
        rot_s = part(1024).rearrange("p (a r t) -> p a r t", a=2, r=2)
        b_t = [part(512).rearrange("p (k n) -> p k n", k=4) for _ in range(2)]
        c_t = [part(512).rearrange("p (k n) -> p k n", k=4) for _ in range(3)]
        lo = [part(256).rearrange("p (a b) -> p a b", a=ST) for _ in range(2)]
        hi = [part(256).rearrange("p (a b) -> p a b", a=ST) for _ in range(2)]
        pt = part(16 * P).rearrange("p (k n) -> p k n", k=16)
        kc_t = part(NB * (WIN + 1)).rearrange("p (b n) -> p b n", b=NB)
        spread = part(NB * 72)
        pcols = part(7 * ST).rearrange("p (a b) -> p a b", a=7)
        x0_t = part(2 * P).rearrange("p (r n) -> p r n", r=2)
        xs_flat = part(2 * P)
        xs_new = xs_flat.rearrange("p (r b a) -> p r a b", r=2, a=ST)
        bu_s = part(2 * P).rearrange("p (r a b) -> p r a b", r=2, a=ST)
        u_spread = bu_s[:, 0].rearrange("p (c j) b -> p c j b", j=4)
        last = part(2 * ST).rearrange("p (r a) -> p r a", r=2)
        mini = part(2 * P)
        rows = fb[:].rearrange("p a b -> p (a b)")[:, 0:16 * P]
        pt_flat = pt.rearrange("p k n -> p (k n)")
        b_raw = pt_flat[:, 0:512].rearrange("p (r a h) -> p r a h", r=2, a=ST)
        b_bd = kc_t.rearrange("p b n -> p (b n)")[:, 0:1024].rearrange("p (r a m) -> p r a m", r=2, a=ST)
        c_raw = pt_flat[:, 512:1024].rearrange("p (r a n) -> p r a n", r=2, a=4)
        c_bd = pt_flat[:, 1024:2048].rearrange("p (r a n) -> p r a n", r=2, a=4)
        n_flat = n_tok[:].rearrange("p a b -> p (a b)")
        sc = n_flat[:, 0:2048].rearrange("p (h n) -> p h n", h=HEADS)
        att = n_flat[:, 2048:3072].rearrange("p (b n) -> p b n", b=2)
        fa_flat = fa[:].rearrange("p a b -> p (a b)")
        kc = fa_flat[:, 0:1024].rearrange("p (b n) -> p b n", b=NB)
        vc = fa_flat[:, 1024:2048].rearrange("p (b n) -> p b n", b=NB)
        y_t = proj[:, 0:4]

        small = sb("small", [P, 160])
        mx, mneg, rsum, esink, rden = (small[:, 8 * i:8 * i + 8] for i in range(5))
        sink_b = small[:, 40:48]
        sink_s = small[:, 48:49]
        s_small = small[:, 49:57]
        kv_tok = sb("kv_tok", [P, 3, P])
        kv_new = sb("kv_new", [NB, 2, P])
        s_sc = sb("s_sc", [64, WIN + 1])
        s_o = sb("s_o", [64, 2, 64])
        s_own = sb("s_own", [64, NB])
        s_ownT = sb("s_ownT", [NB, 64])
        top = sb("top", [P, 3, 48])
        top_i = sb("top_i", [P, 3, 8], U32)
        pick = sb("pick", [P, 2, TOPK, NE])

        used[0] = 0
        b_up = part(2 * FF)
        one_hot = part(C)
        sel = part(3 * 2 * C).rearrange("p (c a s) -> p c a s", c=3, a=2)
        sel_g = part(3 * 2 * C).rearrange("p (c a s) -> p c a s", c=3, a=2)
        xe = part(KD * 2 * C).rearrange("p (k s) -> p k s", k=KD)
        g_lim = part(512)
        w_pp = region[:, used[0] - 512:used[0] - 512 + 2 * D].rearrange("p (k n) -> p k n", k=2)
        u_lim = part(512)
        sig = part(512)
        act_v = part(512)
        act_t = part(512).rearrange("p (j n) -> p j n", j=4)
        logits_t = region[0:NE, used[0]:used[0] + T]
        out_e = part(D).rearrange("p (h n) -> p h n", h=2)
        g_t = part(3 * P)
        gates_t = part(T + C)
        p_tok = part(3 * PLE).rearrange("p (c n) -> p c n", c=3)
        p_t = part(2 * T).rearrange("p (k t) -> p k t", k=2)
        logits = part(3 * NE).rearrange("p (c n) -> p c n", c=3)
        mask = part(3 * NE).rearrange("p (c n) -> p c n", c=3)
        sg_t = part(2 * T).rearrange("p (a t) -> p a t", a=2)
        sq = proj[:, 6:8]

        def bank(b, n=512, parts=P, first=0):
            return ps[first:first + parts, b, 0:n]

        def col(t, n):
            return t.unsqueeze(2).to_broadcast([t.shape[0], t.shape[1], n])

        (ld_x, ld_win, ld_wglu, ld_wout, ld_vec, ld_par, ld_b, ld_c, ld_x0, ld_sink, ld_cache,
         ld_router, ld_bup, ld_gate_w, ld_p) = (sem(n) for n in (
            "ld_x", "ld_win", "ld_wglu", "ld_wout", "ld_vec", "ld_par", "ld_b", "ld_c", "ld_x0",
            "ld_sink", "ld_cache", "ld_router", "ld_bup", "ld_gate_w", "ld_p"))
        up_in = [sem(f"up_in{k}") for k in range(UP)]
        dn_in = [sem(f"dn_in{k}") for k in range(DN)]
        dve_step, act_step, pool_step, dve_loop = (sem(n) for n in ("dve_step", "act_step", "pool_step", "dve_loop"))
        names = ("n_ready st_k q_ps glu_ps s5_free up_free mix_ps dn_free f_out st_y c_ready par_sb b_ready "
                 "rot_ready trig last_in region_free hot_rdy hid_ps vec_ps norm_scaled norm_ps par_rows par_ps "
                 "norm_sb u_ps c_ps x0_ps c_sb b_ps b_sb u_sb bu_read bu_ps y_read y_rot q_sb tok_ps tok_sb "
                 "att_sb att_t score_read score_ps expd p_sb p_ps o_ps att_scaled att_ps kct_ps kct_sb q_spread "
                 "ssc_ps s_expd s_oready s_pps s_pspread s_ops s_ossq s_gps s_onorm s_otps state_s ys_ps gelu "
                 "state_ps ssm_sq ssm_ssq s_ot mix_sb ssm_n back_add back_ps lg_ps mask_sb cnt_ps gtr_ps by_expert_sb "
                 "sel_rdy xg_ps dn_sb gt_sb cmb_read cmb_ps xe_rdy act_rdy at_ps selg_rdy gt_ps at_sb "
                 "hi_ready bus_ps us_sb pT_ps pT_sb pp_sb pp_ps gz_mul gz_sig gz_ps par_exp par_red norm_ssq "
                 "norm_root par_sin vec_sb "
                 "x0_sb m_neg att_ssq att_root s_mneg s_groot ypre ssm_y glu_sig ssm_root topv w_exp g_rdy "
                 "sig_rdy vis_flag vis_pos vis_hot vis_ps v_rank").split()
        Z = {n: sem(n) for n in names}

        def complex_product(tt, chain, out, a, b, scratch):
            tt(scratch[0], a[1], b[1], ALU.mult)
            tt(out[0], a[0], b[0], ALU.mult)
            tt(scratch[1], a[1], b[0], ALU.mult)
            chain(tt(out[1], a[0], b[1], ALU.mult))
            tt(out[0], out[0], scratch[0], ALU.subtract)
            chain(tt(out[1], out[1], scratch[1], ALU.add))

        def power_square(eng, chain, base, n_, scratch):
            out = [rows[:, 8 * P + 32 * n_ + 16 * r:8 * P + 32 * n_ + 16 * r + 16] for r in range(2)]
            complex_product(eng.tensor_tensor, chain, out, base, base, [scratch[:, P * r:P * r + ST] for r in range(2)])
            return out

        def powers(eng, chain, tab, base, n_, scratch):
            eng.memset(tab[0][:, :, 0:1], 1.0)
            eng.memset(tab[1][:, :, 0:1], 0.0)
            for r in range(2):
                m = eng.tensor_copy(tab[r][:, :, 1:2], base[r].unsqueeze(2))
            chain(m)
            step = base
            for j, k in enumerate((2, 4, 8)):
                step = power_square(eng, chain, step, n_ + j, scratch)
                sc_ = [scratch[:, P * r:P * r + ST * k].rearrange("p (a b) -> p a b", b=k) for r in range(2)]
                complex_product(eng.tensor_tensor, chain, [t[:, :, k:2 * k] for t in tab], [t[:, :, 0:k] for t in tab],
                                [x.unsqueeze(2).to_broadcast([P, ST, k]) for x in step], sc_)

        block = ctx.enter_context(nc.Block())

        def further_visits(eng, body, expert_of=False):
            eng.wait_ge(Z["n_ready"], 1)
            n = eng.value_load(vis_int[0:1, VISITS:VISITS + 1], min_val=0, max_val=VISITS)

            def one(v):
                body(v, eng.value_load(vis_int[0:1, bass.ds(v, 1)], min_val=0, max_val=NE - 1)
                     if expert_of else None)

            with eng.If(n > 0):
                one(0)
            with eng.If(n > 1):
                with eng.Fori(1, VISITS) as v:
                    with eng.If(n > v):
                        one(v)
                    eng.nop()
            return n

        @block.sync
        def _(sp):
            x_p, x_s = A["x_prompt"][0], A["x_sample"].rearrange("b l d -> (b l) d")
            sp.dma_start(kst[:], A["shape_constants"]).then_inc(ld_x, 16)
            for c in range(2):
                sp.dma_start(x_tok[:, c], x_p[c * P:(c + 1) * P, :]).then_inc(ld_x, 16)
            sp.dma_start(x_tok[0:NB, 2], x_s).then_inc(ld_x, 16)
            for r, name in enumerate(("ssm_b_re", "ssm_b_im")):
                sp.dma_start(b_raw[:, r], A[name][0].rearrange("(k g) p h -> (g p) k h", g=2)).then_inc(ld_b, 16)
            for r, name in enumerate(("ssm_c_re", "ssm_c_im")):
                sp.dma_start(c_raw[:, r], A[name][0].rearrange("(k g) h p -> (g h) k p", k=4)).then_inc(ld_c, 16)
            for r, name in enumerate(("state_ssm_re", "state_ssm_im")):
                sp.dma_start(rows[:, (10 + r) * P:(11 + r) * P],
                              A[name][0].rearrange("b (k g) p -> (b k) (g p)", g=2)).then_inc(ld_x0, 16)
            w = A["w_in"][0].rearrange("(k p) n -> p k n", p=P)
            for k in range(0, KD, 2):
                sp.dma_start(w_in[:, k:k + 2], w[:, k:k + 2]).then_inc(ld_win, 16)
            sp.dma_start(sink_b, A["sinks"][0].partition_broadcast(P)).then_inc(ld_sink, 16)
            for b_ in range(NB):
                sp.dma_start(sink_s[HEADS * b_:HEADS * (b_ + 1), :], A["sinks"][0].unsqueeze(1)).then_inc(ld_sink, 16)
            sp.dma_start(w_glu, A["w_glu"][0].rearrange("(k p) n -> p k n", p=P)).then_inc(ld_wglu, 16)
            sp.dma_start(w_out[:], A["w_out"][0].rearrange("(k p) n -> p k n", p=P)).then_inc(ld_wout, 16)
            sp.dma_start(final_g[:], A["norm_final"].partition_broadcast(P)).then_inc(ld_router, 16)
            sp.dma_start(router[:], A["w_router"][0].rearrange("(k p) n -> p k n", p=P)).then_inc(ld_router, 16)
            sp.dma_start(router_b[:], A["b_router"][0].partition_broadcast(P)).then_inc(ld_router, 16)
            sp.dma_start(b_down[0:NE], A["b_down"][0]).then_inc(ld_router, 16)
            for src, dst in ((A["cache_k_win"], O[6]), (A["cache_v_win"], O[7])):
                sp.dma_start(dst[0].rearrange("b w n d -> b (w n d)")[:, 0:(WIN - 1) * P],
                             src[0].rearrange("b w n d -> b (w n d)")[:, P:WIN * P]).then_inc(Z["st_k"], 16)

            sp.wait_ge(Z["q_ps"], 6)
            sp.dma_start(kc, A["cache_k_win"][0].rearrange("b w n d -> w b (n d)")).then_inc(ld_cache, 16)
            sp.dma_start(vc, A["cache_v_win"][0].rearrange("b w n d -> w b (n d)")).then_inc(ld_cache, 16)
            sp.wait_ge(Z["tok_sb"], 1)
            sp.dma_start(O[2][0, 0].rearrange("w n d -> w (n d)"), kv_tok[:, 2]).then_inc(Z["st_k"], 16)
            sp.dma_start(O[3][0, 0].rearrange("w n d -> w (n d)"), kv_tok[:, 1]).then_inc(Z["st_k"], 16)
            for j in range(2):
                sp.dma_start(O[6 + j][0].rearrange("b w n d -> b w (n d)")[:, WIN - 1], kv_new[:, j]
                             ).then_inc(Z["st_k"], 16)

            def embedding_loads():
                sp.wait_ge(Z["y_rot"], ST)
                sp.wait_ge(Z["ys_ps"], 1)
                sp.wait_ge(Z["o_ps"], 2)
                sp.dma_start(p_tok[:, 0:2], A["p_prompt"][0, 0].rearrange("(c p) n -> p c n", p=P)).then_inc(ld_p, 16)
                sp.dma_start(p_tok[0:NB, 2], A["p_sample"][0].rearrange("b l n -> (b l) n")).then_inc(ld_p, 16)
                sp.dma_start(w_pp, A["w_ple_proj"][0].rearrange("(k p) n -> p k n", p=P)).then_inc(ld_p, 16)

            up_w = A["w_up"][0].rearrange("e (k p) n -> e k p n", p=P)
            dn_w = A["w_down"][0].rearrange("e (s k p) n -> e s p k n", p=P, k=2)

            def expert(e, t, first=False):
                for k in range(UP):
                    if first and k == 5:
                        embedding_loads()
                    if first:
                        sp.wait_ge(*((Z["q_ps"], 6) if k < 5 else (Z["glu_ps"], KM) if k == 5 else (Z["s5_free"], 1)))
                    else:
                        sp.wait_ge(Z["up_free"], t * UP + (k + 1 - UP))
                    sp.dma_start(ring_up[:, k], up_w[bass.ds(e, 1), k].rearrange("e p n -> (e p) n")
                                 ).then_inc(up_in[k], 16)
                for s in range(DN):
                    if first:
                        sp.wait_ge(Z["mix_ps"], KD)
                    else:
                        sp.wait_ge(Z["dn_free"], t * DN + (s + 1 - DN))
                    sp.dma_start(ring_dn[:, 2 * s:2 * s + 2], dn_w[bass.ds(e, 1), s].rearrange("e p k n -> (e p) k n")
                                 ).then_inc(dn_in[s], 16)

            expert(0, 0, first=True)
            with sp.Fori(1, NE) as e:
                expert(e, e)
            n = further_visits(sp, lambda v, e: expert(e, NE + v), expert_of=True)
            for k in range(4):
                sp.wait_ge(Z["up_free"], (n + (NE - 1)) * UP + (k + 1))
                sp.dma_start(w_gate[:, 2 * k:2 * k + 2], A["w_ple_gate"][0].rearrange("(s k p) n -> s p k n", p=P, k=2)[k]
                             ).then_inc(ld_gate_w, 16)
            sp.wait_ge(Z["f_out"], 3)
            for c in range(2):
                sp.dma_start(O[0][0, c * P:(c + 1) * P, :], n_tok[:, c]).then_inc(Z["st_y"], 16)
            sp.dma_start(O[1].rearrange("b l d -> (b l) d"), n_tok[0:NB, 2]).then_inc(Z["st_y"], 16)
            sp.wait_ge(Z["st_y"], 48)
            sp.wait_ge(Z["st_k"], 32 + 16 * 8)

        @block.gpsimd
        def _(pool):
            n = [0]

            def chain(ins):
                n[0] += 1
                ins.then_inc(pool_step, 1)
                pool.wait_ge(pool_step, n[0])

            tt = nc.gpsimd.tensor_tensor

            def cmul(out, a, b, scratch):
                complex_product(tt, chain, out, a, b, scratch)

            chain(nc.gpsimd.memset(b_down[NE:2 * NE], 0.0))
            chain(nc.gpsimd.memset(b_down[2 * NE:P], 0.0))
            chain(nc.gpsimd.memset(b_bd, 0.0))
            pool.wait_ge(ld_c, 32)
            pool.wait_ge(ld_x, 64)
            for r, sign in ((0, 1.0), (1, -1.0)):
                for par in range(2):
                    chain(nc.gpsimd.tensor_scalar(c_bd[:, r, :, par * S:par * S + S], c_raw[:, r],
                                                  kst[:, K_PAR + par:K_PAR + par + 1], sign, ALU.mult, ALU.mult))
            nc.gpsimd.nop().then_inc(Z["c_ready"], 1)
            pool.wait_ge(Z["par_sb"], 1)
            powers(nc.gpsimd, chain, lo, (pcols[:, 0], pcols[:, 1]), 0, mini)

            def trig(i):
                a = i % 2
                if i >= 2:
                    pool.wait_ge(Z["rot_ready"], i - 1)
                hb = [h[:, i].unsqueeze(2).to_broadcast([P, 16, 16]) for h in hi]
                lb = [l[:, i].unsqueeze(1).to_broadcast([P, 16, 16]) for l in lo]
                out = [x[:, a].rearrange("p (a b) -> p a b", a=16) for x in (cos_t, sin_t)]
                if i == 0:
                    pool.wait_ge(Z["hi_ready"], 1)
                cmul(out, hb, lb, [m.rearrange("p (a b) -> p a b", a=16) for m in (tmp_t, mini)])
                nc.gpsimd.nop().then_inc(Z["trig"], 1)

            def last_state(i):
                a = i % 2
                pool.wait_ge(Z["rot_ready"], i + 1)
                chain(tt(last[:, 0, i:i + 1], rot_c[:, a, 0, 255:256], rot_s[:, a, 1, 255:256], ALU.subtract))
                tt(last[:, 1, i:i + 1], rot_s[:, a, 0, 255:256], rot_c[:, a, 1, 255:256], ALU.add
                   ).then_inc(Z["last_in"], 1)

            for i in range(ST + 2):
                if i < ST:
                    trig(i)
                if i >= 2:
                    last_state(i - 2)

            pool.wait_ge(Z["region_free"], 1)
            nc.gpsimd.memset(b_up, 0.0).then_inc(Z["hot_rdy"], 1)

            def hot(e, t, first=False):
                if not first:
                    pool.wait_ge(Z["hid_ps"], t)
                nc.gpsimd.tensor_copy(one_hot, ident[:, bass.ds(e, 1)].to_broadcast([P, C])).then_inc(Z["hot_rdy"], 1)

            hot(0, 0, first=True)
            with pool.Fori(1, NE) as e:
                hot(e, e)
            further_visits(pool, lambda v, e: hot(e, NE + v), expert_of=True)

        @block.tensor
        def _(pe):
            mm, tr = nc.tensor.matmul, nc.tensor.transpose
            pe.wait_ge(ld_x, 64)
            pe.wait_ge(ld_vec, 16 * 7)
            tr(bank(7, V_N), rows[0:V_N, 0:P], ident[0:V_N, 0:V_N]).then_inc(Z["vec_ps"], 1)
            n = 0
            for c, (t0, nt) in enumerate(CHUNKS):
                pe.wait_ge(Z["norm_scaled"], c + 1)
                for half in range(2):
                    for k in range(4):
                        m = tr(ps[:, 2 * c + half, k * nt:(k + 1) * nt],
                               n_tok[0:nt, c, (4 * half + k) * P:(4 * half + k + 1) * P], ident[0:nt, 0:nt])
                    m.then_inc(Z["norm_ps"], 1)
            pe.wait_ge(Z["par_rows"], 1)
            for j in range(7):
                m = tr(ps[:, 6, j * ST:(j + 1) * ST], rows[0:ST, (2 + j) * P:(3 + j) * P], ident[0:ST, 0:ST])
            m.then_inc(Z["par_ps"], 1)

            def project(slot, b, lhs):
                for k in range(KD):
                    m = mm(bank(b, T), lhs(k), fa[:, k, :], start=(k == 0), stop=(k == KD - 1))
                return m

            pe.wait_ge(Z["norm_sb"], 6)
            pe.wait_ge(ld_win, 64)

            def project_u(j):
                project(6 + j, U_BANK[j], lambda k: w_in[:, k, D_IN - D_SSM + j * P:D_IN - D_SSM + (j + 1) * P]
                        ).then_inc(Z["u_ps"], 1)

            pe.wait_ge(Z["vec_sb"], 1)
            project_u(0)
            project_u(1)
            pe.wait_ge(Z["c_ready"], 1)
            for r in range(2):
                for k in range(4):
                    m = tr(ps[:, 4 + r, k * P:(k + 1) * P], c_bd[:, r, k], ident)
            m.then_inc(Z["c_ps"], 1)
            pe.wait_ge(ld_x0, 32)
            pe.wait_ge(Z["par_sb"], 1)
            for r in range(2):
                m = tr(ps[:, 6, r * P:(r + 1) * P], rows[:, (10 + r) * P:(11 + r) * P], ident)
            m.then_inc(Z["x0_ps"], 1)
            project_u(2)
            pe.wait_ge(Z["b_ready"], 1)
            pe.wait_ge(Z["c_sb"], 1)
            for r in range(2):
                for k in range(4):
                    m = tr(ps[:, 4 + r, k * P:(k + 1) * P],
                           b_bd[:, r, 4 * k:4 * k + 4].rearrange("p a m -> p (a m)"), ident)
            m.then_inc(Z["b_ps"], 1)
            pe.wait_ge(Z["b_sb"], 1)
            pe.wait_ge(Z["u_sb"], 3)

            def drive(i):
                c, j = divmod(i, 4)
                if i >= 2:
                    pe.wait_ge(Z["bu_read"], i - 1)
                if i == 12:
                    pe.wait_ge(Z["u_sb"], 4)
                rows_ = slice(32 * j, 32 * j + 32)
                for r in range(2):
                    m = mm(ps[:, i % 2, SEQ * r:SEQ * r + SEQ], b_t[r][rows_, c, :], proj[rows_, 6 + c, 0:SEQ],
                           start=True, stop=True)
                m.then_inc(Z["bu_ps"], 1)

            def drive_samples():
                pe.wait_ge(Z["us_sb"], 1)
                for r in range(2):
                    for c in range(4):
                        m = mm(ps[:, 7, (4 * r + c) * 32:(4 * r + c + 1) * 32], b_t[r][:, c, :],
                               u_spread[:, c].rearrange("p j b -> p (j b)"), start=True, stop=True)
                m.then_inc(Z["bus_ps"], 1)

            def read_out_samples():
                pe.wait_ge(Z["state_s"], 1)
                for i in range(ST):
                    c, j = divmod(i, 4)
                    for n_ in range(2):
                        m = mm(ps[32 * j:32 * j + 32, 7, NB * c:NB * c + NB], c_t[n_][:, c, 32 * j:32 * j + 32],
                               xs_new[:, n_, i, :], start=(n_ == 0), stop=(n_ == 1))
                m.then_inc(Z["ys_ps"], 1)

            def read_out(i):
                c, j = divmod(i, 4)
                pe.wait_ge(Z["rot_ready"], i + 1)
                if j == 0 and c >= 1:
                    pe.wait_ge(Z["y_read"], c)
                a = i % 2
                out = ps[32 * j:32 * j + 32, 4, 0:SEQ]
                cols = slice(32 * j, 32 * j + 32)
                for n_, (w, v) in enumerate(((0, rot_c[:, a, 0]), (1, rot_c[:, a, 1]), (2, rot_s[:, a, 1]),
                                            (1, rot_s[:, a, 0]))):
                    m = mm(out, c_t[w][:, c, cols], v, start=(n_ == 0), stop=(n_ == 3))
                m.then_inc(Z["y_rot"], 1)

            def project_q(c, b):
                for k in range(KD):
                    for n_ in range(KV):
                        h = 4 * n_ + c
                        m = mm(ps[64 * n_:64 * n_ + 64, b, 0:T], w_in[:, k, h * HD:(h + 1) * HD], fa[:, k, :],
                               start=(k == 0), stop=(k == KD - 1))
                return m

            def project_one(n_):
                slot, b = (4, 5, 0, 1, 2, 3)[n_], 5 + n_ % 2
                if n_ >= 2:
                    pe.wait_ge(Z["q_sb"], n_ - 1)
                if slot >= 4:
                    m = project(slot, b, lambda k: w_in[:, k, D_ATTN + (slot - 4) * P:D_ATTN + (slot - 3) * P])
                else:
                    m = project_q(slot, b)
                m.then_inc(Z["q_ps"], 1)

            def kv_to_tokens():
                pe.wait_ge(Z["q_sb"], 6)
                pe.wait_ge(Z["ypre"], 1)
                for j, (slot, c) in enumerate(((5, 0), (5, 1), (4, 1))):
                    tr(ps[:, 7, j * P:(j + 1) * P], proj[:, slot, c * P:(c + 1) * P], ident)
                for j, slot in enumerate((4, 5)):
                    m = tr(ps[0:NB, 6, j * P:(j + 1) * P], proj[:, slot, SEQ:T], ident)
                m.then_inc(Z["tok_ps"], 1)

            def scores(b):
                K = P * (b + 1)

                def head(c, n_, bank_, at):
                    r = slice(64 * n_, 64 * n_ + 64)
                    return mm(ps[:, bank_, at * K:(at + 1) * K], proj[r, c, b * P:(b + 1) * P], proj[r, 4, 0:K],
                              start=True, stop=True)

                if b == 0:
                    pe.wait_ge(Z["tok_sb"], 1)
                    for c in range(4):
                        for n_ in range(KV):
                            m = head(c, n_, 5 + n_, c)
                    m.then_inc(Z["score_ps"], 1)
                else:
                    for c in range(2):
                        for n_ in range(KV):
                            m = head(c, n_, 5 + n_, c)
                    m.then_inc(Z["score_ps"], 1)
                    for n_ in range(KV):
                        if n_ == 0:
                            pe.wait_ge(Z["att_sb"], 1)
                        else:
                            pe.wait_ge(Z["score_read"], 2)
                        for c in (2, 3):
                            m = head(c, n_, (7, 5)[n_], c - 2)
                        m.then_inc(Z["score_ps"], 1)

            p_fills = [0]

            def p_transposes(b):
                nk = b + 1
                pe.wait_ge(Z["expd"], b + 1)
                for f in range(2 * nk):
                    if f >= 2:
                        pe.wait_ge(Z["p_sb"], p_fills[0] - 1)
                    for q in range(4):
                        h, kc_ = divmod(4 * f + q, nk)
                        m = tr(ps[:, P_BANK[b][f % 2], q * P:(q + 1) * P], sc[:, h, kc_ * P:(kc_ + 1) * P], ident)
                    m.then_inc(Z["p_ps"], 1)
                    p_fills[0] += 1

            def values(b):
                nk = b + 1
                pe.wait_ge(Z["p_sb"], p_fills[0])
                if b == 1:
                    pe.wait_ge(Z["att_t"], 1)
                for h in range(HEADS):
                    for kc_ in range(nk):
                        m = mm(ps[:, V_BANK[b], h * HD:(h + 1) * HD], pt[:, h * nk + kc_, :],
                               kv_tok[:, kc_, (h // 4) * HD:(h // 4 + 1) * HD], start=(kc_ == 0), stop=(kc_ == nk - 1))
                m.then_inc(Z["o_ps"], 1)

            def att_transposes(b):
                pe.wait_ge(Z["att_scaled"], b + 1)
                if b == 0:
                    pe.wait_ge(Z["score_read"], 4)
                for k in range(4):
                    m = tr(ps[:, 6, k * P:(k + 1) * P], att[:, b, k * P:(k + 1) * P], ident)
                m.then_inc(Z["att_ps"], 1)

            def cache_transposes():
                pe.wait_ge(ld_cache, 32)
                pe.wait_ge(Z["p_sb"], p_fills[0])
                for f, b_ in enumerate((5, 7)):
                    for q in range(4):
                        m = tr(ps[:, b_, q * P:(q + 1) * P], kc[:, 4 * f + q], ident)
                    m.then_inc(Z["kct_ps"], 1)

            def sample_scores():
                pe.wait_ge(Z["kct_sb"], 3)
                pe.wait_ge(Z["q_spread"], 1)
                for b_ in range(NB):
                    m = mm(ps[0:64, 5, 0:WIN + 1], spread[:, b_ * 64:(b_ + 1) * 64], kc_t[:, b_, :],
                           start=(b_ == 0), stop=(b_ == NB - 1))
                m.then_inc(Z["ssc_ps"], 1)

            def turn_sample_probs():
                pe.wait_ge(Z["s_expd"], 1)
                pe.wait_ge(Z["s_oready"], 1)
                tr(ps[:, 7, 0:64], s_sc[:, 0:WIN], ident[0:64, 0:64])
                tr(ps[0:NB, 7, 64:128], s_own[:], ident[0:64, 0:64]).then_inc(Z["s_pps"], 1)

            def sample_values():
                pe.wait_ge(Z["s_pspread"], 2)
                for b_ in range(NB):
                    mm(ps[0:64, 5, 0:P], spread[:, b_ * 64:(b_ + 1) * 64], vc[:, b_, :], start=(b_ == 0), stop=False)
                mm(ps[0:64, 5, 0:P], s_ownT[:], kv_new[:, 1, :], start=False, stop=True).then_inc(Z["s_ops"], 1)

            def sample_norm():
                pe.wait_ge(Z["s_ossq"], 1)
                mm(ps[0:64, 5, 0:1], kst[0:64, K_SAME:K_SAME + 64], s_small[0:64, 5:6], start=True, stop=True
                   ).then_inc(Z["s_gps"], 1)

            def turn_sample_outputs():
                pe.wait_ge(Z["s_onorm"], 1)
                tr(ps[:, 4, 0:64], s_o[:].rearrange("p a d -> p (a d)"), ident[0:64, 0:64]).then_inc(Z["s_otps"], 1)

            drive(0)
            project_u(3)
            for i in range(ST + 1):
                if i + 1 < ST:
                    drive(i + 1)
                if i >= 1:
                    read_out(i - 1)
                if i == 1:
                    drive_samples()
                if i == 3:
                    read_out_samples()
                if i < 6:
                    project_one(i)
                if i == AT_KVTOK:
                    kv_to_tokens()
                for b in range(2):
                    if i == AT_SCORES[b]:
                        scores(b)
                    if i == AT_VALUES[b]:
                        p_transposes(b)
                        values(b)
                    if i == AT_TURN[b]:
                        att_transposes(b)
                if i == AT_S_SCORES:
                    cache_transposes()
                    sample_scores()
                if i == AT_S_TURN:
                    turn_sample_probs()
                if i == AT_S_VALUES:
                    sample_values()
            pe.wait_ge(ld_wglu, 16)
            pe.wait_ge(Z["gelu"], 1)
            for c in range(KM):
                for k in range(KM):
                    m = mm(bank(c, T), w_glu[:, k, c * P:(c + 1) * P], y_t[:, k, :], start=(k == 0), stop=(k == KM - 1))
                m.then_inc(Z["glu_ps"], 1)
            pe.wait_ge(Z["last_in"], ST)
            for r in range(2):
                tr(ps[:, 7, r * P:(r + 1) * P], xs_flat[:, r * P:(r + 1) * P], ident)
            for r in range(2):
                m = tr(ps[0:ST, 7, (2 + r) * P:(3 + r) * P], last[:, r], ident)
            m.then_inc(Z["state_ps"], 1)
            sample_norm()
            for c in range(KM):
                pe.wait_ge(Z["ssm_sq"], c + 1)
                m = mm(bank(6, T), ones, sq[:, c % 2], start=(c == 0), stop=(c == KM - 1))
                m.then_inc(Z["ssm_ssq"], 1)
            turn_sample_outputs()
            pe.wait_ge(ld_wout, 16)
            pe.wait_ge(Z["att_t"], 2)
            def mixed_back(half):
                pe.wait_ge(Z["mix_sb"], 4 * (half + 1))
                for c, (t0, nt) in enumerate(CHUNKS):
                    n_ = 3 * half + c
                    if n_ >= 2:
                        pe.wait_ge(Z["back_add"], n_ - 1)
                    for k in range(4):
                        m = tr(ps[0:nt, 4 + n_ % 2, k * P:(k + 1) * P], fa[:, 4 * half + k, t0:t0 + nt], ident)
                    m.then_inc(Z["back_ps"], 1)

            pe.wait_ge(Z["s_ot"], 1)
            for o in range(KD):
                if o >= 4:
                    pe.wait_ge(Z["mix_sb"], o - 3)
                for k in range(KD):
                    if o == 0 and k == 4:
                        pe.wait_ge(Z["ssm_n"], KM)
                    m = mm(bank(o % 4, T), w_out[:, k, o * P:(o + 1) * P], fb[:, k, :], start=(k == 0), stop=(k == KD - 1))
                m.then_inc(Z["mix_ps"], 1)
                if o == 5:
                    mixed_back(0)
            mixed_back(1)
            for c, (t0, nt) in enumerate(CHUNKS):
                pe.wait_ge(Z["norm_scaled"], 3 + c + 1)
                for half in range(2):
                    b_ = (0, 1, 2, 3, 6, 7)[2 * c + half]
                    for k in range(4):
                        m = tr(ps[:, b_, k * nt:(k + 1) * nt],
                               n_tok[0:nt, c, (4 * half + k) * P:(4 * half + k + 1) * P], ident[0:nt, 0:nt])
                    m.then_inc(Z["norm_ps"], 1)
            pe.wait_ge(Z["norm_sb"], 12)
            pe.wait_ge(ld_router, 64)
            for k in range(KD):
                m = mm(ps[0:NE, 4, 0:T], router[:, k, :], fb[:, k, :], start=(k == 0), stop=(k == KD - 1))
            m.then_inc(Z["lg_ps"], 1)
            pe.wait_ge(ld_p, 48)
            for k in range(2):
                for c, (t0, nt) in enumerate(CHUNKS):
                    m = tr(ps[:, 6 + k, t0:t0 + nt], p_tok[0:nt, c, k * P:(k + 1) * P], ident[0:nt, 0:nt])
            m.then_inc(Z["pT_ps"], 1)
            pe.wait_ge(Z["by_expert_sb"], 1)
            for c, (t0, nt) in enumerate(CHUNKS):
                m = tr(ps[0:nt, 5, c * NE:(c + 1) * NE], logits_t[:, t0:t0 + nt], ident[0:NE, 0:NE])
            m.then_inc(Z["lg_ps"], 1)
            pe.wait_ge(Z["pT_sb"], 1)

            def embedding(pieces):
                for o in pieces:
                    if o >= 5:
                        pe.wait_ge(Z["pp_sb"], o - 4)
                    for k in range(2):
                        m = mm(bank(PP_BANK[o], T), w_pp[:, k, o * P:(o + 1) * P], p_t[:, k, :],
                               start=(k == 0), stop=(k == 1))
                    m.then_inc(Z["pp_ps"], 1)

            embedding(range(6))
            pe.wait_ge(Z["mask_sb"], 1)
            for c, (t0, nt) in enumerate(CHUNKS):
                for k in range(c):
                    mm(ps[:, 5, c * NE:(c + 1) * NE], ones, mask[:, k, :], start=(k == 0), stop=False)
                mm(ps[:, 5, c * NE:(c + 1) * NE], tri[0:nt, :], mask[0:nt, c, :], start=(c == 0), stop=True)
            for c, (t0, nt) in enumerate(CHUNKS):
                m = mm(ps[:, 5, 3 * NE:4 * NE], ones[0:nt, :], mask[0:nt, c, :], start=(c == 0), stop=(c == 2))
            m.then_inc(Z["cnt_ps"], 1)
            for c, (t0, nt) in enumerate(CHUNKS):
                m = tr(ps[0:NE, 3, t0:t0 + nt], gate[0:nt, c, 0:NE], ident[0:nt, 0:nt])
            m.then_inc(Z["gtr_ps"], 1)

            embedding(range(6, KD))

            G_B, U_B, T_B, O_B, X_B = 0, 1, 3, 4, (2, 5)
            SHARE_B = ((6, 7), (G_B, U_B), (2, 2))

            def shares(weights, outputs, rows_=slice(0, P)):
                for c, (t0, nt) in enumerate(CHUNKS):
                    for half in range(2):
                        if c < 2:
                            m = mm(ps[:, SHARE_B[c][half], :], weights[rows_, t0:t0 + P], outputs(half),
                                   start=True, stop=True)
                        else:
                            m = mm(ps[64 * half:64 * half + 64, SHARE_B[c][half], :], weights[rows_, t0:t0 + 64], outputs(half),
                                   start=True, stop=True)
                    m.then_inc(Z["cmb_ps"], 1)

            def output_biases():
                pe.wait_ge(Z["by_expert_sb"], 2)
                shares(gates_t, lambda half: b_down[:, half * 512:(half + 1) * 512])

            def visit_list():
                pe.wait_ge(Z["vis_flag"], 1)
                mm(ps[:, 5, 0:1], tri, v_flag, start=True, stop=True).then_inc(Z["vis_pos"], 1)
                pe.wait_ge(Z["vis_hot"], 1)
                mm(ps[:, 5, 0:VISITS], ones, v_from, start=True, stop=True)
                mm(ps[0:1, 5, 64:64 + VISITS], kst[:, K_OF + 1:K_OF + 2], v_hot, start=True, stop=True)
                mm(ps[0:1, 5, 64 + VISITS:65 + VISITS], ones[:, 0:1], v_flag, start=True, stop=True
                   ).then_inc(Z["vis_ps"], 1)
                pe.wait_ge(Z["n_ready"], 1)

            def gather(p):
                if isinstance(p, int) and p == 0:
                    pe.wait_ge(Z["pp_sb"], 5)
                pe.wait_ge(Z["sel_rdy"], p + 1)
                for k in range(KD):
                    for c, (t0, nt) in enumerate(CHUNKS):
                        m = mm(ps[:, X_B[k // 4], (k % 4) * P:(k % 4 + 1) * P], n_tok[0:nt, c, k * P:(k + 1) * P],
                               sel[0:nt, c].rearrange("p a s -> p (a s)"), start=(c == 0), stop=(c == 2))
                    if k % 4 == 3:
                        m.then_inc(Z["xg_ps"], 1)

            def up(t, slots):
                for k in range(UP + 1):
                    if k < UP:
                        pe.wait_ge(up_in[k], 16 * t + 16)
                    else:
                        pe.wait_ge(Z["hot_rdy"], t + 2)
                    for q in range(4):
                        w = (ring_up[:, k] if k < UP else b_up)[:, q * 512:(q + 1) * 512]
                        m = mm(ps[64 * (q % 2):64 * (q % 2) + 64, q // 2, :], xe[:, k, slots] if k < UP else one_hot, w,
                               start=(k == 0), stop=(k == UP))
                    m.then_inc(Z["up_free"] if k < UP else Z["hid_ps"], 1)

            def turn_activations(t):
                pe.wait_ge(Z["act_rdy"], t + 1)
                for j in range(4):
                    m = tr(ps[:, T_B, j * P:(j + 1) * P], act_v[:, j * P:(j + 1) * P], ident)
                m.then_inc(Z["at_ps"], 1)

            def down(t):
                pe.wait_ge(Z["at_sb"], t + 1)
                for f in range(FF // P):
                    if f % 2 == 0:
                        pe.wait_ge(dn_in[f // 2], 16 * t + 16)
                    for half in range(2):
                        m = mm(ps[64 * half:64 * half + 64, O_B, :], act_t[:, f % 4, 64 * (f // 4):64 * (f // 4) + 64],
                               ring_dn[:, f, 512 * half:512 * half + 512], start=(f == 0), stop=(f == FF // P - 1))
                    if f % 2 == 1:
                        m.then_inc(Z["dn_free"], 1)

            def turn_selection(n_):
                pe.wait_ge(Z["selg_rdy"], n_ + 1)
                for c, (t0, nt) in enumerate(CHUNKS):
                    m = tr(ps[:, T_B, t0:t0 + nt], sel_g[0:nt, c].rearrange("p a s -> p (a s)"), ident[0:nt, 0:nt])
                m.then_inc(Z["gt_ps"], 1)

            def combine(p):
                pe.wait_ge(Z["dn_sb"], 2 * p + 2)
                pe.wait_ge(Z["gt_sb"], p + 1)
                shares(g_t, lambda half: out_e[:, half])

            def pair(p, place=None):
                t = 2 * p
                pe.wait_ge(Z["xe_rdy"], 2 * p + 2)
                if place == "first":
                    pe.wait_ge(ld_bup, 16)
                    pe.wait_ge(Z["pp_sb"], KD)
                else:
                    pe.wait_ge(Z["cmb_read"], 4 * p)
                if place == "last":
                    visit_list()
                up(t, slice(0, C))
                turn_activations(t)
                if place != "first":
                    combine(p - 1)
                down(t)
                turn_selection(p)
                if place != "first":
                    pe.wait_ge(Z["cmb_read"], 4 * p + 4)
                up(t + 1, slice(C, 2 * C))
                if place == "last":
                    gather_visit(0)
                else:
                    gather(p + 1)
                pe.wait_ge(Z["gt_sb"], p + 1)
                turn_activations(t + 1)
                if place == "first":
                    pe.wait_ge(Z["xe_rdy"], 4)
                    output_biases()
                pe.wait_ge(Z["dn_sb"], t + 1)
                down(t + 1)

            def gather_visit(v):
                pe.wait_ge(Z["sel_rdy"], PAIRS + 1 + v)
                for k in range(KD):
                    for c, (t0, nt) in enumerate(CHUNKS):
                        m = mm(ps[:, 2, k * C:(k + 1) * C], n_tok[0:nt, c, k * P:(k + 1) * P], sel[0:nt, c, 0],
                               start=(c == 0), stop=(c == 2))
                m.then_inc(Z["xg_ps"], 1)

            def visit(v, _):
                t = NE + v
                if not isinstance(v, int):
                    pe.wait_ge(Z["cmb_read"], 4 * (PAIRS + 1) + 4 * v)
                    gather_visit(v)
                pe.wait_ge(Z["xe_rdy"], 2 * PAIRS + 1 + v)
                if isinstance(v, int):
                    pe.wait_ge(Z["cmb_read"], 4 * (PAIRS + 1))
                up(t, slice(0, C))
                turn_activations(t)
                down(t)
                turn_selection(PAIRS + v)
                pe.wait_ge(Z["dn_sb"], t + 1)
                pe.wait_ge(Z["gt_sb"], PAIRS + 1 + v)
                shares(g_t, lambda half: out_e[0:C, half], slice(0, C))

            gather(0)
            pair(0, "first")
            with pe.Fori(1, PAIRS - 1) as p:
                pair(p)
            pair(PAIRS - 1, "last")
            pe.wait_ge(Z["xe_rdy"], 2 * PAIRS + 1)
            combine(PAIRS - 1)
            further_visits(pe, visit)

            for c, (t0, nt) in enumerate(CHUNKS):
                pe.wait_ge(Z["norm_scaled"], 6 + c + 1)
                for half in range(2):
                    b_ = (0, 1, 6, 7, 2, 5)[2 * c + half]
                    for k in range(4):
                        m = tr(ps[:, b_, k * nt:(k + 1) * nt],
                               n_tok[0:nt, c, (4 * half + k) * P:(4 * half + k + 1) * P], ident[0:nt, 0:nt])
                    m.then_inc(Z["norm_ps"], 1)
            pe.wait_ge(Z["norm_sb"], 18)
            pe.wait_ge(ld_gate_w, 64)

            def back(half):
                pe.wait_ge(Z["gz_mul"], 4 * (half + 1))
                for c, (t0, nt) in enumerate(CHUNKS):
                    n_ = 3 * half + c
                    if n_ >= 2:
                        pe.wait_ge(Z["back_add"], 6 + n_ - 1)
                    for k in range(4):
                        m = tr(ps[0:nt, 4 + n_ % 2, k * P:(k + 1) * P], fa[:, 4 * half + k, t0:t0 + nt], ident)
                    m.then_inc(Z["back_ps"], 1)

            for o in range(KD):
                b_ = o % 4
                if o >= 4:
                    pe.wait_ge(Z["gz_sig"], o - 3)
                for k in range(KD):
                    m = mm(bank(b_, T), w_gate[:, k, o * P:(o + 1) * P], fb[:, k, :], start=(k == 0), stop=(k == KD - 1))
                m.then_inc(Z["gz_ps"], 1)
                if o == 5:
                    back(0)
            back(1)

        @block.scalar
        def _(act):
            f = nc.scalar.activation
            n = [0]

            def chain(ins):
                n[0] += 1
                ins.then_inc(act_step, 1)
                act.wait_ge(act_step, n[0])

            for j, name in enumerate(("ssm_lam_re", "ssm_lam_im")):
                act.dma_start(rows[0:ST, (12 + j) * P:(13 + j) * P], A[name][0].rearrange("(k g) p -> k (g p)", g=2)
                              ).then_inc(ld_par, 16)
            act.dma_start(rows[0:ST, 14 * P:14 * P + 2], A["ssm_log_step"][0].rearrange("(k g) -> k g", g=2)
                          ).then_inc(ld_par, 16)
            r0 = 0
            for name, k in (("norm_mix", 8), ("norm_ffn", 8), ("norm_ple", 8), ("norm_attn_out", 4),
                            ("norm_ssm_out", 4)):
                act.dma_start(rows[r0:r0 + k, 0:P], A[name][0].rearrange("(k p) -> k p", p=P)).then_inc(ld_vec, 16)
                r0 += k
            act.dma_start(rows[r0:r0 + 4, 0:P], A["ssm_d"][0].rearrange("(k g) h -> k (g h)", k=4)).then_inc(ld_vec, 16)
            act.dma_start(rows[r0 + 4:r0 + 8, 0:P], A["b_glu"][0].rearrange("(k p) -> k p", p=P)).then_inc(ld_vec, 16)
            def roots(n_):
                for c, (t0, nt) in enumerate(CHUNKS):
                    act.wait_ge(Z["norm_ssq"], 3 * n_ + c + 1)
                    f(stat[0:nt, c, 1:2], stat[0:nt, c, 0:1], ACT.Sqrt, scale=1.0 / D, bias=eps[0:nt]
                      ).then_inc(Z["norm_root"], 1)

            R = [rows[0:ST, j * P:(j + 1) * P] for j in range(16)]
            act.wait_ge(ld_par, 48)
            f(rows[0:ST, 14 * P + 2:14 * P + 4], rows[0:ST, 14 * P:14 * P + 2], ACT.Exp).then_inc(Z["par_exp"], 1)
            act.wait_ge(Z["par_red"], 1)
            f(R[4], R[15], ACT.Exp).then_inc(Z["par_exp"], 1)
            for c, (t0, nt) in enumerate(CHUNKS):
                if c == 0:
                    act.wait_ge(ld_x, 64)
                f(n_tok[0:nt, c], x_tok[0:nt, c], ACT.Square, accum_out=stat[0:nt, c, 0:1]).then_inc(Z["norm_ssq"], 1)
            roots(0)
            act.wait_ge(Z["par_red"], 3)
            f(R[3], R[9], ACT.Sin)
            f(R[15], R[9], ACT.Sin, scale=0.5).then_inc(Z["par_sin"], 1)

            act.wait_ge(Z["vec_ps"], 1)
            f(vecs[:], bank(7, V_N), ACT.Copy).then_inc(Z["vec_sb"], 1)
            act.wait_ge(Z["par_ps"], 1)
            f(pcols, ps[:, 6, 0:7 * ST].rearrange("p (a b) -> p a b", a=7), ACT.Copy).then_inc(Z["par_sb"], 1)
            def u_copies(pieces):
                for j in pieces:
                    act.wait_ge(Z["u_ps"], j + 1)
                    f(proj[:, 6 + j, :], bank(U_BANK[j], T), ACT.Copy).then_inc(Z["u_sb"], 1)

            u_copies((0, 1))
            act.wait_ge(Z["c_ps"], 1)
            f(c_t[0], ps[:, 4].rearrange("p (k n) -> p k n", k=4), ACT.Copy)
            f(c_t[1], ps[:, 5].rearrange("p (k n) -> p k n", k=4), ACT.Copy)
            f(c_t[2], ps[:, 4].rearrange("p (k n) -> p k n", k=4), ACT.Copy, scale=-1.0).then_inc(Z["c_sb"], 1)
            act.wait_ge(Z["x0_ps"], 1)
            f(x0_t, ps[:, 6, 0:2 * P].rearrange("p (r n) -> p r n", r=2), ACT.Copy).then_inc(Z["x0_sb"], 1)
            u_copies((2,))
            act.wait_ge(Z["b_ps"], 1)
            f(b_t[0], ps[:, 4].rearrange("p (k n) -> p k n", k=4), ACT.Copy)
            f(b_t[1], ps[:, 5].rearrange("p (k n) -> p k n", k=4), ACT.Copy).then_inc(Z["b_sb"], 1)

            u_copies((3,))

            def qkv():
                for n_, slot in enumerate((4, 5, 0, 1, 2, 3)):
                    act.wait_ge(Z["q_ps"], n_ + 1)
                    m = f(proj[:, slot, :], bank(5 + n_ % 2, T), ACT.Copy)
                    m.then_inc(Z["q_sb"], 1)

            def kv_tokens():
                act.wait_ge(Z["tok_ps"], 1)
                chain(f(kv_tok[:], ps[:, 7, 0:3 * P].rearrange("p (a n) -> p a n", a=3), ACT.Copy))
                chain(f(kv_new[:], ps[0:NB, 6, 0:2 * P].rearrange("p (a n) -> p a n", a=2), ACT.Copy))
                nc.scalar.nop().then_inc(Z["tok_sb"], 1)

            def exps(b):
                K = P * (b + 1)
                act.wait_ge(Z["m_neg"], b + 1)
                for h in range(HEADS):
                    f(sc[:, h, 0:K], sc[:, h, 0:K], ACT.Exp, bias=mneg[:, h:h + 1], scale=SCALE,
                      accum_out=rsum[:, h:h + 1])
                f(esink, esink, ACT.Exp).then_inc(Z["expd"], 1)

            fills = [0]

            def p_copies(b):
                for q in range(2 * (b + 1)):
                    fills[0] += 1
                    act.wait_ge(Z["p_ps"], fills[0])
                    f(pt[:, 4 * q:4 * q + 4], ps[:, P_BANK[b][q % 2]].rearrange("p (k n) -> p k n", k=4), ACT.Copy
                      ).then_inc(Z["p_sb"], 1)

            def att_root(b):
                act.wait_ge(Z["att_sb"], b + 1)
                f(pt_flat[:, 0:D_ATTN], att[:, b], ACT.Square,
                  accum_out=small[:, 80 + b:81 + b]).then_inc(Z["att_ssq"], 1)
                act.wait_ge(Z["att_ssq"], b + 1)
                f(small[:, 84 + b:85 + b], small[:, 80 + b:81 + b], ACT.Sqrt, scale=1.0 / D_ATTN, bias=eps
                  ).then_inc(Z["att_root"], 1)

            def cache_copies():
                for q, b_ in enumerate((5, 7)):
                    act.wait_ge(Z["kct_ps"], q + 1)
                    f(kc_t[:, 4 * q:4 * q + 4, 0:WIN], ps[:, b_].rearrange("p (k n) -> p k n", k=4), ACT.Copy
                      ).then_inc(Z["kct_sb"], 1)
                f(kc_t[:, :, WIN:WIN + 1], proj[:, 4, SEQ:T].unsqueeze(2), ACT.Copy).then_inc(Z["kct_sb"], 1)

            def sample_exp():
                act.wait_ge(Z["s_mneg"], 1)
                f(s_sc[:], s_sc[:], ACT.Exp, bias=s_small[0:64, 1:2], scale=SCALE, accum_out=s_small[0:64, 2:3])
                f(s_small[0:64, 3:4], s_small[0:64, 3:4], ACT.Exp).then_inc(Z["s_expd"], 1)

            qkv()
            kv_tokens()
            for b in range(2):
                exps(b)
                p_copies(b)
                att_root(b)
            cache_copies()
            sample_exp()

            act.wait_ge(Z["ypre"], 2)
            f(y_t, proj[:, 6:10], ACT.Gelu_apprx_tanh).then_inc(Z["gelu"], 1)
            for c in range(KM):
                act.wait_ge(Z["glu_ps"], c + 1)
                if c >= 2:
                    act.wait_ge(Z["ssm_y"], c - 1)
                f(kc_t.rearrange("p b n -> p (b n)")[:, (c % 2) * T:(c % 2 + 1) * T], bank(c, T), ACT.Sigmoid,
                  bias=vecs[:, V_GLU + c:V_GLU + c + 1]).then_inc(Z["glu_sig"], 1)
            act.wait_ge(Z["state_ps"], 1)
            f(x0_t, ps[:, 7, 0:2 * P].rearrange("p (r n) -> p r n", r=2), ACT.Copy)
            chain(f(mini[0:ST, :].rearrange("p (r n) -> p r n", r=2),
                    ps[0:ST, 7, 2 * P:4 * P].rearrange("p (r n) -> p r n", r=2), ACT.Copy))
            for c in range(KM):
                act.wait_ge(Z["ssm_y"], c + 1)
                if c >= 2:
                    act.wait_ge(Z["ssm_ssq"], c - 1)
                f(sq[:, c % 2], fb[:, 4 + c, :], ACT.Square).then_inc(Z["ssm_sq"], 1)
            act.wait_ge(Z["s_gps"], 1)
            f(s_small[0:64, 6:7], ps[0:64, 5, 0:1], ACT.Sqrt, scale=1.0 / D_ATTN, bias=eps[0:64]
              ).then_inc(Z["s_groot"], 1)
            act.wait_ge(Z["ssm_ssq"], KM)
            f(sq[:, 1], bank(6, T), ACT.Sqrt, scale=1.0 / D_SSM, bias=eps).then_inc(Z["ssm_root"], 1)
            for r in range(2):
                act.dma_start(O[8 + r][0].rearrange("b (k g) p -> (b k) (g p)", g=2), x0_t[:, r]).then_inc(Z["st_k"], 16)
                act.dma_start(O[4 + r][0, 0].rearrange("(k g) p -> k (g p)", g=2), mini[0:ST, r * P:(r + 1) * P]
                              ).then_inc(Z["st_k"], 16)
            for o in range(KD):
                act.wait_ge(Z["mix_ps"], o + 1)
                f(fa[:, o, :], bank(o % 4, T), ACT.Copy).then_inc(Z["mix_sb"], 1)
            for c, (t0, nt) in enumerate(CHUNKS):
                act.wait_ge(Z["back_add"], 4 + c)
                f(n_tok[0:nt, c], x_tok[0:nt, c], ACT.Square, accum_out=stat[0:nt, c, 0:1]).then_inc(Z["norm_ssq"], 1)
            roots(1)
            act.wait_ge(Z["lg_ps"], 1)
            f(logits_t, ps[0:NE, 4, 0:T], ACT.Copy).then_inc(Z["by_expert_sb"], 1)
            act.wait_ge(Z["pT_ps"], 1)
            f(p_t, ps[:, 6:8, 0:T], ACT.Copy).then_inc(Z["pT_sb"], 1)

            act.wait_ge(Z["topv"], 1)
            for c, (t0, nt) in enumerate(CHUNKS):
                f(top[0:nt, c, 16:20], top[0:nt, c, 0:4], ACT.Exp, bias=top[0:nt, c, 12:13],
                  accum_out=top[0:nt, c, 20:21]).then_inc(Z["w_exp"], 1)
            for o in range(KD):
                act.wait_ge(Z["pp_ps"], o + 1)
                f(fa[:, o, :], bank(PP_BANK[o], T), ACT.Copy).then_inc(Z["pp_sb"], 1)
            act.wait_ge(Z["gtr_ps"], 1)
            f(gates_t[0:NE, 0:T], ps[0:NE, 3, 0:T], ACT.Copy).then_inc(Z["by_expert_sb"], 1)
            act.wait_ge(Z["hot_rdy"], 1)
            act.dma_start(b_up[0:NE, :], A["b_up"][0]).then_inc(ld_bup, 16)
            def activation(t):
                act.wait_ge(Z["g_rdy"], t + 1)
                f(sig, g_lim, ACT.Sigmoid, scale=ALPHA).then_inc(Z["sig_rdy"], 1)
                act.wait_ge(Z["at_ps"], t + 1)
                f(act_t, ps[:, 3].rearrange("p (j n) -> p j n", j=4), ACT.Copy).then_inc(Z["at_sb"], 1)

            def selection(n_):
                act.wait_ge(Z["gt_ps"], n_ + 1)
                f(g_t[:, 0:T], ps[:, 3, 0:T], ACT.Copy).then_inc(Z["gt_sb"], 1)

            def outputs(t, a):
                act.wait_ge(Z["dn_free"], DN * t + DN)
                for half in range(2):
                    m = f(out_e[C * a:C * a + C, half], ps[64 * half:64 * half + 64, 4], ACT.Copy)
                m.then_inc(Z["dn_sb"], 1)

            with act.Fori(0, PAIRS) as p:
                activation(2 * p)
                outputs(2 * p, 0)
                selection(p)
                activation(2 * p + 1)
                outputs(2 * p + 1, 1)
            def visit(v, _):
                activation(NE + v)
                outputs(NE + v, 0)
                selection(PAIRS + v)

            n_visits = further_visits(act, visit)

            for c, (t0, nt) in enumerate(CHUNKS):
                act.wait_ge(Z["cmb_read"], (n_visits + PAIRS) * 4 + (1, 2, 4)[c])
                f(n_tok[0:nt, c], x_tok[0:nt, c], ACT.Square, accum_out=stat[0:nt, c, 0:1]).then_inc(Z["norm_ssq"], 1)
            roots(2)
            for o in range(KD):
                act.wait_ge(Z["gz_ps"], o + 1)
                if o >= 2:
                    act.wait_ge(Z["gz_mul"], o - 1)
                f(sg_t[:, o % 2], bank(o % 4, T), ACT.Sigmoid).then_inc(Z["gz_sig"], 1)
            for c, (t0, nt) in enumerate(CHUNKS):
                act.wait_ge(Z["back_add"], 6 + 4 + c)
                f(n_tok[0:nt, c], x_tok[0:nt, c], ACT.Square, accum_out=stat[0:nt, c, 0:1]).then_inc(Z["norm_ssq"], 1)
            roots(3)
            act.wait_ge(Z["st_k"], 32 + 16 * 8)

        @block.vector
        def _(dve):
            V = nc.vector
            n = [0]

            def chain(ins):
                n[0] += 1
                ins.then_inc(dve_step, 1)
                dve.wait_ge(dve_step, n[0])

            def norm_rows(n_):
                for c, (t0, nt) in enumerate(CHUNKS):
                    dve.wait_ge(Z["norm_root"], 3 * n_ + c + 1)
                    chain(V.reciprocal(stat[0:nt, c, 2:3], stat[0:nt, c, 1:2]))
                    if n_ < 3:
                        V.tensor_scalar(n_tok[0:nt, c], x_tok[0:nt, c], stat[0:nt, c, 2:3], None, ALU.mult
                                        ).then_inc(Z["norm_scaled"], 1)

            R = [rows[0:ST, j * P:(j + 1) * P] for j in range(16)]
            l_re, l_im = R[12], R[13]
            dt = rows[0:ST, 14 * P + 2:14 * P + 4].unsqueeze(2).to_broadcast([ST, 2, S])

            def halves(x):
                return x.rearrange("k (g p) -> k g p", g=2)

            dve.wait_ge(Z["par_exp"], 1)
            V.tensor_tensor(halves(R[15]), halves(l_re), dt, ALU.mult).then_inc(Z["par_red"], 1)
            chain(V.tensor_tensor(halves(R[9]), halves(l_im), dt, ALU.mult))
            two_pi_hi, magic = 6.28125, 12582912.0
            two_pi_lo = 2.0 * np.pi - two_pi_hi
            chain(V.tensor_scalar(R[8], R[9], 1.0 / (2.0 * np.pi), magic, ALU.mult, ALU.add))
            chain(V.tensor_scalar(R[8], R[8], -magic, None, ALU.add))
            chain(V.scalar_tensor_tensor(R[9], R[8], -two_pi_hi, R[9], ALU.mult, ALU.add))
            chain(V.scalar_tensor_tensor(R[9], R[8], -float(two_pi_lo), R[9], ALU.mult, ALU.add))
            dve.wait_ge(Z["par_exp"], 2)
            V.tensor_scalar(R[9], R[9], 3.1415925, -3.1415925, ALU.min, ALU.max).then_inc(Z["par_red"], 2)
            chain(V.tensor_tensor(R[8], l_re, l_re, ALU.mult))
            chain(V.tensor_tensor(R[7], l_im, l_im, ALU.mult))
            chain(V.tensor_tensor(R[8], R[8], R[7], ALU.add))
            chain(V.reciprocal(R[8], R[8]))
            norm_rows(0)
            dve.wait_ge(Z["par_sin"], 1)
            chain(V.tensor_tensor(R[2], R[15], R[15], ALU.mult))
            chain(V.tensor_scalar(R[2], R[2], -2.0, 1.0, ALU.mult, ALU.add))
            chain(V.tensor_tensor(R[5], R[4], R[2], ALU.mult))
            chain(V.tensor_tensor(R[6], R[4], R[3], ALU.mult))
            chain(V.tensor_scalar(R[9], R[5], -1.0, None, ALU.add))
            chain(V.tensor_tensor(R[7], R[9], l_re, ALU.mult))
            chain(V.tensor_tensor(R[15], R[6], l_im, ALU.mult))
            chain(V.tensor_tensor(R[7], R[7], R[15], ALU.add))
            chain(V.tensor_tensor(R[7], R[7], R[8], ALU.mult))
            chain(V.tensor_tensor(R[15], R[9], l_im, ALU.mult))
            chain(V.tensor_tensor(R[9], R[6], l_re, ALU.mult))
            chain(V.tensor_tensor(R[9], R[9], R[15], ALU.subtract))
            V.tensor_tensor(R[8], R[9], R[8], ALU.mult).then_inc(Z["par_rows"], 1)
            dve.wait_ge(Z["vec_sb"], 1)
            for c, (t0, nt) in enumerate(CHUNKS):
                for half in range(2):
                    dve.wait_ge(Z["norm_ps"], 0 + 2 * c + half + 1)
                    V.tensor_tensor(fa[:, 4 * half:4 * half + 4, t0:t0 + nt],
                                    ps[:, 2 * c + half, 0:4 * nt].rearrange("p (k n) -> p k n", k=4),
                                    col(vecs[:, V_MIX + 4 * half:V_MIX + 4 * half + 4], nt), ALU.mult
                                    ).then_inc(Z["norm_sb"], 1)
            dve.wait_ge(Z["par_sb"], 1)
            prod_flat = prod_p.rearrange("p r t -> p (r t)")
            base = (pcols[:, 0], pcols[:, 1])
            for j in range(4):
                base = power_square(V, chain, base, 3 + j % 2, prod_flat)
            powers(V, chain, hi, base, 5, prod_flat)
            V.engine_nop().then_inc(Z["hi_ready"], 1)
            dve.wait_ge(ld_b, 32)
            dve.wait_ge(Z["c_ready"], 1)
            fr, fi = col(pcols[:, 5], H), col(pcols[:, 6], H)
            t1, t2 = (prod_p[:, r].rearrange("p (a h) -> p a h", h=H) for r in range(2))
            for r, (f0, f1, op) in enumerate(((fr, fi, ALU.subtract), (fi, fr, ALU.add))):
                V.tensor_tensor(t1, b_raw[:, 0], f0, ALU.mult)
                chain(V.tensor_tensor(t2, b_raw[:, 1], f1, ALU.mult))
                for par in range(2):
                    rows_ = slice(par * S, par * S + S)
                    m = V.tensor_tensor(b_bd[rows_, r, :, par * H:par * H + H], t1[rows_], t2[rows_], op)
                chain(m)
            V.engine_nop().then_inc(Z["b_ready"], 1)

            def spread_sample_u():
                chain(V.memset(u_spread, 0.0))
                dve.wait_ge(Z["u_sb"], 4)
                for j in range(4):
                    r = slice(32 * j, 32 * j + 32)
                    m = V.tensor_copy(u_spread[r, :, j], proj[r, 6:10, SEQ:T])
                m.then_inc(Z["us_sb"], 1)

            def scan(i):
                a = i % 2
                cs = cos_t[:, a].unsqueeze(1).to_broadcast([P, 2, SEQ])
                sn = sin_t[:, a].unsqueeze(1).to_broadcast([P, 2, SEQ])
                decay = pcols[:, 2, i:i + 1].to_broadcast([P, SEQ])
                dve.wait_ge(Z["trig"], i + 1)
                dve.wait_ge(Z["bu_ps"], i + 1)
                bu = ps[:, a].rearrange("p (r t) -> p r t", r=2)
                V.tensor_tensor(prod_p, bu, cs, ALU.mult)
                q = ps[:, 2].rearrange("p (r t) -> p r t", r=2)
                z = ps[:, 3].rearrange("p (r t) -> p r t", r=2)
                V.tensor_tensor(q, bu, sn, ALU.mult).then_inc(Z["bu_read"], 1)
                dve.wait_ge(Z["bu_read"], i + 1)
                V.tensor_tensor(z_in[:, 0], prod_p[:, 0], q[:, 1], ALU.add)
                chain(V.tensor_tensor(z_in[:, 1], prod_p[:, 1], q[:, 0], ALU.subtract))
                V.tensor_tensor_scan(z[:, 0], decay, z_in[:, 0], 0.0, ALU.mult, ALU.add)
                chain(V.tensor_tensor_scan(z[:, 1], decay, z_in[:, 1], 0.0, ALU.mult, ALU.add))
                if i >= 2:
                    dve.wait_ge(Z["y_rot"], i - 1)
                    dve.wait_ge(Z["last_in"], i - 1)
                V.tensor_tensor(rot_c[:, a], z, cs, ALU.mult)
                V.tensor_tensor(rot_s[:, a], z, sn, ALU.mult).then_inc(Z["rot_ready"], 1)

            def biases(b):
                K = P * (b + 1)
                steps = ([[(4 * n_ + c, 5 + n_, c) for c in range(4) for n_ in range(KV)]] if b == 0 else
                         [[(4 * n_ + c, 5 + n_, c) for n_ in range(KV) for c in range(2)],
                          [(c, 7, c - 2) for c in (2, 3)], [(4 + c, 5, c - 2) for c in (2, 3)]])
                for n_, heads in enumerate(steps):
                    dve.wait_ge(Z["score_ps"], b + n_ + 1)
                    for h, bank_, at in heads:
                        m = V.scalar_tensor_tensor(sc[:, h, 0:K], kst[:, K_DIST + 2 * P - K:K_DIST + 2 * P],
                                                   -SLOPES[h] / SCALE, ps[:, bank_, at * K:(at + 1) * K],
                                                   ALU.mult, ALU.add)
                    m.then_inc(Z["score_read"], 1)
                if b == 0:
                    dve.wait_ge(ld_sink, 16 * (NB + 1))
                dve.wait_ge(Z["score_read"], (1, 4)[b])
                chain(V.tensor_reduce(mx, sc[:, :, 0:K], AX.X, ALU.max))
                chain(V.scalar_tensor_tensor(mx, mx, SCALE, sink_b, ALU.mult, ALU.max))
                chain(V.tensor_scalar(mneg, mx, -1.0, None, ALU.mult))
                V.tensor_tensor(esink, sink_b, mneg, ALU.add).then_inc(Z["m_neg"], 1)

            def attended(b):
                dve.wait_ge(Z["expd"], b + 1)
                chain(V.tensor_tensor(rden, rsum, esink, ALU.add))
                chain(V.reciprocal(rden, rden))
                dve.wait_ge(Z["o_ps"], b + 1)
                V.tensor_tensor(att[:, b].rearrange("p (h d) -> p h d", h=HEADS),
                                ps[:, V_BANK[b]].rearrange("p (h d) -> p h d", h=HEADS), col(rden, HD), ALU.mult
                                ).then_inc(Z["att_sb"], 1)

            def att_scale(b):
                dve.wait_ge(Z["att_root"], b + 1)
                chain(V.reciprocal(small[:, 86 + b:87 + b], small[:, 84 + b:85 + b]))
                V.tensor_scalar(att[:, b], att[:, b], small[:, 86 + b:87 + b], None, ALU.mult
                                ).then_inc(Z["att_scaled"], 1)

            def att_turned(b):
                dve.wait_ge(Z["att_ps"], b + 1)
                V.tensor_tensor(fb[:, 0:4, b * P:(b + 1) * P], ps[:, 6].rearrange("p (k n) -> p k n", k=4),
                                col(vecs[:, V_OUT:V_OUT + 4], P), ALU.mult).then_inc(Z["att_t"], 1)

            sp72 = spread.rearrange("p (b s) -> p b s", s=72)

            def spread_queries():
                dve.wait_ge(Z["q_sb"], 6)
                chain(V.memset(spread, 0.0))
                for c in range(4):
                    for n_ in range(KV):
                        r = slice(64 * n_, 64 * n_ + 64)
                        m = V.tensor_copy(sp72[r, :, 4 * n_ + c:4 * n_ + c + 1], proj[r, c, SEQ:T].unsqueeze(2))
                m.then_inc(Z["q_spread"], 1)

            def sample_bias():
                dve.wait_ge(Z["ssc_ps"], 1)
                chain(V.tensor_tensor(s_sc[:], ps[0:64, 5, 0:WIN + 1], kst[0:64, K_SBIAS:K_SBIAS + WIN + 1], ALU.add))
                chain(V.tensor_reduce(s_small[0:64, 0:1], s_sc[:], AX.X, ALU.max))
                chain(V.scalar_tensor_tensor(s_small[0:64, 0:1], s_small[0:64, 0:1], SCALE, sink_s[0:64], ALU.mult, ALU.max))
                chain(V.tensor_scalar(s_small[0:64, 1:2], s_small[0:64, 0:1], -1.0, None, ALU.mult))
                V.tensor_tensor(s_small[0:64, 3:4], sink_s[0:64], s_small[0:64, 1:2], ALU.add).then_inc(Z["s_mneg"], 1)

            def sample_own():
                dve.wait_ge(Z["s_expd"], 1)
                V.tensor_scalar(s_own[:], kst[0:64, K_OWN:K_OWN + NB], s_sc[:, WIN:WIN + 1], None, ALU.mult
                                ).then_inc(Z["s_oready"], 1)
                chain(V.tensor_tensor(s_small[0:64, 4:5], s_small[0:64, 2:3], s_small[0:64, 3:4], ALU.add))
                chain(V.reciprocal(s_small[0:64, 4:5], s_small[0:64, 4:5]))

            def spread_probs():
                dve.wait_ge(Z["s_pps"], 1)
                V.tensor_copy(s_ownT[:], ps[0:NB, 7, 64:128]).then_inc(Z["s_pspread"], 1)
                V.tensor_copy(sp72[:, :, 0:HEADS], ps[:, 7, 0:64].rearrange("p (b h) -> p b h", b=NB)
                              ).then_inc(Z["s_pspread"], 1)

            def sample_outputs():
                dve.wait_ge(Z["s_ops"], 1)
                chain(V.tensor_scalar(s_o[:, 0], ps[0:64, 5, 0:64], kst[0:64, K_HALF:K_HALF + 1], s_small[0:64, 4:5],
                                      ALU.mult, ALU.mult))
                chain(V.tensor_scalar(s_o[:, 1], ps[0:64, 5, 64:128], kst[0:64, K_HALF + 1:K_HALF + 2],
                                      s_small[0:64, 4:5], ALU.mult, ALU.mult))
                chain(V.tensor_tensor(s_o[:, 0], s_o[:, 0], s_o[:, 1], ALU.add))
                chain(V.tensor_tensor(s_o[:, 1], s_o[:, 0], s_o[:, 0], ALU.mult))
                V.tensor_reduce(s_small[0:64, 5:6], s_o[:, 1], AX.X, ALU.add).then_inc(Z["s_ossq"], 1)

            def sample_scaled():
                dve.wait_ge(Z["s_groot"], 1)
                chain(V.reciprocal(s_small[0:64, 7:8], s_small[0:64, 6:7]))
                chain(V.tensor_scalar(s_o[:, 0], s_o[:, 0], s_small[0:64, 7:8], None, ALU.mult))
                V.tensor_copy(s_o[:, 1], s_o[:, 0]).then_inc(Z["s_onorm"], 1)

            def sample_turned():
                dve.wait_ge(Z["s_otps"], 1)
                for par in range(2):
                    r = slice(64 * par, 64 * par + 64)
                    m = V.tensor_tensor(fb[r, 0:4, SEQ:T],
                                        ps[r, 4, 0:64].rearrange("p (b c a) -> p a c b", b=NB, a=2)[:, par],
                                        col(vecs[r, V_OUT:V_OUT + 4], NB), ALU.mult)
                m.then_inc(Z["s_ot"], 1)

            def sample_states():
                dve.wait_ge(Z["bus_ps"], 1)
                for r in range(2):
                    m = V.tensor_copy(bu_s[:, r].rearrange("p a b -> p (a b)"), ps[:, 7, P * r:P * (r + 1)])
                chain(m)
                dve.wait_ge(Z["x0_sb"], 1)
                x0 = [x0_t[:, r].rearrange("p (b a) -> p a b", a=ST) for r in range(2)]
                lr, li = col(pcols[:, 3], NB), col(pcols[:, 4], NB)
                t1 = prod_flat[:, 0:P].rearrange("p (a b) -> p a b", a=ST)
                for r, (f0, f1, op) in enumerate(((lr, li, ALU.subtract), (li, lr, ALU.add))):
                    chain(V.tensor_tensor(xs_new[:, r], x0[0], f0, ALU.mult))
                    chain(V.tensor_tensor(t1, x0[1], f1, ALU.mult))
                    chain(V.tensor_tensor(xs_new[:, r], xs_new[:, r], t1, op))
                    chain(V.tensor_tensor(xs_new[:, r], xs_new[:, r], bu_s[:, r], ALU.add))
                V.engine_nop().then_inc(Z["state_s"], 1)

            def sample_y():
                dve.wait_ge(Z["ys_ps"], 1)
                for c in range(KM):
                    m = V.scalar_tensor_tensor(proj[:, 6 + c, SEQ:T], proj[:, 6 + c, SEQ:T],
                                               vecs[:, V_D + c:V_D + c + 1], ps[:, 7, NB * c:NB * c + NB],
                                               ALU.mult, ALU.add)
                m.then_inc(Z["ypre"], 1)

            for i in range(ST + 1):
                if i < ST:
                    scan(i)
                if i == 0:
                    spread_sample_u()
                if i == 2:
                    sample_states()
                if i == 3:
                    sample_y()
                if i == AT_SPREAD:
                    spread_queries()
                for b in range(2):
                    if i == AT_BIAS[b]:
                        biases(b)
                    if i == AT_ATTENDED[b]:
                        attended(b)
                    if i == AT_SCALE[b]:
                        att_scale(b)
                    if i == AT_TURNED[b]:
                        att_turned(b)
                if i == AT_S_BIAS:
                    sample_bias()
                if i == AT_S_OWN:
                    sample_own()
                    spread_probs()
                if i >= 4 and i % 4 == 0:
                    c = i // 4 - 1
                    dve.wait_ge(Z["y_rot"], 4 * c + 4)
                    dve.wait_ge(Z["bu_ps"], 4 * c + 4)
                    V.scalar_tensor_tensor(proj[:, 6 + c, 0:SEQ], proj[:, 6 + c, 0:SEQ], vecs[:, V_D + c:V_D + c + 1],
                                           ps[:, 4, 0:SEQ], ALU.mult, ALU.add).then_inc(Z["y_read"], 1)
            V.engine_nop().then_inc(Z["ypre"], 1)
            sample_outputs()
            dve.wait_ge(Z["last_in"], ST)
            V.engine_nop().then_inc(Z["s5_free"], 1)
            for c in range(KM):
                dve.wait_ge(Z["glu_sig"], c + 1)
                V.tensor_tensor(fb[:, 4 + c, :], y_t[:, c, :],
                                kc_t.rearrange("p b n -> p (b n)")[:, (c % 2) * T:(c % 2 + 1) * T], ALU.mult
                                ).then_inc(Z["ssm_y"], 1)
            sample_scaled()
            dve.wait_ge(Z["ssm_root"], 1)
            chain(V.reciprocal(sq[:, 0], sq[:, 1]))
            sample_turned()
            for c in range(KM):
                V.scalar_tensor_tensor(fb[:, 4 + c, :], fb[:, 4 + c, :], vecs[:, V_OUT + 4 + c:V_OUT + 5 + c], sq[:, 0],
                                       ALU.mult, ALU.mult).then_inc(Z["ssm_n"], 1)
            n_ = 0
            for half in range(2):
                for c, (t0, nt) in enumerate(CHUNKS):
                    n_ += 1
                    dve.wait_ge(Z["back_ps"], n_)
                    xh = x_tok[0:nt, c, 512 * half:512 * half + 512]
                    V.tensor_tensor(xh, xh, ps[0:nt, 4 + (n_ - 1) % 2, :], ALU.add).then_inc(Z["back_add"], 1)
            norm_rows(1)
            for c, (t0, nt) in enumerate(CHUNKS):
                for half in range(2):
                    dve.wait_ge(Z["norm_ps"], 6 + 2 * c + half + 1)
                    b_ = (0, 1, 2, 3, 6, 7)[2 * c + half]
                    V.tensor_tensor(fb[:, 4 * half:4 * half + 4, t0:t0 + nt],
                                    ps[:, b_, 0:4 * nt].rearrange("p (k n) -> p k n", k=4),
                                    col(vecs[:, V_FFN + 4 * half:V_FFN + 4 * half + 4], nt), ALU.mult
                                    ).then_inc(Z["norm_sb"], 1)
            V.memset(mask, 0.0)
            V.memset(gate[:], 0.0)
            chain(V.memset(rank[:], -1.0))
            chain(V.memset(sel_g, 0.0))
            chain(V.memset(g_t, 0.0))
            chain(V.memset(gates_t, 0.0))
            V.engine_nop().then_inc(Z["region_free"], 1)
            dve.wait_ge(Z["lg_ps"], 2)
            dve.wait_ge(ld_router, 64)
            groups = ((slice(0, 2), P), (slice(2, 3), NB))
            for cs, nt in groups:
                r, nc_ = slice(0, nt), cs.stop - cs.start
                chain(V.tensor_tensor(logits[r, cs], ps[r, 5, cs.start * NE:cs.stop * NE].rearrange("p (c n) -> p c n", n=NE),
                                      router_b[r].unsqueeze(1).to_broadcast([nt, nc_, NE]), ALU.add))
                for c in range(cs.start, cs.stop):
                    m = V.max(top[r, c, 0:8], logits[r, c])
                chain(m)
                V.tensor_scalar(top[r, cs, 12:13], top[r, cs, 0:1], -1.0, None, ALU.mult)
                for c in range(cs.start, cs.stop):
                    m = V.max_index(top_i[r, c], top[r, c, 0:8], logits[r, c])
                chain(m)
                chain(V.tensor_copy(top[r, cs, 24:32], top_i[r, cs]))
            V.engine_nop().then_inc(Z["topv"], 1)
            for cs, nt in groups:
                r, nc_ = slice(0, nt), cs.stop - cs.start
                shape = [nt, nc_, TOPK, NE]
                iota = kst[r, K_IOTA:K_IOTA + NE].unsqueeze(1).unsqueeze(1).to_broadcast(shape)
                by_expert = pick[r, 0:nc_].rearrange("p c k e -> p c e k")
                chain(V.tensor_tensor(pick[r, 0:nc_], iota, top[r, cs, 24:28].unsqueeze(3).to_broadcast(shape), ALU.is_equal))
                chain(V.tensor_reduce(mask[r, cs], by_expert, AX.X, ALU.add))
                dve.wait_ge(Z["w_exp"], cs.stop)
                chain(V.reciprocal(top[r, cs, 21:22], top[r, cs, 20:21]))
                chain(V.tensor_tensor(top[r, cs, 16:20], top[r, cs, 16:20],
                                      top[r, cs, 21:22].to_broadcast([nt, nc_, TOPK]), ALU.mult))
                chain(V.tensor_tensor(pick[r, 0:nc_], pick[r, 0:nc_], top[r, cs, 16:20].unsqueeze(3).to_broadcast(shape),
                                      ALU.mult))
                chain(V.tensor_reduce(gate[r, cs, 0:NE], by_expert, AX.X, ALU.add))
            V.engine_nop().then_inc(Z["mask_sb"], 1)
            dve.wait_ge(Z["cnt_ps"], 1)
            chain(V.scalar_tensor_tensor(rank[:, :, 0:NE], ps[:, 5, 0:3 * NE].rearrange("p (c n) -> p c n", c=3), 1.0, mask,
                                         ALU.add, ALU.mult))
            chain(V.tensor_scalar(rank[:, :, 0:NE], rank[:, :, 0:NE], -1.0, None, ALU.add))
            chain(V.tensor_tensor(v_cnt, ps[:, 5, 3 * NE:4 * NE], kst[:, K_NTH:K_NTH + NE], ALU.mult))

            iota2 = kst[:, K_IOTA:K_IOTA + C].unsqueeze(1).unsqueeze(1).to_broadcast([P, 3, 2, C])

            def of_pair(table, p):
                return table[:, :, bass.ds(2 * p, 2)].unsqueeze(3).to_broadcast([P, 3, 2, C])

            def select(p):
                V.tensor_tensor(sel, iota2, of_pair(rank, p), ALU.is_equal).then_inc(Z["sel_rdy"], 1)

            def visit_list():
                chain(V.tensor_reduce(v_flag, v_cnt, AX.X, ALU.add))
                V.tensor_tensor(v_flag, v_flag, kst[:, K_OF:K_OF + 1], ALU.is_gt).then_inc(Z["vis_flag"], 1)
                dve.wait_ge(Z["vis_pos"], 1)
                dve.wait_ge(Z["vis_flag"], 1)
                chain(V.tensor_copy(v_pos, ps[:, 5, 0:1]))
                chain(V.tensor_scalar(v_hot, kst[:, K_IOTA:K_IOTA + VISITS], v_pos, None, ALU.is_equal))
                chain(V.tensor_scalar(v_hot, v_hot, v_flag, None, ALU.mult))
                V.tensor_scalar(v_from, v_hot, kst[:, K_OF:K_OF + 1], None, ALU.mult).then_inc(Z["vis_hot"], 1)
                dve.wait_ge(Z["vis_ps"], 1)
                chain(V.tensor_copy(v_first, ps[:, 5, 0:VISITS]))
                V.tensor_copy(vis_int[:], ps[0:1, 5, 64:65 + VISITS]).then_inc(Z["n_ready"], 1)

            def gathered(p):
                for h in range(2):
                    dve.wait_ge(Z["xg_ps"], 2 * p + h + 1)
                    V.tensor_tensor(xe[:, 4 * h:4 * h + 4], ps[:, (2, 5)[h]].rearrange("p (k s) -> p k s", k=4),
                                    col(vecs[:, V_FFN + 4 * h:V_FFN + 4 * h + 4], 2 * C), ALU.mult
                                    ).then_inc(Z["xe_rdy"], 1)

            def added(n_):
                if not (isinstance(n_, int) and n_ == 0):
                    dve.wait_ge(Z["cmb_read"], 4 * n_)
                for c, (t0, nt) in enumerate(CHUNKS):
                    dve.wait_ge(Z["cmb_ps"], 3 * n_ + c + 1)
                    xh = x_tok[0:nt, c].rearrange("p (a n) -> p a n", a=2)
                    if c < 2:
                        b_ = (6, 0)[c]
                        V.tensor_tensor(xh, xh, ps[0:nt, b_:b_ + 2, :], ALU.add).then_inc(Z["cmb_read"], 1)
                    else:
                        V.tensor_tensor(xh[:, 0], xh[:, 0], ps[0:nt, 2, :], ALU.add).then_inc(Z["cmb_read"], 1)
                        V.tensor_tensor(xh[:, 1], xh[:, 1], ps[64:64 + nt, 2, :], ALU.add).then_inc(Z["cmb_read"], 1)

            def activation(t):
                dve.wait_ge(Z["hid_ps"], t + 1)
                V.tensor_scalar(g_lim, bank(0), LIMIT, None, ALU.min).then_inc(Z["g_rdy"], 1)
                V.tensor_scalar(u_lim, bank(1), -LIMIT, LIMIT, ALU.max, ALU.min).then_inc(dve_loop, 1)
                dve.wait_ge(dve_loop, 2 * t + 1)
                dve.wait_ge(Z["g_rdy"], t + 1)
                V.scalar_tensor_tensor(u_lim, u_lim, 1.0, g_lim, ALU.add, ALU.mult).then_inc(dve_loop, 1)
                dve.wait_ge(dve_loop, 2 * t + 2)
                dve.wait_ge(Z["sig_rdy"], t + 1)
                V.tensor_tensor(act_v, u_lim, sig, ALU.mult).then_inc(Z["act_rdy"], 1)

            def pair(p, place=None):
                dve.wait_ge(Z["sel_rdy"], p + 1)
                if place != "first":
                    dve.wait_ge(Z["gt_ps"], p)
                V.tensor_tensor(sel_g, sel, of_pair(gate, p), ALU.mult).then_inc(Z["selg_rdy"], 1)
                dve.wait_ge(Z["selg_rdy"], p + 1)
                if place == "last":
                    visit_list()
                    dve.wait_ge(Z["n_ready"], 1)
                    select_visit(0, dve.value_load(vis_int[0:1, 0:1], min_val=0, max_val=NE - 1))
                else:
                    select(p + 1)
                activation(2 * p)
                if place != "first":
                    added(p)
                activation(2 * p + 1)
                if place == "last":
                    gathered_visit(0)
                else:
                    gathered(p + 1)
                if place == "first":
                    added(0)

            def select_visit(v, e):
                if not isinstance(v, int):
                    dve.wait_ge(Z["sel_rdy"], PAIRS + v)
                V.tensor_tensor(v_rank.unsqueeze(2), rank[:, :, bass.ds(e, 1)],
                                v_first[:, bass.ds(v, 1)].unsqueeze(1).to_broadcast([P, 3, 1]), ALU.subtract
                                ).then_inc(Z["v_rank"], 1)
                dve.wait_ge(Z["v_rank"], v + 1)
                V.tensor_tensor(sel[:, :, 0], kst[:, K_IOTA:K_IOTA + C].unsqueeze(1).to_broadcast([P, 3, C]),
                                v_rank.unsqueeze(2).to_broadcast([P, 3, C]), ALU.is_equal).then_inc(Z["sel_rdy"], 1)

            def gathered_visit(v):
                dve.wait_ge(Z["xg_ps"], 2 * PAIRS + 1 + v)
                V.tensor_tensor(xe[:, :, 0:C], ps[:, 2].rearrange("p (k s) -> p k s", k=KD),
                                col(vecs[:, V_FFN:V_FFN + KD], C), ALU.mult).then_inc(Z["xe_rdy"], 1)

            def visit(v, e):
                if not isinstance(v, int):
                    select_visit(v, e)
                dve.wait_ge(Z["sel_rdy"], PAIRS + 1 + v)
                dve.wait_ge(Z["gt_ps"], PAIRS + v)
                V.tensor_tensor(sel_g[:, :, 0], sel[:, :, 0], gate[:, :, bass.ds(e, 1)].to_broadcast([P, 3, C]), ALU.mult
                                ).then_inc(Z["selg_rdy"], 1)
                if not isinstance(v, int):
                    gathered_visit(v)
                activation(NE + v)
                added(PAIRS + 1 + v)

            select(0)
            gathered(0)
            pair(0, "first")
            with dve.Fori(1, PAIRS - 1) as p:
                pair(p)
            pair(PAIRS - 1, "last")
            added(PAIRS)
            further_visits(dve, visit, expert_of=True)

            norm_rows(2)
            for c, (t0, nt) in enumerate(CHUNKS):
                for half in range(2):
                    dve.wait_ge(Z["norm_ps"], 12 + 2 * c + half + 1)
                    b_ = (0, 1, 6, 7, 2, 5)[2 * c + half]
                    V.tensor_tensor(fb[:, 4 * half:4 * half + 4, t0:t0 + nt],
                                    ps[:, b_, 0:4 * nt].rearrange("p (k n) -> p k n", k=4),
                                    col(vecs[:, V_PLE + 4 * half:V_PLE + 4 * half + 4], nt), ALU.mult
                                    ).then_inc(Z["norm_sb"], 1)

            def residual(half):
                for c, (t0, nt) in enumerate(CHUNKS):
                    n_ = 3 * half + c
                    dve.wait_ge(Z["back_ps"], 6 + n_ + 1)
                    xh = x_tok[0:nt, c, 512 * half:512 * half + 512]
                    V.tensor_tensor(xh, xh, ps[0:nt, 4 + n_ % 2, :], ALU.add).then_inc(Z["back_add"], 1)

            dve.wait_ge(Z["pp_sb"], KD)
            for o in range(KD):
                dve.wait_ge(Z["gz_sig"], o + 1)
                V.tensor_tensor(fa[:, o, :], fa[:, o, :], sg_t[:, o % 2], ALU.mult).then_inc(Z["gz_mul"], 1)
                if o == 5:
                    residual(0)
            residual(1)
            norm_rows(3)
            dve.wait_ge(ld_router, 64)
            for c, (t0, nt) in enumerate(CHUNKS):
                V.scalar_tensor_tensor(n_tok[0:nt, c], x_tok[0:nt, c], stat[0:nt, c, 2:3], final_g[0:nt, :], ALU.mult,
                                       ALU.mult).then_inc(Z["f_out"], 1)


_INS = ['x_prompt', 'x_sample', 'cache_k_win', 'cache_v_win', 'state_ssm_re', 'state_ssm_im', 'p_prompt', 'p_sample',
        'norm_mix', 'w_in', 'sinks', 'ssm_lam_re', 'ssm_lam_im', 'ssm_log_step', 'ssm_b_re', 'ssm_b_im', 'ssm_c_re',
        'ssm_c_im', 'ssm_d', 'w_glu', 'b_glu', 'norm_attn_out', 'norm_ssm_out', 'w_out', 'norm_ffn', 'w_router',
        'b_router', 'w_up', 'b_up', 'w_down', 'b_down', 'norm_ple', 'w_ple_gate', 'w_ple_proj', 'norm_final']
_OUTS = [(1, SEQ, D), (NB, 1, D), (1, 1, WIN, KV, HD), (1, 1, WIN, KV, HD), (1, 1, G, S), (1, 1, G, S),
         (1, NB, WIN, KV, HD), (1, NB, WIN, KV, HD), (1, NB, G, S), (1, NB, G, S)]


def kernel(**inputs):
    import numpy as _np
    import concourse.bacc as _bacc
    from concourse import mybir as _mybir
    from concourse.bass_utils import run_bass_kernel_spmd as _run

    nc = _bacc.Bacc("TRN2", target_bir_lowering=False, num_devices=1)
    arrays, aps = {}, {}
    for name in _INS + ["shape_constants"]:
        a = shape_constants() if name == "shape_constants" else _np.ascontiguousarray(inputs[name])
        arrays[f"in_{name}_dram"] = a
        aps[name] = nc.dram_tensor(f"in_{name}_dram", a.shape, _mybir.dt.from_np(a.dtype), kind="ExternalInput").ap()
    outs = [nc.dram_tensor(f"out_{i}_dram", shape, F32, kind="ExternalOutput").ap() for i, shape in enumerate(_OUTS)]
    hybrid_layer(nc, aps, outs)
    r = _run(nc, [arrays], core_ids=[0])
    return tuple(r.results[0][f"out_{i}_dram"] for i in range(len(_OUTS)))
```
